# Optimizing a Trainium2 kernel written in Bass

```python
import math
import jax, jax.numpy as jnp
from jax import lax
import numpy as np

D_MODEL = 1024
BATCH = 1
SEQ = 256
DEPTH = 2
DEC_BATCH = 8
DEC_SEQ = 1
PAST_LEN = 256
PAGE_SIZE = 128

S5_WIDTH = D_MODEL // 4
S5_GROUP = 16
S5_GROUPS = S5_WIDTH // S5_GROUP
S5_STATE = 64
SB_HEADS = 4
SB_HEAD_DIM = 64
SB_WIDTH = SB_HEADS * SB_HEAD_DIM
SB_BLOCK = 128
SB_BIAS_INIT = -7.0
RET_WIDTH = D_MODEL - S5_WIDTH - SB_WIDTH
RET_HEADS = 4
RET_DV = RET_WIDTH // RET_HEADS
RET_DK = RET_DV // 2
RET_QK = RET_HEADS * RET_DK
RET_CHUNK = 128
ROPE_BASE = 10000.0
D_FF = 2816
CONV_W = 3
LN_EPS = 1e-5
RMS_EPS = 1e-6
ALPHA = (2.0 * DEPTH) ** 0.25
BETA = (8.0 * DEPTH) ** -0.25
SPLITS = [S5_WIDTH, SB_WIDTH, SB_WIDTH, SB_WIDTH, RET_QK, RET_QK, RET_WIDTH, RET_WIDTH]
D_IN = sum(SPLITS)

kernel_name = "hybrid_s5_stickbreak_retention_convffn_step"

F32 = jnp.float32

def layer_norm(x, g, b):
    xf = x.astype(F32)
    mu = jnp.mean(xf, -1, keepdims=True)
    var = jnp.mean(jnp.square(xf - mu), -1, keepdims=True)
    return ((xf - mu) * lax.rsqrt(var + LN_EPS) * g + b).astype(x.dtype)

def rms_norm(x, g):
    xf = x.astype(F32)
    return (xf * lax.rsqrt(jnp.mean(xf * xf, -1, keepdims=True) + RMS_EPS) * g).astype(x.dtype)

def s5_discretize(lam_re, lam_im, log_step, b_re, b_im):
    lam_re = jnp.minimum(lam_re.astype(F32), -1e-4)
    lam_im = lam_im.astype(F32)
    dt = jnp.exp(log_step.astype(F32))[:, None]
    ldt_re, ldt_im = lam_re * dt, lam_im * dt
    mag = jnp.exp(ldt_re)
    a_re, a_im = mag * jnp.cos(ldt_im), mag * jnp.sin(ldt_im)
    den = lam_re * lam_re + lam_im * lam_im
    n_re, n_im = a_re - 1.0, a_im
    f_re = (n_re * lam_re + n_im * lam_im) / den
    f_im = (n_im * lam_re - n_re * lam_im) / den
    b_re, b_im = b_re.astype(F32), b_im.astype(F32)
    bb_re = f_re[..., None] * b_re - f_im[..., None] * b_im
    bb_im = f_re[..., None] * b_im + f_im[..., None] * b_re
    return ldt_re, ldt_im, a_re, a_im, bb_re, bb_im

def s5_combine(e1, e2):
    a1r, a1i, b1r, b1i = e1
    a2r, a2i, b2r, b2i = e2
    return (a2r * a1r - a2i * a1i, a2r * a1i + a2i * a1r,
            a2r * b1r - a2i * b1i + b2r, a2r * b1i + a2i * b1r + b2i)

def s5_branch(u, x0_re, x0_im, lam_re, lam_im, log_step, b_re, b_im, c_re, c_im, d, w_glu):
    bn, L, _ = u.shape
    uf = u.astype(F32)
    ug = uf.reshape(bn, L, S5_GROUPS, S5_GROUP)
    ldt_re, ldt_im, a_re, a_im, bb_re, bb_im = s5_discretize(lam_re, lam_im, log_step, b_re, b_im)
    bu_re = jnp.einsum('blgh,gph->blgp', ug, bb_re)
    bu_im = jnp.einsum('blgh,gph->blgp', ug, bb_im)
    ar = jnp.broadcast_to(a_re, bu_re.shape)
    ai = jnp.broadcast_to(a_im, bu_re.shape)
    _, _, xr, xi = lax.associative_scan(s5_combine, (ar, ai, bu_re, bu_im), axis=1)
    steps = jnp.arange(1, L + 1, dtype=F32)[:, None, None]
    pm = jnp.exp(ldt_re * steps)
    pr, pi = pm * jnp.cos(ldt_im * steps), pm * jnp.sin(ldt_im * steps)
    x0r, x0i = x0_re.astype(F32)[:, None], x0_im.astype(F32)[:, None]
    xr = xr + pr * x0r - pi * x0i
    xi = xi + pr * x0i + pi * x0r
    y = (jnp.einsum('blgp,ghp->blgh', xr, c_re.astype(F32))
         - jnp.einsum('blgp,ghp->blgh', xi, c_im.astype(F32)))
    y = y.reshape(bn, L, S5_WIDTH) + d * uf
    h = jax.nn.gelu(y)
    out = h * jax.nn.sigmoid(h @ w_glu)
    return out, xr[:, -1], xi[:, -1]

def stick_breaking(q, k, v, bias, q_pos, k_pos):
    z = (jnp.einsum('bqhd,bkhd->bhqk', q, k).astype(F32) * (SB_HEAD_DIM ** -0.5)
         + bias.astype(F32)[None, :, None, None])
    valid = k_pos[None, :] < q_pos[:, None]
    log_beta = jax.nn.log_sigmoid(z)
    log_rest = jnp.where(valid, log_beta - z, 0.0)
    tail = lax.cumsum(log_rest, axis=3, reverse=True) - log_rest
    w = jnp.where(valid, jnp.exp(log_beta + tail), 0.0)
    return jnp.einsum('bhqk,bkhd->bqhd', w, v.astype(F32))

def sb_prompt(q, k, v, bias):
    L = q.shape[1]
    pos = jnp.arange(L)
    outs = [stick_breaking(q[:, lo:lo + SB_BLOCK], k[:, :lo + SB_BLOCK], v[:, :lo + SB_BLOCK], bias,
                           pos[lo:lo + SB_BLOCK], pos[:lo + SB_BLOCK])
            for lo in range(0, L, SB_BLOCK)]
    return jnp.concatenate(outs, axis=1)

def make_sb_sample(k_pool, v_pool, page_table):
    def attend(q, k, v, bias):
        bn, L = q.shape[:2]
        k_past = k_pool[page_table].reshape(bn, -1, SB_HEADS, SB_HEAD_DIM)
        v_past = v_pool[page_table].reshape(bn, -1, SB_HEADS, SB_HEAD_DIM)
        past = k_past.shape[1]
        k_all = jnp.concatenate([k_past.astype(k.dtype), k], axis=1)
        v_all = jnp.concatenate([v_past.astype(v.dtype), v], axis=1)
        return stick_breaking(q, k_all, v_all, bias, past + jnp.arange(L), jnp.arange(past + L))
    return attend

def rope(x, pos):
    half = RET_DK // 2
    inv = ROPE_BASE ** (-jnp.arange(half, dtype=F32) / half)
    ang = pos[:, None] * inv[None, :]
    cos, sin = jnp.cos(ang)[None, :, None, :], jnp.sin(ang)[None, :, None, :]
    x1, x2 = x[..., :half], x[..., half:]
    return jnp.concatenate([x1 * cos - x2 * sin, x1 * sin + x2 * cos], -1)

def ret_log_decay():
    return jnp.log1p(-jnp.exp2(-5.0 - jnp.arange(RET_HEADS, dtype=F32)))

def retention_chunk(s, q, k, v):
    L = q.shape[1]
    lg = ret_log_decay()
    idx = jnp.arange(L, dtype=F32)
    diff = idx[:, None] - idx[None, :]
    decay = jnp.where(diff >= 0, jnp.exp(lg[:, None, None] * jnp.maximum(diff, 0.0)), 0.0)
    inner = jnp.einsum('blhd,bmhd->bhlm', q, k) * decay
    o = jnp.einsum('bhlm,bmhe->blhe', inner, v)
    q_dec = q * jnp.exp(lg[None, :] * (idx[:, None] + 1.0))[None, :, :, None]
    o = o + jnp.einsum('blhd,bhde->blhe', q_dec, s)
    k_dec = k * jnp.exp(lg[None, :] * (L - 1.0 - idx[:, None]))[None, :, :, None]
    s = jnp.exp(lg * L)[None, :, None, None] * s + jnp.einsum('blhd,blhe->bhde', k_dec, v)
    return o, s

def retention_branch(q, k, v, g, pos, s0, gn_g, gn_b):
    bn, L = q.shape[:2]
    q = rope(q.astype(F32).reshape(bn, L, RET_HEADS, RET_DK), pos) * (RET_DK ** -0.5)
    k = rope(k.astype(F32).reshape(bn, L, RET_HEADS, RET_DK), pos)
    v = v.astype(F32).reshape(bn, L, RET_HEADS, RET_DV)
    chunk = RET_CHUNK if L % RET_CHUNK == 0 else L
    n = L // chunk

    def to_chunks(t):
        return t.reshape(bn, n, chunk, *t.shape[2:]).swapaxes(0, 1)

    def step(s, qkv):
        o, s = retention_chunk(s, *qkv)
        return s, o

    s_new, o = lax.scan(step, s0.astype(F32), (to_chunks(q), to_chunks(k), to_chunks(v)))
    o = o.swapaxes(0, 1).reshape(bn, L, RET_HEADS, RET_DV)
    mu = jnp.mean(o, -1, keepdims=True)
    var = jnp.mean(jnp.square(o - mu), -1, keepdims=True)
    o = ((o - mu) * lax.rsqrt(var + LN_EPS)).reshape(bn, L, RET_WIDTH) * gn_g + gn_b
    return jax.nn.silu(g) * o, s_new

def conv_ffn(x, prev, w_up, conv_w, conv_b, w_down):
    L = x.shape[1]
    h = x @ w_up
    hp = jnp.concatenate([prev.astype(h.dtype), h], axis=1)
    c = conv_b + sum(conv_w[j] * hp[:, j:j + L] for j in range(CONV_W))
    a, gate = jnp.split(c, 2, axis=-1)
    return (jax.nn.silu(gate) * a) @ w_down, hp[:, -(CONV_W - 1):]

def trunk_layer(x, pos, s5_re0, s5_im0, ret_s0, conv_prev, sb_attend, p):
    bn, L, _ = x.shape
    h = x @ p['w_in']
    u_a, q_b, k_b, v_b, q_c, k_c, v_c, g_c = jnp.split(h, list(np.cumsum(SPLITS)[:-1]), axis=-1)
    ya, s5r, s5i = s5_branch(u_a, s5_re0, s5_im0, p['lam_re'], p['lam_im'], p['log_step'],
                             p['b_re'], p['b_im'], p['c_re'], p['c_im'], p['d'], p['w_glu'])
    ya = rms_norm(ya, p['norm_a_g'])
    kb = k_b.reshape(bn, L, SB_HEADS, SB_HEAD_DIM)
    vb = v_b.reshape(bn, L, SB_HEADS, SB_HEAD_DIM)
    yb = sb_attend(q_b.reshape(bn, L, SB_HEADS, SB_HEAD_DIM), kb, vb, p['sb_bias']).reshape(bn, L, SB_WIDTH)
    yb = rms_norm(yb, p['norm_b_g'])
    yc, ret_s = retention_branch(q_c, k_c, v_c, g_c, pos, ret_s0, p['gn_g'], p['gn_b'])
    mix = jnp.concatenate([ya, yb, yc], axis=-1).astype(x.dtype) @ p['w_out']
    x = layer_norm(ALPHA * x + mix, p['ln1_g'], p['ln1_b'])
    f, conv_new = conv_ffn(x, conv_prev, p['w_up'], p['conv_w'], p['conv_b'], p['w_down'])
    x = layer_norm(ALPHA * x + f, p['ln2_g'], p['ln2_b'])
    return x, (kb, vb, s5r, s5i, ret_s, conv_new)

def setup_inputs(seed: int = 0) -> dict:
    key = jax.random.key(seed)
    ks = jax.random.split(key, 40)
    ctr = [0]

    def nxt():
        k = ks[ctr[0]]
        ctr[0] += 1
        return k

    def nrm(shape, scale):
        return scale * jax.random.normal(nxt(), shape, F32)

    n_pages = PAST_LEN // PAGE_SIZE
    n_used = DEC_BATCH * n_pages
    n_pool = n_used + (n_used + 3) // 4
    G, P = S5_GROUPS, S5_STATE
    inp = {}
    inp['x_prompt'] = nrm((BATCH, SEQ, D_MODEL), 1.0)
    inp['x_sample'] = nrm((DEC_BATCH, DEC_SEQ, D_MODEL), 1.0)
    inp['cache_k'] = nrm((DEPTH, n_pool, PAGE_SIZE, SB_HEADS, SB_HEAD_DIM), 1.0)
    inp['cache_v'] = nrm((DEPTH, n_pool, PAGE_SIZE, SB_HEADS, SB_HEAD_DIM), 1.0)
    inp['state_s5_re'] = nrm((DEPTH, DEC_BATCH, G, P), 1.0)
    inp['state_s5_im'] = nrm((DEPTH, DEC_BATCH, G, P), 1.0)
    inp['state_ret'] = nrm((DEPTH, DEC_BATCH, RET_HEADS, RET_DK, RET_DV), 1.0)
    inp['state_conv'] = nrm((DEPTH, DEC_BATCH, CONV_W - 1, 2 * D_FF), 1.0)
    inp['page_table'] = jax.random.permutation(nxt(), n_pool)[:n_used].reshape(DEC_BATCH, n_pages).astype(jnp.int32)
    inp['ln_in_g'] = 1.0 + nrm((D_MODEL,), 0.01)
    inp['ln_in_b'] = nrm((D_MODEL,), 0.01)
    inp['w_in'] = nrm((DEPTH, D_MODEL, D_IN), D_MODEL ** -0.5)
    inp['s5_lambda_re'] = -0.5 + nrm((DEPTH, G, P), 0.01)
    inp['s5_lambda_im'] = math.pi * jnp.arange(P, dtype=F32) + nrm((DEPTH, G, P), 0.01)
    inp['s5_log_step'] = jax.random.uniform(nxt(), (DEPTH, G), F32, math.log(1e-3), math.log(1e-1))
    inp['s5_b_re'] = nrm((DEPTH, G, P, S5_GROUP), (2.0 * S5_GROUP) ** -0.5)
    inp['s5_b_im'] = nrm((DEPTH, G, P, S5_GROUP), (2.0 * S5_GROUP) ** -0.5)
    inp['s5_c_re'] = nrm((DEPTH, G, S5_GROUP, P), (2.0 * P) ** -0.5)
    inp['s5_c_im'] = nrm((DEPTH, G, S5_GROUP, P), (2.0 * P) ** -0.5)
    inp['s5_d'] = nrm((DEPTH, S5_WIDTH), 1.0)
    inp['s5_w_glu'] = nrm((DEPTH, S5_WIDTH, S5_WIDTH), S5_WIDTH ** -0.5)
    inp['norm_a_g'] = 1.0 + nrm((DEPTH, S5_WIDTH), 0.01)
    inp['norm_b_g'] = 1.0 + nrm((DEPTH, SB_WIDTH), 0.01)
    inp['sb_logit_bias'] = SB_BIAS_INIT + nrm((DEPTH, SB_HEADS), 0.1)
    inp['ret_gn_g'] = 1.0 + nrm((DEPTH, RET_WIDTH), 0.01)
    inp['ret_gn_b'] = nrm((DEPTH, RET_WIDTH), 0.01)
    inp['w_out'] = nrm((DEPTH, D_MODEL, D_MODEL), BETA * D_MODEL ** -0.5)
    inp['ln1_g'] = 1.0 + nrm((DEPTH, D_MODEL), 0.01)
    inp['ln1_b'] = nrm((DEPTH, D_MODEL), 0.01)
    inp['ffn_w_up'] = nrm((DEPTH, D_MODEL, 2 * D_FF), D_MODEL ** -0.5)
    inp['ffn_conv_w'] = nrm((DEPTH, CONV_W, 2 * D_FF), CONV_W ** -0.5)
    inp['ffn_conv_b'] = nrm((DEPTH, 2 * D_FF), 0.01)
    inp['ffn_w_down'] = nrm((DEPTH, D_FF, D_MODEL), BETA * D_FF ** -0.5)
    inp['ln2_g'] = 1.0 + nrm((DEPTH, D_MODEL), 0.01)
    inp['ln2_b'] = nrm((DEPTH, D_MODEL), 0.01)
    return inp

def reference(x_prompt, x_sample, cache_k, cache_v, state_s5_re, state_s5_im, state_ret, state_conv,
              page_table, ln_in_g, ln_in_b, w_in, s5_lambda_re, s5_lambda_im, s5_log_step,
              s5_b_re, s5_b_im, s5_c_re, s5_c_im, s5_d, s5_w_glu, norm_a_g, norm_b_g, sb_logit_bias,
              ret_gn_g, ret_gn_b, w_out, ln1_g, ln1_b, ffn_w_up, ffn_conv_w, ffn_conv_b,
              ffn_w_down, ln2_g, ln2_b):
    xp = layer_norm(x_prompt, ln_in_g, ln_in_b)
    xs = layer_norm(x_sample, ln_in_g, ln_in_b)
    bp = xp.shape[0]
    pos_p = jnp.arange(xp.shape[1], dtype=F32)
    pos_s = PAST_LEN + jnp.arange(xs.shape[1], dtype=F32)
    zero_s5 = jnp.zeros((bp, S5_GROUPS, S5_STATE), F32)
    zero_ret = jnp.zeros((bp, RET_HEADS, RET_DK, RET_DV), F32)
    zero_conv = jnp.zeros((bp, CONV_W - 1, 2 * D_FF), xp.dtype)
    out_p, out_s = [], []
    for l in range(DEPTH):
        p = dict(w_in=w_in[l], lam_re=s5_lambda_re[l], lam_im=s5_lambda_im[l], log_step=s5_log_step[l],
                 b_re=s5_b_re[l], b_im=s5_b_im[l], c_re=s5_c_re[l], c_im=s5_c_im[l], d=s5_d[l],
                 w_glu=s5_w_glu[l], norm_a_g=norm_a_g[l], norm_b_g=norm_b_g[l], sb_bias=sb_logit_bias[l],
                 gn_g=ret_gn_g[l], gn_b=ret_gn_b[l], w_out=w_out[l], ln1_g=ln1_g[l], ln1_b=ln1_b[l],
                 w_up=ffn_w_up[l], conv_w=ffn_conv_w[l], conv_b=ffn_conv_b[l], w_down=ffn_w_down[l],
                 ln2_g=ln2_g[l], ln2_b=ln2_b[l])
        xp, st_p = trunk_layer(xp, pos_p, zero_s5, zero_s5, zero_ret, zero_conv, sb_prompt, p)
        xs, st_s = trunk_layer(xs, pos_s, state_s5_re[l], state_s5_im[l], state_ret[l], state_conv[l],
                               make_sb_sample(cache_k[l], cache_v[l], page_table), p)
        out_p.append(st_p)
        out_s.append(st_s)
    stk = lambda outs, i: jnp.stack([o[i] for o in outs], axis=0)
    return (xp, xs,
            stk(out_p, 0), stk(out_p, 1), stk(out_s, 0), stk(out_s, 1),
            stk(out_p, 2), stk(out_p, 3), stk(out_s, 2), stk(out_s, 3),
            stk(out_p, 4), stk(out_s, 4),
            stk(out_p, 5), stk(out_s, 5))


_drawn_inputs = setup_inputs


def setup_inputs(seed=0):
    import zlib

    import numpy as np

    out = dict(_drawn_inputs(seed))
    spreads = {}
    factors = {'ln_in_g': 3.771,
     's5_lambda_re': 4.469,
     'norm_a_g': 8.0,
     'norm_b_g': 8.0,
     'ret_gn_g': 8.0,
     'ret_gn_b': 8.0,
     'ln1_g': 3.774,
     'ln1_b': 2.812,
     'ffn_conv_b': 8.0,
     'ln2_g': 3.832,
     'ln2_b': 3.185}
    for name, (base, spread) in spreads.items():
        noise = np.random.default_rng([zlib.crc32(name.encode()), seed]).standard_normal(out[name].shape)
        drawn = base * np.exp(spread * noise) if base else spread * noise
        out[name] = __import__('jax').numpy.asarray(drawn.astype(out[name].dtype))
    for name, factor in factors.items():
        out[name] = (out[name] * factor).astype(out[name].dtype)
    return out
```

```python
import math
from contextlib import ExitStack

import numpy as np

import concourse.bass as bass
from concourse import mybir

F32 = mybir.dt.float32
ALU = mybir.AluOpType
ACT = mybir.ActivationFunctionType

P = 128
SEQ, NS = 256, 8
T = SEQ + NS
DEPTH, D_MODEL, D_FF = 2, 1024, 2816
KT = D_MODEL // P
FT = D_FF // P
HEADS, DH, DV = 4, 64, 128
PAGES, PAGE, POOL = 2, 128, 20
ALPHA = (2.0 * DEPTH) ** 0.25
LN_EPS, RMS_EPS = 1e-5, 1e-6
J = 8
HJ = J // 2
DEC = 384

IN_ORDER = [0, 1, 10, 11, 8, 9, 12, 13, 14, 15, 4, 5, 2, 3, 6, 7, 16, 17, 18, 19]
U, KC, QC, VC, KB, QB_, VB_, GC = 0, 2, 4, 6, 10, 12, 14, 16
N_IN, N_OUT, N_UP = len(IN_ORDER), KT, 2 * FT
N_DOWN = KT * FT // 8
UNITS = N_IN + N_OUT + N_UP + N_DOWN
RING = 6
TILES = N_IN + N_OUT + N_UP + KT

PER = {"norm_a_g": 2, "norm_b_g": 2, "gn_g": 4, "gn_b": 4, "ln1_g": 8, "ln1_b": 8, "ln2_g": 8,
       "ln2_b": 8, "s5_d": 2, "cw0": N_UP, "cw1": N_UP, "cw2": N_UP, "cb": N_UP, "bias": HEADS}
COL, _at = {}, 2 * KT
for _n, _w in PER.items():
    COL[_n] = _at
    _at += _w
PER_LAYER = _at - 2 * KT
N_VEC = 2 * KT + DEPTH * PER_LAYER

CONSTS = ["ident", "tri", "ones", "mask", "perm", "mean_d", "mean_w", "mean_v"]
LOG_GAMMA = np.log1p(-np.exp2(-5.0 - np.arange(HEADS)))
TWO_PI = 2.0 * math.pi
TWO_PI_HI = float(np.float32(6.28125))
TWO_PI_LO = TWO_PI - TWO_PI_HI
PI_SAFE = 3.1415925
TWO_PI_IN = 6.283185
ROUND = 1.5 * 2.0**23
ROUND_15 = 1.5 * 2.0**8


def hybrid_step(nc, A, O):
    with ExitStack() as ctx:
        def sb(name, shape, dt=F32):
            return ctx.enter_context(nc.sbuf_tensor(name, shape, dt))

        sems = {}

        def S(name):
            if name not in sems:
                sems[name] = ctx.enter_context(nc.semaphore(name))
            return sems[name]

        ring = sb("ring", [P, RING, 8, P])
        x = sb("x", [P, KT, T])
        z = sb("z", [P, KT, T])
        hb = sb("hb", [P, N_IN, T])
        work = sb("work", [P, 6, HJ, T])
        BR, BI, P1, P2, P3, P4 = (work[:, i] for i in range(6))
        hff = work[:].rearrange("p a b t -> p (a b) t")
        turn = sb("turn", [P, 2, HJ, T])
        TC, TS = turn[:, 0, :, 0:SEQ], turn[:, 1, :, 0:SEQ]
        ZT = sb("ZT", [P, 2, 1600])
        Z, SPL = ZT[:, 0], ZT[:, 1]
        tmp = ZT[:].rearrange("p a b -> p (a b)")[:, 0:12 * 264].rearrange("p (a b) -> p a b", b=264)
        s5in = sb("s5in", [P, 3, 264])
        s5b = sb("s5b", [P, 2, 256])
        bb = sb("bb", [P, 2, 256])
        s5c = sb("s5c", [P, 2, J, 32])
        s5x0 = sb("s5x0", [P, 2, J, NS])
        are, aim, mag, fhi, flo = (sb(n, [P, J]) for n in ("are", "aim", "mag", "fhi", "flo"))
        stmp = sb("stmp", [P, 4, HJ, NS])
        s5o = sb("s5o", [P, 2, J, NS + 1])
        wglu = sb("wglu", [P, 2, 256])
        yd = sb("yd", [P, 2, T])
        yg = sb("yg", [P, 2, T])
        yb = sb("yb", [P, 2, T])
        sg = yb
        sq2 = sb("sq2", [P, 2, T])
        rs2 = sb("rs2", [P, T])
        lnr = sb("lnr", [P, T])
        kv = sb("kv", [P, NS, PAGES, 256])
        qbd = sb("qbd", [P, 2, NS, 2])
        VBt = sb("VBt", [P, 2, 256])
        SR = sb("SR", [P, NS, 2, DV])
        VBC = sb("VBC", [P, NS, 2, DV])
        eps_all, halfpi = sb("eps_all", [P, 2]), sb("halfpi", [P, 1])
        eps_t = {LN_EPS: eps_all[:, 0:1], RMS_EPS: eps_all[:, 1:2]}
        VS = sb("VS", [NS, HEADS * DV])
        RI = sb("RI", [P, HEADS, DEC])
        sqo = RI[:].rearrange("p a b -> p (a b)")[:, 0:HEADS * T].rearrange("p (a b) -> p a b", b=T)
        rg = turn[:, 0]
        KD = sb("KD", [P, 2, 256])
        VT = sb("VT", [P, 2, HEADS * DV])
        Oh = sb("Oh", [P, HEADS, T])
        RSO = sb("RSO", [P, 2, DV])
        qs = sb("qs", [P, 2, NS])
        conv = sb("conv", [P, 4, T])
        prev = sb("prev", [P, N_UP, 2, NS])
        spre = sb("spre", [P, N_UP, NS])
        cout = sb("cout", [P, N_UP, 10])
        vec = sb("vec", [P, N_VEC])
        cst = sb("cst", [P, len(CONSTS), P])
        dtab = sb("dtab", [P, HEADS, SEQ])
        rope = sb("rope", [P, 2, T])
        steps = sb("steps", [P, SEQ])
        kdec = sb("kdec", [P, 2, HEADS])
        gam = sb("gam", [P, 2])
        pidx = sb("pidx", [1, NS * PAGES], mybir.dt.int32)
        C = {n: cst[:, i] for i, n in enumerate(CONSTS)}
        ps = ctx.enter_context(nc.psum_tensor("ps", [P, 8, 512], F32))
        vs_dram = [nc.dram_tensor(f"vs_scratch{l}", [NS, HEADS * DV], F32, kind="Internal").ap()
                   for l in range(DEPTH)]

        def pv(L, name, i=0, n=1):
            c = L * PER_LAYER + COL[name] + i
            return vec[:, c:c + n]

        per = {}

        class Engine:

            def __init__(self, eng, own):
                self.eng, self.own, self.n, self.last = eng, own, {}, None

            def did(self, ins, name=None):
                name = name or self.own
                ins.then_inc(S(name), 1)
                self.n[name] = self.n.get(name, 0) + 1
                self.last = (name, self.n[name])

            def settle(self):
                if self.last:
                    self.eng.wait_ge(S(self.last[0]), self.last[1])

        def need(eng, name, L, k):
            eng.wait_ge(S(name), L * PERL.get(name, 0) + k)

        PERL = {"tile": TILES, "in_evac": N_IN, "z": 16, "lnmean": 2, "lnd": 4, "lnsq": 4, "lnvar": 2,
                "lnv1": 2, "lnr": 2, "x": 16, "bb": 1, "tph": 2, "tab": 4, "cneg": 1, "bu": 16, "buev": 16,
                "pre": 2, "poolpre": 2, "scan": 2, "poolpost": 2, "s5x": 2, "s5y": 2, "yd": 2, "gelu": 2,
                "glu": 2, "sig": 2, "ya": 1, "sqa": 1, "rmsa": 1, "rmsar": 1, "cata": 2,
                "rot": 4, "rotrd": 4, "qk": 1, "trk": 1, "kd": 1, "trv": 2, "vt": 2, "trvb": 1, "vbt": 1,
                "trvs": 1, "vs": 1, "rin": 4, "ri": 4, "rstate": 1, "rso": 1, "srg": 2, "sr": 1, "qs": 1,
                "ro": 4, "oev": 4, "gmean": 4, "gd": 4, "gsq": 4, "gvar": 4, "gv1": 4, "gr": 4, "sgc": 1,
                "catc": 4, "qb": 2, "sbz": 4, "zev": 4, "sbzs": 1, "zs": 1, "absz": 1, "spe": 1, "spl": 1,
                "sbs": 4, "zsub": 4, "sbss": 1, "zsubs": 1, "zmin": 1, "wexp": 1, "w": 1, "sby": 2, "ybev": 2,
                "sbys": 1, "ybs": 1, "sqb": 1, "rmsb": 1, "rmsbr": 1, "catb": 2,
                "up_free": N_UP, "fc": N_UP, "fs": FT, "hff": FT, "spre": 1, "used": UNITS}

        def ring_slot(n):
            return n % RING

        block = ctx.enter_context(nc.Block())

        @block.sync
        def _(sp):
            sp.dma_start(x[:], A["xT"]).then_inc(S("ld_x"), 16)
            sp.dma_start(cst[:], A["cst"]).then_inc(S("ld_cst"), 16)
            sp.dma_start(vec[:], A["vec"]).then_inc(S("ld_vec"), 16)
            sp.dma_start(steps[:], A["steps"]).then_inc(S("ld_steps"), 16)
            sp.dma_start(pidx[:], A["pages"]).then_inc(S("ld_pages"), 16)

            def layer_params(L):
                if L > 0:
                    need(sp, "s5y", L - 1, 2)
                    need(sp, "bb", L - 1, 1)
                    need(sp, "glu", L - 1, 2)
                    need(sp, "bu", L - 1, 16)
                    sp.wait_ge(S("dve_x0"), L * 2)
                sp.dma_start(s5in[:], A["s5in"][L]).then_inc(S("ld_s5in"), 16)
                sp.dma_start(s5b[:], A["s5b"][L]).then_inc(S("ld_s5b"), 16)
                sp.dma_start(s5c[:], A["s5c"][L]).then_inc(S("ld_s5c"), 16)
                sp.dma_start(s5x0[:], A["s5x0"][L]).then_inc(S("ld_x0"), 16)
                sp.dma_start(wglu[:], A["wglu"][L]).then_inc(S("ld_wglu"), 16)

            def unit(L, i):
                n = L * UNITS + i
                if n >= RING:
                    sp.wait_ge(S("used"), n - RING + 1)
                sp.dma_start(ring[:, ring_slot(n)], A["units"][n]).then_inc(S(f"ld_w{ring_slot(n)}"), 16)

            def pages(L, what):
                for s in range(NS * PAGES):
                    idx = sp.value_load(pidx[0:1, s:s + 1], min_val=0, max_val=POOL - 1)
                    src = A[what][L][bass.ds(idx, 1)].rearrange("a p c -> p (a c)")
                    sp.dma_start(kv[:, s // PAGES, s % PAGES], src).then_inc(S("ld_kv"), 16)

            layer_params(0)
            for L in range(DEPTH):
                for i in range(4):
                    unit(L, i)
                if L == 0:
                    sp.dma_start(rope[:], A["rope"]).then_inc(S("ld_rope"), 16)
                    sp.dma_start(dtab[:], A["dtab"]).then_inc(S("ld_dtab"), 16)
                    sp.dma_start(kdec[:], A["kdec"]).then_inc(S("ld_kdec"), 16)
                    sp.dma_start(gam[:], A["gam"]).then_inc(S("ld_gam"), 16)
                    sp.wait_ge(S("ld_pages"), 16)
                else:
                    sp.wait_ge(S("st_sr"), 16 * L)
                    need(sp, "sbys", L - 1, 1)
                    need(sp, "spre", L - 1, 1)
                    sp.wait_ge(S("st_prev"), 16 * L)
                pages(L, "kpool")
                sp.dma_start(SR[:], A["sret"][L]).then_inc(S("ld_sr"), 16)
                for i in range(4, N_IN + RING):
                    unit(L, i)
                sp.dma_start(prev[:], A["prev"][L]).then_inc(S("ld_prev"), 16)
                need(sp, "sbzs", L, 1)
                pages(L, "vpool")
                for i in range(N_IN + RING, UNITS):
                    unit(L, i)
                    if i == N_IN + N_OUT + N_UP // 2 and L + 1 < DEPTH:
                        layer_params(L + 1)

        @block.tensor
        def _(pe):
            E = Engine(pe, "pe_step")
            mm = nc.tensor.matmul
            holder = {}
            freed = []

            def claim(bank, reader, L, k):
                if bank in holder:
                    need(pe, *holder[bank])
                holder[bank] = (reader, L, k)
                return ps[:, bank]

            def main_bank(reader, L, k):
                n = len(freed)
                if n >= 4:
                    need(pe, *freed[n - 4])
                freed.append((reader, L, k))
                return ps[:, n % 4, 0:T]

            def unit_ready(n):
                pe.wait_ge(S(f"ld_w{ring_slot(n)}"), 16 * (n // RING + 1))

            def tile8(L, i, out, rhs):
                n = L * UNITS + i
                unit_ready(n)
                for k in range(8):
                    ins = mm(out, ring[:, ring_slot(n), k], rhs(k), start=(k == 0), stop=(k == 7))
                    if k == 7:
                        E.did(ins, "used")

            def ln_mean(L, k, ready):
                bank = claim(4, "lnd" if L is not None else "lnd0", L or 0, 2 * k)
                for t in range(KT):
                    ready(t)
                    ins = mm(bank[:, 0:T], C["mean_d"], z[:, t] if L is not None else x[:, t],
                             start=(t == 0), stop=(t == KT - 1))
                E.did(ins, "lnmean" if L is not None else "lnmean0")

            def ln_var(L, k):
                sfx = "" if L is not None else "0"
                bank = claim(5, "lnv1" + sfx, L or 0, k)
                for t in range(KT):
                    if t % 4 == 0:
                        need(pe, "lnsq" + sfx, L or 0, 2 * (k - 1) + t // 4 + 1)
                    ins = mm(bank[:, 0:T], C["mean_d"], hb[:, t], start=(t == 0), stop=(t == KT - 1))
                E.did(ins, "lnvar" + sfx)

            def s5_b(L, hf):
                if hf == 0:
                    need(pe, "bb", L, 1)
                for jj in range(HJ):
                    for c in range(2):
                        k = 8 * hf + 2 * jj + c + 1
                        bank = claim(4 + 2 * (jj % 2) + c, "buev", L, k)
                        E.did(mm(bank[:, 0:T], bb[32 * jj:32 * jj + 32, c, hf * P:(hf + 1) * P],
                                 hb[32 * jj:32 * jj + 32, U + hf], start=True, stop=True), "bu")

            def s5_c(L, hf):
                need(pe, "s5x", L, hf + 1)
                if hf == 0:
                    need(pe, "cneg", L, 1)
                bank = claim(4, "yd", L, hf + 1)
                for jj in range(HJ):
                    o = bank[32 * jj:32 * jj + 32, 0:T]
                    j = hf * HJ + jj
                    mm(o, s5c[:, 0, j], P1[:, jj], start=True, stop=False, tile_position=(0, 32 * jj))
                    ins = mm(o, s5c[:, 1, j], P3[:, jj], start=False, stop=True, tile_position=(0, 32 * jj))
                E.did(ins, "s5y")

            def s5_glu(L):
                need(pe, "gelu", L, 2)
                pe.wait_ge(S("ld_wglu"), 16 * (L + 1))
                for m in range(2):
                    bank = claim(6 + m, "sig", L, m + 1)
                    for k in range(2):
                        ins = mm(bank[:, 0:T], wglu[:, k, m * P:(m + 1) * P], yg[:, k],
                                 start=(k == 0), stop=(k == 1))
                    E.did(ins, "glu")

            def rms(L, sq, wait, reader, name):
                need(pe, wait, L, 1)
                bank = claim(5, reader, L, 1)
                for k in range(2):
                    ins = mm(bank[:, 0:T], C["mean_w"], sq[:, k], start=(k == 0), stop=(k == 1))
                E.did(ins, name)

            def rotate(L):
                for i in range(4):
                    need(pe, "in_evac", L, KC + i + 1)
                    bank = claim(4 + i, "rotrd", L, i + 1)
                    E.did(mm(bank[:, 0:T], C["perm"], hb[:, KC + i], start=True, stop=True), "rot")

            def transposes(L):
                need(pe, "in_evac", L, VC + 4)
                for tt in range(2):
                    bank = claim(4 + tt, "vt", L, tt + 1)
                    for h in range(HEADS):
                        ins = nc.tensor.transpose(bank[:, h * P:(h + 1) * P],
                                                  hb[:, VC + h, tt * P:(tt + 1) * P], C["ident"])
                    E.did(ins, "trv")
                bank = claim(6, "vs", L, 1)
                for h in range(HEADS):
                    ins = nc.tensor.transpose(bank[0:NS, h * P:(h + 1) * P], hb[:, VC + h, SEQ:T], C["ident"])
                E.did(ins, "trvs")

            def k_transposes(L):
                need(pe, "qk", L, 1)
                bank = claim(7, "kd", L, 1)
                for tt in range(2):
                    for ht in range(2):
                        ins = nc.tensor.transpose(bank[:, tt * 256 + ht * P:tt * 256 + (ht + 1) * P],
                                                  hb[:, KC + ht, tt * P:(tt + 1) * P], C["ident"])
                E.did(ins, "trk")

            def causal(bank, kt, qt, h, k0, q0):
                r = slice(64 * (h % 2), 64 * (h % 2) + 64)
                kk, qq = hb[r, k0 + h // 2], hb[r, q0 + h // 2]
                mm(bank[:, 0:SEQ], kk[:, 0:P], qq[:, 0:SEQ], start=True, stop=True)
                return mm(bank[:, SEQ:DEC], kk[:, P:SEQ], qq[:, P:SEQ], start=True, stop=True)

            def ret_inner(L):
                for h in range(HEADS):
                    bank = claim(4 + h, "ri", L, h + 1)
                    E.did(causal(bank, None, None, h, KC, QC), "rin")

            def ret_state(L):
                need(pe, "kd", L, 1)
                need(pe, "vt", L, 2)
                bank = claim(4, "rso", L, 1)
                for h in range(HEADS):
                    o = bank[64 * (h % 2):64 * (h % 2) + 64, (h // 2) * DV:(h // 2 + 1) * DV]
                    for tt in range(2):
                        ins = mm(o, KD[:, tt, 64 * h:64 * h + 64], VT[:, tt, h * DV:(h + 1) * DV],
                                 start=(tt == 0), stop=(tt == 1))
                E.did(ins, "rstate")

            def ret_out(L):
                need(pe, "sr", L, 1)
                need(pe, "qs", L, 1)
                need(pe, "vt", L, 2)
                for h in range(HEADS):
                    need(pe, "ri", L, h + 1)
                    bank = claim(4 + h, "oev", L, h + 1)
                    mm(bank[:, 0:SEQ], VT[:, 0, h * DV:(h + 1) * DV], RI[:, h, 0:SEQ], start=True, stop=False)
                    mm(bank[:, P:SEQ], VT[:, 1, h * DV:(h + 1) * DV], RI[:, h, SEQ:DEC], start=False, stop=True)
                    r = slice(64 * (h % 2), 64 * (h % 2) + 64)
                    for b in range(NS):
                        ins = mm(bank[:, SEQ + b:SEQ + b + 1], SR[r, b, h // 2], qs[r, h // 2, b:b + 1],
                                 start=True, stop=True)
                    E.did(ins, "ro")

            def group_norm(L):
                for h in range(HEADS):
                    need(pe, "oev", L, h + 1)
                    bank = claim(4 + h, "gd", L, h + 1)
                    E.did(mm(bank[:, 0:T], C["mean_v"], Oh[:, h], start=True, stop=True), "gmean")
                for h in range(HEADS):
                    need(pe, "gsq", L, h + 1)
                    bank = claim(4 + h, "gv1", L, h + 1)
                    E.did(mm(bank[:, 0:T], C["mean_v"], sqo[:, h], start=True, stop=True), "gvar")

            def vb_transposes(L):
                need(pe, "in_evac", L, VB_ + 2)
                bank = claim(4, "vbt", L, 1)
                for tt in range(2):
                    for ht in range(2):
                        ins = nc.tensor.transpose(bank[:, tt * 256 + ht * P:tt * 256 + (ht + 1) * P],
                                                  hb[:, VB_ + ht, tt * P:(tt + 1) * P], C["ident"])
                E.did(ins, "trvb")

            def sb_scores(L):
                need(pe, "in_evac", L, QB_ + 2)
                for h in range(HEADS):
                    bank = claim(4 + h, "zev", L, h + 1)
                    E.did(causal(bank, None, None, h, KB, QB_), "sbz")
                need(pe, "qb", L, 2)
                pe.wait_ge(S("ld_kv"), 16 * NS * PAGES * (2 * L + 1))
                bank = claim(4, "zs", L, 1)
                for pg in range(PAGES):
                    for b in range(NS):
                        for ht in range(2):
                            c = 32 * pg + 4 * b + 2 * ht
                            ins = mm(bank[:, c:c + 2], kv[:, b, pg, ht * P:(ht + 1) * P], qbd[:, ht, b],
                                     start=True, stop=True)
                E.did(ins, "sbzs")

            def sb_tails(L):
                need(pe, "spl", L, 1)
                for h in range(HEADS):
                    bank = claim(4 + h, "zsub", L, h + 1)
                    s0, s1 = SPL[:, h * DEC:h * DEC + SEQ], SPL[:, h * DEC + SEQ:(h + 1) * DEC]
                    mm(bank[:, 0:SEQ], C["tri"], s0, start=True, stop=False)
                    mm(bank[:, P:SEQ], C["ones"], s1, start=False, stop=True)
                    E.did(mm(bank[:, SEQ:DEC], C["tri"], s1, start=True, stop=True), "sbs")
                bank = claim(4, "zsubs", L, 1)
                s0, s1 = SPL[:, 4 * DEC:4 * DEC + 32], SPL[:, 4 * DEC + 32:4 * DEC + 64]
                mm(bank[:, 0:32], C["tri"], s0, start=True, stop=False)
                mm(bank[:, 0:32], C["ones"], s1, start=False, stop=True)
                E.did(mm(bank[:, 32:64], C["tri"], s1, start=True, stop=True), "sbss")

            def sb_values(L):
                need(pe, "w", L, 1)
                need(pe, "vbt", L, 1)
                for ht in range(2):
                    bank = claim(4 + ht, "ybev", L, ht + 1)
                    for h in (2 * ht, 2 * ht + 1):
                        r = 64 * (h % 2)
                        o = bank[r:r + 64]
                        w0, w1 = Z[:, h * DEC:h * DEC + SEQ], Z[:, h * DEC + SEQ:(h + 1) * DEC]
                        mm(o[:, 0:SEQ], VBt[:, 0, 64 * h:64 * h + 64], w0, start=True, stop=False,
                           tile_position=(0, r))
                        ins = mm(o[:, P:SEQ], VBt[:, 1, 64 * h:64 * h + 64], w1, start=False, stop=True,
                                 tile_position=(0, r))
                    E.did(ins, "sby")
                pe.wait_ge(S("ld_kv"), 16 * NS * PAGES * (2 * L + 2))
                bank = claim(6, "ybs", L, 1)
                for ht in range(2):
                    for b in range(NS):
                        for pg in range(PAGES):
                            wc = 4 * DEC + 32 * pg + 4 * b + 2 * ht
                            oc = 16 * ht + 2 * b
                            ins = mm(bank[:, oc:oc + 2], kv[:, b, pg, ht * P:(ht + 1) * P], Z[:, wc:wc + 2],
                                     start=(pg == 0), stop=(pg == 1))
                E.did(ins, "sbys")

            pe.wait_ge(S("ld_x"), 16)
            pe.wait_ge(S("ld_cst"), 16)
            ln_mean(None, 1, lambda t: None)
            ln_var(None, 1)
            for L in range(DEPTH):
                for i in range(N_IN):
                    out = main_bank("in_evac", L, i + 1)
                    if i == 0:
                        if L == 0:
                            pe.wait_ge(S("x0"), KT)
                        else:
                            need(pe, "x", L - 1, 16)
                    tile8(L, i, out, lambda k: x[:, k])
                    if i == 3:
                        need(pe, "in_evac", L, 2)
                        s5_b(L, 0)
                    if i == 7:
                        rotate(L)
                    if i == 10:
                        transposes(L)
                    if i == 13:
                        k_transposes(L)
                        ret_inner(L)
                        s5_c(L, 0)
                        s5_b(L, 1)
                    if i == 16:
                        ret_state(L)
                        vb_transposes(L)
                sb_scores(L)
                ret_out(L)
                sb_tails(L)
                group_norm(L)
                sb_values(L)
                rms(L, sq2, "sqb", "rmsbr", "rmsb")
                s5_c(L, 1)
                s5_glu(L)
                rms(L, sq2, "sqa", "rmsar", "rmsa")
                cat = [hb[:, U], hb[:, U + 1], hb[:, QB_], hb[:, QB_ + 1]] + [hb[:, GC + h] for h in range(4)]
                for i in range(N_OUT):
                    out = main_bank("z", L, i + 1)
                    if i == 0:
                        need(pe, "cata", L, 2)
                        need(pe, "catb", L, 2)
                        need(pe, "catc", L, 4)
                    tile8(L, N_IN + i, out, lambda k: cat[k])
                ln_mean(L, 1, lambda t: need(pe, "z", L, t + 1))
                ln_var(L, 1)
                for i in range(N_UP):
                    out = main_bank("up_free", L, i + 1)
                    if i == 0:
                        need(pe, "x", L, 8)
                    tile8(L, N_IN + N_OUT + i, out, lambda k: x[:, k])
                for m in range(KT):
                    out = main_bank("z", L, 8 + m + 1)
                    for k in range(FT):
                        blk = m * FT + k
                        n = L * UNITS + N_IN + N_OUT + N_UP + blk // 8
                        if blk % 8 == 0:
                            unit_ready(n)
                        if m == 0:
                            need(pe, "hff", L, k + 1)
                        ins = mm(out, ring[:, ring_slot(n), blk % 8], hff[:, k], start=(k == 0), stop=(k == FT - 1))
                        if blk % 8 == 7:
                            E.did(ins, "used")
                        elif k == FT - 1:
                            E.did(ins, "down")
                ln_mean(L, 2, lambda t: need(pe, "z", L, 8 + t + 1))
                ln_var(L, 2)

        def tile_done(eng, L, i):
            eng.wait_ge(S("used"), L * UNITS + i + 1)

        def down_done(eng, L, m):
            last = (m + 1) * FT - 1
            if last % 8 == 7:
                eng.wait_ge(S("used"), L * UNITS + N_IN + N_OUT + N_UP + last // 8 + 1)
            else:
                ends = [q for q in range(KT) if ((q + 1) * FT) % 8 != 0]
                eng.wait_ge(S("down"), L * len(ends) + ends.index(m) + 1)

        def bcast(ap, shape, axis):
            return ap.unsqueeze(axis).to_broadcast(shape)

        @block.scalar
        def _(act):
            E = Engine(act, "act_step")
            f = nc.scalar.activation

            def inv_sqrt(dst, src, eps, first, last, settle_first=True):
                E.did(f(dst, src, ACT.Ln, bias=eps_t[eps]), first)
                E.settle()
                E.did(f(dst, dst, ACT.Exp, scale=-0.5), last)

            def ln(L, k):
                sfx = "" if L is not None else "0"
                LL = L or 0
                src = z
                for hf in range(2):
                    need(act, "lnd" + sfx, LL, 2 * (k - 1) + hf + 1)
                    E.did(f(hb[:, 4 * hf:4 * hf + 4], src[:, 4 * hf:4 * hf + 4], ACT.Square), "lnsq" + sfx)
                need(act, "lnvar" + sfx, LL, k)
                if k == 2:
                    need(act, "x", L, 8)
                elif L is not None:
                    need(act, "x", L - 1, 16) if L else act.wait_ge(S("x0"), 8)
                inv_sqrt(lnr[:], ps[:, 5, 0:T], LN_EPS, "lnv1" + sfx, "lnr" + sfx)

            def s5_params(L):
                act.wait_ge(S("ld_s5in"), 16 * (L + 1))
                if L > 0:
                    need(act, "w", L - 1, 1)
                    need(act, "sbys", L - 1, 1)
                act.wait_ge(S("v_s5clear"), L + 1)
                E.did(f(tmp[:, 0], s5in[:, 2], ACT.Exp), "a_dt")
                act.wait_ge(S("v_ldt"), L + 1)
                E.did(f(tmp[:, 2], tmp[:, 1], ACT.Exp), "a_mag")
                act.wait_ge(S("v_red"), L + 1)
                f(tmp[:, 5], tmp[:, 4], ACT.Sin)
                E.did(f(tmp[:, 6], tmp[:, 7], ACT.Sin, bias=halfpi[:], scale=-1.0), "a_sc")

            def s5_tables(L, hf):
                need(act, "tph", L, hf + 1)
                E.did(f(TS, TS, ACT.Sin, scale=TWO_PI_IN), "tab")
                E.did(f(TC, TC, ACT.Sin, bias=halfpi[:], scale=-TWO_PI_IN), "tab")

            def neg_c(L):
                act.wait_ge(S("ld_s5c"), 16 * (L + 1))
                E.did(nc.scalar.mul(s5c[:, 1], s5c[:, 1], -1.0), "cneg")

            act.wait_ge(S("eps_set"), 3)
            s5_params(0)
            ln(None, 1)
            s5_tables(0, 0)
            for L in range(DEPTH):
                for i in range(N_IN):
                    tile_done(act, L, i)
                    if L > 0 and i == 0:
                        act.wait_ge(S("st_k"), 16 * L)
                        act.wait_ge(S("st_kv"), 16 * L)
                    E.did(nc.scalar.copy(hb[:, i], ps[:, (L * TILES + i) % 4, 0:T]), "in_evac")
                    if i == 3:
                        neg_c(L)
                    if i in (3, 13):
                        hf = i // 10
                        for k in range(8):
                            need(act, "bu", L, 8 * hf + k + 1)
                            if k == 0 and hf == 1:
                                need(act, "s5x", L, 1)
                            E.did(nc.scalar.copy((BR, BI)[k % 2][:, k // 2], ps[:, 4 + k % 4, 0:T]), "buev")
                    if i == 10:
                        for tt in range(2):
                            need(act, "trv", L, tt + 1)
                            E.did(nc.scalar.copy(VT[:, tt], ps[:, 4 + tt]), "vt")
                        need(act, "trvs", L, 1)
                        E.did(nc.scalar.copy(VS[:], ps[0:NS, 6]), "vs")
                        E.settle()
                        act.dma_start(vs_dram[L], VS[:]).then_inc(S("st_vs"), 16)
                        act.wait_ge(S("ld_sr"), 16 * (L + 1))
                        act.wait_ge(S("ld_gam"), 16)
                        for ht in range(2):
                            E.did(nc.scalar.mul(SR[:, :, ht], SR[:, :, ht], gam[:, ht:ht + 1]), "srg")
                        act.wait_ge(S("st_vs"), 16 * (L + 1))
                        v5 = vs_dram[L].rearrange("b (a c e) -> c b a e", a=2, c=2)
                        for c in range(2):
                            act.dma_start(VBC[64 * c:64 * c + 64], v5[c:c + 1].to_broadcast([64, NS, 2, DV])
                                          ).then_inc(S("ld_vbc"), 16)
                    if i == 13:
                        s5_tables(L, 1)
                    if i == 16:
                        need(act, "rstate", L, 1)
                        if L > 0:
                            act.wait_ge(S("st_rso"), 16 * L)
                        E.did(nc.scalar.copy(RSO[:], ps[:, 4, 0:2 * DV].rearrange("p (a b) -> p a b", a=2)), "rso")
                        need(act, "trvb", L, 1)
                        E.did(nc.scalar.copy(VBt[:], ps[:, 4].rearrange("p (a b) -> p a b", a=2)), "vbt")
                E.settle()
                act.dma_start(O["kv"][L, :, 0:2], hb[:, KB:KB + 2]).then_inc(S("st_k"), 16)
                act.dma_start(O["kv"][L, :, 2:4], hb[:, VB_:VB_ + 2]).then_inc(S("st_kv"), 16)
                act.dma_start(O["rprompt"][L], RSO[:]).then_inc(S("st_rso"), 16)
                for h in range(HEADS):
                    need(act, "ro", L, h + 1)
                    E.did(nc.scalar.copy(Oh[:, h], ps[:, 4 + h, 0:T]), "oev")
                act.dma_start(O["rsample"][L], SR[:]).then_inc(S("st_sr"), 16)
                need(act, "absz", L, 1)
                E.did(f(SPL[:], SPL[:], ACT.Exp, scale=-1.0))
                E.settle()
                E.did(f(SPL[:], SPL[:], ACT.Ln, bias=1.0), "spe")
                for h in range(HEADS):
                    need(act, "gd", L, h + 1)
                    E.did(f(sqo[:, h], Oh[:, h], ACT.Square), "gsq")
                need(act, "zmin", L, 1)
                E.did(f(Z[:], Z[:], ACT.Exp), "wexp")
                for h in range(HEADS):
                    need(act, "gvar", L, h + 1)
                    inv_sqrt(rg[:, h], ps[:, 4 + h, 0:T], LN_EPS, "gv1", "gr")
                E.did(f(hb[:, GC:GC + 4], hb[:, GC:GC + 4], ACT.Silu), "sgc")
                need(act, "ybev", L, 2)
                need(act, "ybs", L, 1)
                E.did(f(sq2[:], yb[:], ACT.Square), "sqb")
                need(act, "rmsb", L, 1)
                E.did(f(rs2[:], ps[:, 5, 0:T], ACT.Ln, bias=eps_t[RMS_EPS]))
                E.settle()
                E.did(f(rs2[:], rs2[:], ACT.Exp, scale=-0.5), "rmsbr")
                for hf in range(2):
                    need(act, "yd", L, hf + 1)
                    E.did(f(yg[:, hf], yd[:, hf], ACT.Gelu_apprx_tanh), "gelu")
                need(act, "catb", L, 2)
                for m in range(2):
                    need(act, "glu", L, m + 1)
                    E.did(f(sg[:, m], ps[:, 6 + m, 0:T], ACT.Sigmoid), "sig")
                need(act, "ya", L, 1)
                E.did(f(sq2[:], yg[:], ACT.Square), "sqa")
                need(act, "rmsa", L, 1)
                E.did(f(rs2[:], ps[:, 5, 0:T], ACT.Ln, bias=eps_t[RMS_EPS]))
                E.settle()
                E.did(f(rs2[:], rs2[:], ACT.Exp, scale=-0.5), "rmsar")
                ln(L, 1)
                for i in range(N_UP):
                    tile_done(act, L, N_IN + N_OUT + i)
                    if i == 0:
                        act.wait_ge(S("ld_vec"), 16)
                    if i >= 4:
                        need(act, "hff", L, (i - 4) // 2 + 1)
                    elif L > 0:
                        need(act, "hff", L - 1, FT)
                    E.did(f(conv[:, i % 4], ps[:, (L * TILES + N_IN + N_OUT + i) % 4, 0:T], ACT.Identity,
                            scale=pv(L, "cw2", i), bias=pv(L, "cb", i)), "fc")
                    if i % 2 == 1:
                        need(act, "up_free", L, i + 1)
                        E.did(f(conv[:, i % 4], conv[:, i % 4], ACT.Silu), "fs")
                if L + 1 < DEPTH:
                    s5_params(L + 1)
                    s5_tables(L + 1, 0)
                ln(L, 2)
            for name, n in (("st_k", DEPTH), ("st_kv", DEPTH), ("st_rso", DEPTH), ("st_sr", DEPTH), ("st_vs", DEPTH)):
                act.wait_ge(S(name), 16 * n)

        @block.vector
        def _(dve):
            E = Engine(dve, "dve_step")
            tt, ts, stt = nc.vector.tensor_tensor, nc.vector.tensor_scalar, nc.vector.scalar_tensor_tensor
            cp = nc.vector.tensor_copy

            E.did(nc.vector.memset(eps_all[:, 0:1], LN_EPS), "eps_set")
            E.did(nc.vector.memset(eps_all[:, 1:2], RMS_EPS), "eps_set")
            E.did(nc.vector.memset(halfpi[:], math.pi / 2), "eps_set")
            E.did(nc.vector.memset(qbd[:], 0.0))
            E.settle()

            def seq(*makers):
                for m in makers:
                    E.settle()
                    E.did(m())

            def ln(L, k, src):
                sfx = "" if L is not None else "0"
                LL = L or 0
                need(dve, "lnmean" + sfx, LL, k)
                mean = bcast(ps[:, 4, 0:T], [P, 4, T], 1)
                for hf in range(2):
                    E.did(tt(z[:, 4 * hf:4 * hf + 4], src[:, 4 * hf:4 * hf + 4], mean, ALU.subtract), "lnd" + sfx)
                need(dve, "lnr" + sfx, LL, k)
                g, b = (vec[:, 0:8], vec[:, 8:16]) if L is None else (pv(L, f"ln{k}_g", 0, 8), pv(L, f"ln{k}_b", 0, 8))
                if L is None:
                    dve.wait_ge(S("ld_vec"), 16)
                E.settle()
                for hf in range(2):
                    E.did(tt(z[:, 4 * hf:4 * hf + 4], z[:, 4 * hf:4 * hf + 4], bcast(lnr[:], [P, 4, T], 1), ALU.mult))
                for t in range(KT):
                    if t == 0:
                        E.settle()
                    E.did(ts(x[:, t], z[:, t], g[:, t:t + 1], b[:, t:t + 1], ALU.mult, ALU.add), "x" + sfx)

            def s5_params(L):
                dve.wait_ge(S("ld_s5in"), 16 * (L + 1))
                lr, li = s5in[:, 0], s5in[:, 1]
                dt, ldr, mg, n, r, sn, cs, ab, den, t0, t1, t2 = (tmp[:, i] for i in range(12))
                E.did(ts(lr, lr, -1e-4, None, ALU.min), "v_s5clear")
                dve.wait_ge(S("a_dt"), L + 1)
                E.settle()
                E.did(tt(ldr, lr, dt, ALU.mult), "v_ldt")
                seq(lambda: tt(t0, li, dt, ALU.mult),
                    lambda: ts(n, t0, 1.0 / TWO_PI, ROUND, ALU.mult, ALU.add),
                    lambda: ts(n, n, -ROUND, None, ALU.add),
                    lambda: stt(r, n, -TWO_PI_HI, t0, ALU.mult, ALU.add),
                    lambda: stt(r, n, -TWO_PI_LO, r, ALU.mult, ALU.add),
                    lambda: ts(r, r, PI_SAFE, -PI_SAFE, ALU.min, ALU.max))
                E.settle()
                E.did(stt(ab, r, -1.0, r, ALU.mult, ALU.max), "v_red")
                E.settle()
                E.did(ts(fhi[:], r[:, 0:J], 1.0 / TWO_PI, ROUND_15, ALU.mult, ALU.add))
                seq(lambda: ts(fhi[:], fhi[:], -ROUND_15, None, ALU.add),
                    lambda: ts(t1[:, 0:J], r[:, 0:J], 1.0 / TWO_PI, None, ALU.mult),
                    lambda: tt(flo[:], t1[:, 0:J], fhi[:], ALU.subtract),
                    lambda: tt(den, lr, lr, ALU.mult),
                    lambda: tt(t1, li, li, ALU.mult),
                    lambda: tt(den, den, t1, ALU.add),
                    lambda: nc.vector.reciprocal(den, den))
                dve.wait_ge(S("a_sc"), L + 1)
                dve.wait_ge(S("a_mag"), L + 1)
                seq(lambda: cp(mag[:], mg[:, 0:J]),
                    lambda: tt(t0, mg, cs, ALU.mult),
                    lambda: tt(sn, mg, sn, ALU.mult),
                    lambda: cp(are[:], t0[:, 0:J]),
                    lambda: cp(aim[:], sn[:, 0:J]),
                    lambda: ts(t0, t0, -1.0, None, ALU.add),
                    lambda: tt(t1, t0, lr, ALU.mult),
                    lambda: tt(t2, sn, li, ALU.mult),
                    lambda: tt(t1, t1, t2, ALU.add),
                    lambda: tt(t1, t1, den, ALU.mult),
                    lambda: tt(sn, sn, lr, ALU.mult),
                    lambda: tt(t0, t0, li, ALU.mult),
                    lambda: tt(t0, sn, t0, ALU.subtract),
                    lambda: tt(t0, t0, den, ALU.mult))
                dve.wait_ge(S("ld_s5b"), 16 * (L + 1))
                fr, fi = t1[:, J:264], t0[:, J:264]
                seq(lambda: tt(bb[:, 0], fr, s5b[:, 0], ALU.mult),
                    lambda: tt(t2[:, 0:256], fi, s5b[:, 1], ALU.mult),
                    lambda: tt(bb[:, 0], bb[:, 0], t2[:, 0:256], ALU.subtract),
                    lambda: tt(bb[:, 1], fr, s5b[:, 1], ALU.mult),
                    lambda: tt(t2[:, 0:256], fi, s5b[:, 0], ALU.mult))
                E.settle()
                E.did(tt(bb[:, 1], bb[:, 1], t2[:, 0:256], ALU.add), "bb")

            def s5_phases(L, hf):
                if L == 0 and hf == 0:
                    dve.wait_ge(S("ld_steps"), 16)
                p, q = TS, TC
                st = bcast(steps[:], [P, HJ, SEQ], 1)
                fh = bcast(fhi[:, hf * HJ:(hf + 1) * HJ], [P, HJ, SEQ], 2)
                fl = bcast(flo[:, hf * HJ:(hf + 1) * HJ], [P, HJ, SEQ], 2)
                seq(lambda: tt(p, st, fh, ALU.mult),
                    lambda: ts(q, p, ROUND, -ROUND, ALU.add, ALU.add),
                    lambda: tt(p, p, q, ALU.subtract),
                    lambda: tt(q, st, fl, ALU.mult),
                    lambda: tt(p, p, q, ALU.add),
                    lambda: ts(q, p, ROUND, -ROUND, ALU.add, ALU.add),
                    lambda: tt(p, p, q, ALU.subtract))
                E.settle()
                E.did(stt(q, p, -1.0, p, ALU.mult, ALU.max), "tph")

            def s5_half(L, hf):
                tm = slice(0, SEQ)
                need(dve, "buev", L, 8 * hf + 8)
                need(dve, "tab", L, 2 * hf + 2)
                if hf == 1:
                    need(dve, "s5y", L, 1)
                E.did(tt(P1[:, :, tm], TC, BR[:, :, tm], ALU.mult))
                E.did(tt(P2[:, :, tm], TS, BI[:, :, tm], ALU.mult))
                E.settle()
                E.did(tt(P1[:, :, tm], P1[:, :, tm], P2[:, :, tm], ALU.add))
                need(dve, "poolpre", L, hf + 1)
                E.did(tt(P3[:, :, tm], P3[:, :, tm], P4[:, :, tm], ALU.subtract))
                E.settle()
                for jj in range(HJ):
                    m = mag[:, hf * HJ + jj:hf * HJ + jj + 1].to_broadcast([P, SEQ])
                    E.did(nc.vector.tensor_tensor_scan(BR[:, jj, tm], m, P1[:, jj, tm], 0.0, ALU.mult, ALU.add))
                    ins = nc.vector.tensor_tensor_scan(BI[:, jj, tm], m, P3[:, jj, tm], 0.0, ALU.mult, ALU.add)
                    E.did(ins, "scan" if jj == HJ - 1 else None)
                E.settle()
                E.did(tt(P1[:, :, tm], TC, BR[:, :, tm], ALU.mult))
                E.did(tt(P2[:, :, tm], TS, BI[:, :, tm], ALU.mult))
                E.settle()
                E.did(tt(P1[:, :, tm], P1[:, :, tm], P2[:, :, tm], ALU.subtract))
                if hf == 0:
                    dve.wait_ge(S("ld_x0"), 16 * (L + 1))
                jr = slice(hf * HJ, (hf + 1) * HJ)
                ar, ai = bcast(are[:, jr], [P, HJ, NS], 2), bcast(aim[:, jr], [P, HJ, NS], 2)
                x0r, x0i = s5x0[:, 0, jr], s5x0[:, 1, jr]
                E.did(tt(stmp[:, 0], ar, x0r, ALU.mult))
                E.did(tt(stmp[:, 1], ai, x0i, ALU.mult))
                E.did(tt(stmp[:, 2], ar, x0i, ALU.mult))
                E.did(tt(stmp[:, 3], ai, x0r, ALU.mult), "dve_x0")
                E.settle()
                E.did(tt(stmp[:, 0], stmp[:, 0], stmp[:, 1], ALU.subtract))
                E.did(tt(stmp[:, 2], stmp[:, 2], stmp[:, 3], ALU.add))
                E.settle()
                E.did(tt(P1[:, :, SEQ:T], stmp[:, 0], BR[:, :, SEQ:T], ALU.add))
                E.did(tt(P3[:, :, SEQ:T], stmp[:, 2], BI[:, :, SEQ:T], ALU.add))
                need(dve, "poolpost", L, hf + 1)
                E.settle()
                E.did(tt(P3[:, :, tm], P3[:, :, tm], P4[:, :, tm], ALU.add))
                E.settle()
                if L > 0 and hf == 0:
                    dve.wait_ge(S("st_s5"), 16 * L)
                E.did(cp(s5o[:, 0, jr], P1[:, :, SEQ - 1:T]))
                E.did(cp(s5o[:, 1, jr], P3[:, :, SEQ - 1:T]), "s5x")

            def rotary(L):
                if L == 0:
                    dve.wait_ge(S("ld_rope"), 16)
                qk = hb[:, KC:KC + 4]
                for i in range(4):
                    need(dve, "rot", L, i + 1)
                    if i == 0:
                        E.settle()
                    E.did(tt(P2[:, i], ps[:, 4 + i, 0:T], rope[:, 1], ALU.mult), "rotrd")
                E.settle()
                E.did(tt(qk, qk, bcast(rope[:, 0], [P, 4, T], 1), ALU.mult))
                E.settle()
                E.did(tt(qk, qk, P2[:], ALU.add), "qk")
                E.settle()
                E.did(ts(qs[:], hb[:, QC:QC + 2, SEQ:T], DH ** -0.5, None, ALU.mult), "qs")

            def ret_inner(L):
                if L == 0:
                    dve.wait_ge(S("ld_dtab"), 16)
                    dve.wait_ge(S("ld_kdec"), 16)
                need(dve, "trk", L, 1)
                kd = kdec[:].unsqueeze(3).to_broadcast([P, 2, HEADS, 64])
                for t2 in range(2):
                    E.did(tt(KD[:, t2].rearrange("p (h d) -> p h d", h=HEADS),
                             ps[:, 7, 256 * t2:256 * t2 + 256].rearrange("p (h d) -> p h d", h=HEADS),
                             kd[:, t2], ALU.mult), "kd" if t2 else None)
                for h in range(HEADS):
                    need(dve, "rin", L, h + 1)
                    E.did(tt(RI[:, h, 0:SEQ], ps[:, 4 + h, 0:SEQ], dtab[:, h], ALU.mult))
                    E.did(tt(RI[:, h, SEQ:DEC], ps[:, 4 + h, SEQ:DEC], dtab[:, h, 0:P], ALU.mult), "ri")

            def ret_samples(L):
                need(dve, "srg", L, 2)
                dve.wait_ge(S("ld_vbc"), 32 * (L + 1))
                for b in range(NS):
                    for ht in range(2):
                        last = b == NS - 1 and ht == 1
                        E.did(stt(SR[:, b, ht], VBC[:, b, ht], hb[:, KC + ht, SEQ + b:SEQ + b + 1], SR[:, b, ht],
                                  ALU.mult, ALU.add), "sr" if last else None)

            def query_blocks(L):
                need(dve, "in_evac", L, QB_ + 2)
                for c in range(2):
                    r = slice(64 * c, 64 * c + 64)
                    E.did(cp(qbd[r, :, :, c], hb[r, QB_:QB_ + 2, SEQ:T]), "qb")

            def sb_first(L):
                for h in range(HEADS):
                    need(dve, "sbz", L, h + 1)
                    E.did(ts(Z[:, h * DEC:(h + 1) * DEC], ps[:, 4 + h, 0:DEC], DH ** -0.5, pv(L, "bias", h),
                             ALU.mult, ALU.add), "zev")
                need(dve, "sbzs", L, 1)
                E.did(stt(Z[:, 4 * DEC:4 * DEC + 64].rearrange("p (n h) -> p n h", h=HEADS),
                          ps[:, 4, 0:64].rearrange("p (n h) -> p n h", h=HEADS), DH ** -0.5,
                          bcast(pv(L, "bias", 0, HEADS), [P, 16, HEADS], 1), ALU.mult, ALU.add), "zs")
                E.settle()
                E.did(stt(SPL[:], Z[:], -1.0, Z[:], ALU.mult, ALU.max), "absz")

            def diagonals(buf):
                v = buf[:, 0:4 * DEC].rearrange("p (h c) -> p h c", h=HEADS)
                return v[:, :, 0:P], v[:, :, SEQ:DEC]

            mask = bcast(C["mask"], [P, HEADS, P], 1)

            def sb_second(L):
                need(dve, "spe", L, 1)
                E.did(stt(SPL[:], Z[:], 0.0, SPL[:], ALU.max, ALU.add))
                E.settle()
                d0, d1 = diagonals(SPL)
                E.did(tt(d0, d0, mask, ALU.mult))
                E.did(tt(d1, d1, mask, ALU.mult), "spl")

            def sb_third(L):
                for h in range(HEADS):
                    need(dve, "sbs", L, h + 1)
                    E.did(tt(Z[:, h * DEC:(h + 1) * DEC], Z[:, h * DEC:(h + 1) * DEC], ps[:, 4 + h, 0:DEC],
                             ALU.subtract), "zsub")
                need(dve, "sbss", L, 1)
                E.did(tt(Z[:, 4 * DEC:4 * DEC + 64], Z[:, 4 * DEC:4 * DEC + 64], ps[:, 4, 0:64], ALU.subtract), "zsubs")
                E.settle()
                E.did(ts(Z[:], Z[:], 0.0, None, ALU.min), "zmin")

            def sb_mask(L):
                need(dve, "wexp", L, 1)
                d0, d1 = diagonals(Z)
                E.did(tt(d0, d0, mask, ALU.mult))
                E.did(tt(d1, d1, mask, ALU.mult), "w")

            def sb_out(L):
                for ht in range(2):
                    need(dve, "sby", L, ht + 1)
                    E.did(cp(yb[:, ht, 0:SEQ], ps[:, 4 + ht, 0:SEQ]), "ybev")
                need(dve, "sbys", L, 1)
                for c in range(2):
                    r = slice(64 * c, 64 * c + 64)
                    E.did(cp(yb[r, :, SEQ:T], ps[r, 6, 0:32].rearrange("p (a b c) -> p a b c", a=2, c=2)[:, :, :, c]),
                          "ybs" if c else None)
                need(dve, "rmsbr", L, 1)
                E.settle()
                for t in range(2):
                    E.did(stt(hb[:, QB_ + t], yb[:, t], pv(L, "norm_b_g", t), rs2[:], ALU.mult, ALU.mult), "catb")

            def gn_center(L):
                for h in range(HEADS):
                    need(dve, "gmean", L, h + 1)
                    E.did(tt(Oh[:, h], Oh[:, h], ps[:, 4 + h, 0:T], ALU.subtract), "gd")

            def gn_out(L):
                for h in range(HEADS):
                    need(dve, "gr", L, h + 1)
                    E.settle()
                    E.did(tt(Oh[:, h], Oh[:, h], rg[:, h], ALU.mult))
                    E.settle()
                    E.did(ts(Oh[:, h], Oh[:, h], pv(L, "gn_g", h), pv(L, "gn_b", h), ALU.mult, ALU.add))
                need(dve, "sgc", L, 1)
                E.settle()
                for h in range(HEADS):
                    E.did(tt(hb[:, GC + h], Oh[:, h], hb[:, GC + h], ALU.mult), "catc")

            def s5_skip(L, hf):
                need(dve, "s5y", L, hf + 1)
                E.did(stt(yd[:, hf], hb[:, U + hf], pv(L, "s5_d", hf), ps[:, 4, 0:T], ALU.mult, ALU.add), "yd")

            def s5_out(L):
                need(dve, "sig", L, 2)
                E.did(tt(yg[:], yg[:], sg[:], ALU.mult), "ya")
                need(dve, "rmsar", L, 1)
                E.settle()
                for t in range(2):
                    E.did(stt(hb[:, U + t], yg[:, t], pv(L, "norm_a_g", t), rs2[:], ALU.mult, ALU.mult), "cata")

            def residual(L, first, i):
                bank = ps[:, (L * TILES + (N_IN if first else N_IN + N_OUT + N_UP) + i) % 4, 0:T]
                tile_done(dve, L, N_IN + i) if first else down_done(dve, L, i)
                E.did(stt(z[:, i], x[:, i], ALPHA, bank, ALU.mult, ALU.add), "z")

            s5_params(0)
            s5_phases(0, 0)
            ln(None, 1, x)
            for L in range(DEPTH):
                s5_half(L, 0)
                rotary(L)
                ret_inner(L)
                s5_skip(L, 0)
                s5_phases(L, 1)
                s5_half(L, 1)
                query_blocks(L)
                ret_samples(L)
                sb_first(L)
                sb_second(L)
                sb_third(L)
                gn_center(L)
                sb_mask(L)
                sb_out(L)
                gn_out(L)
                s5_skip(L, 1)
                s5_out(L)
                for i in range(N_OUT):
                    residual(L, True, i)
                ln(L, 1, z)
                dve.wait_ge(S("ld_prev"), 16 * (L + 1))
                if L > 0:
                    dve.wait_ge(S("st_conv"), 16 * L)
                w0 = bcast(pv(L, "cw0", 0, N_UP), [P, N_UP, NS], 2)
                w1 = bcast(pv(L, "cw1", 0, N_UP), [P, N_UP, NS], 2)
                c10 = cout[:, :, 2:10]
                E.did(tt(spre[:], prev[:, :, 0], w0, ALU.mult))
                E.did(tt(c10, prev[:, :, 1], w1, ALU.mult))
                E.settle()
                E.did(tt(spre[:], spre[:], c10, ALU.add), "spre")
                for i in range(N_UP):
                    need(dve, "fc", L, i + 1)
                    bank, c = ps[:, (L * TILES + N_IN + N_OUT + i) % 4], conv[:, i % 4]
                    E.settle()
                    E.did(cp(cout[:, i], bank[:, SEQ - 2:T]))
                    E.did(stt(c[:, 1:SEQ], bank[:, 0:SEQ - 1], pv(L, "cw1", i), c[:, 1:SEQ], ALU.mult, ALU.add))
                    E.did(tt(c[:, SEQ:T], c[:, SEQ:T], spre[:, i], ALU.add))
                    E.settle()
                    E.did(stt(c[:, 2:SEQ], bank[:, 0:SEQ - 2], pv(L, "cw0", i), c[:, 2:SEQ], ALU.mult, ALU.add), "up_free")
                    if i % 2 == 1:
                        need(dve, "fs", L, i // 2 + 1)
                        E.settle()
                        E.did(tt(hff[:, i // 2], conv[:, (i - 1) % 4], c, ALU.mult), "hff")
                if L + 1 < DEPTH:
                    s5_params(L + 1)
                    s5_phases(L + 1, 0)
                for i in range(KT):
                    residual(L, False, i)
                ln(L, 2, z)

        @block.gpsimd
        def _(pool):
            E = Engine(pool, "pool_step")
            tt = nc.gpsimd.tensor_tensor
            tm = slice(0, SEQ)
            for L in range(DEPTH):
                for hf in range(2):
                    need(pool, "buev", L, 8 * hf + 8)
                    need(pool, "tab", L, 2 * hf + 2)
                    if hf == 1:
                        need(pool, "s5y", L, 1)
                    E.settle()
                    E.did(tt(P4[:, :, tm], TS, BR[:, :, tm], ALU.mult))
                    E.did(tt(P3[:, :, tm], TC, BI[:, :, tm], ALU.mult), "poolpre")
                    need(pool, "scan", L, hf + 1)
                    E.settle()
                    E.did(tt(P4[:, :, tm], TS, BR[:, :, tm], ALU.mult))
                    E.did(tt(P3[:, :, tm], TC, BI[:, :, tm], ALU.mult), "poolpost")
                need(pool, "s5x", L, 2)
                pool.dma_start(O["s5"][L], s5o[:]).then_inc(S("st_s5"), 16)
                need(pool, "spre", L, 1)
                pool.dma_start(O["convprev"][L], prev[:, :, 1]).then_inc(S("st_prev"), 16)
                need(pool, "hff", L, FT)
                pool.dma_start(O["conv"][L], cout[:]).then_inc(S("st_conv"), 16)
            need(pool, "x", DEPTH - 1, 16)
            pool.dma_start(O["y"], x[:]).then_inc(S("st_y"), 16)
            pool.wait_ge(S("st_y"), 16)
            for name in ("st_s5", "st_prev", "st_conv"):
                pool.wait_ge(S(name), 16 * DEPTH)


def constants():
    f = np.float32
    eye = np.eye(P, dtype=f)
    k, q = np.arange(P)[:, None], np.arange(P)[None, :]
    perm = np.zeros((P, P), f)
    for m in range(P):
        perm[m + 32 if m % 64 < 32 else m - 32, m] = -1.0 if m % 64 < 32 else 1.0
    cst = np.stack([eye, (k >= q).astype(f), np.ones((P, P), f), (k < q).astype(f), perm,
                    np.full((P, P), 1 / D_MODEL, f), np.full((P, P), 1 / 256, f), np.full((P, P), 1 / P, f)], 1)
    pos = np.concatenate([np.arange(SEQ), np.full(NS, SEQ)]).astype(f)
    inv = (10000.0 ** (-np.arange(32, dtype=f) / 32)).astype(f)[np.arange(P) % 32]
    ang = (inv[:, None] * pos[None, :]).astype(f)
    rope = np.stack([np.cos(ang), np.sin(ang)], 1).astype(f)
    gap = np.arange(SEQ)[None, None, :] - np.arange(P)[:, None, None]
    dtab = np.where(gap >= 0, np.exp(LOG_GAMMA[None, :, None] * np.maximum(gap, 0)), 0.0) * DH ** -0.5
    left = SEQ - 1 - (np.arange(P)[:, None] + P * np.arange(2)[None, :])
    kdec = np.exp(LOG_GAMMA[None, None, :] * left[:, :, None])
    gam = np.exp(LOG_GAMMA)[2 * np.arange(2)[None, :] + (np.arange(P) // 64)[:, None]]
    steps = np.broadcast_to(np.arange(SEQ, dtype=f), (P, SEQ))
    return {"cst": cst, "rope": rope, "dtab": dtab.astype(f), "kdec": kdec.astype(f), "gam": gam.astype(f),
            "steps": steps}


def lay_out(i):
    f = np.float32
    D = DEPTH
    a = {}
    xt = np.concatenate([i["x_prompt"][0], i["x_sample"][:, 0]], 0)
    a["xT"] = xt.T.reshape(KT, P, T).transpose(1, 0, 2)
    w_in = i["w_in"].reshape(D, 8, P, N_IN, P).transpose(0, 3, 2, 1, 4)[:, IN_ORDER]
    w_out = i["w_out"].reshape(D, 8, P, KT, P).transpose(0, 3, 2, 1, 4)
    up_order = [m + FT * g for m in range(FT) for g in range(2)]
    w_up = i["ffn_w_up"].reshape(D, 8, P, N_UP, P).transpose(0, 3, 2, 1, 4)[:, up_order]
    w_dn = i["ffn_w_down"].reshape(D, FT, P, KT, P).transpose(0, 3, 1, 2, 4)
    w_dn = w_dn.reshape(D, N_DOWN, 8, P, P).transpose(0, 1, 3, 2, 4)
    a["units"] = np.concatenate([w_in, w_out, w_up, w_dn], 1).reshape(D * UNITS, P, 8, P)
    col = lambda v: v.reshape(-1, P).T
    upc = lambda v: col(v)[:, up_order]
    cols = [col(i["ln_in_g"]), col(i["ln_in_b"])]
    for l in range(D):
        cols += [col(i[n][l]) for n in ("norm_a_g", "norm_b_g", "ret_gn_g", "ret_gn_b", "ln1_g", "ln1_b",
                                        "ln2_g", "ln2_b", "s5_d")]
        cols += [upc(i["ffn_conv_w"][l, j]) for j in range(3)] + [upc(i["ffn_conv_b"][l])]
        cols += [np.broadcast_to(i["sb_logit_bias"][l], (P, HEADS))]
    a["vec"] = np.concatenate(cols, 1)
    j8 = lambda v: v.reshape(D, J, 2 * 64).transpose(0, 2, 1)
    def rows(v):
        v = v.reshape(D, 2, HJ, 1, 1, 2, 64)
        v = np.broadcast_to(v, (D, 2, HJ, 2, 16, 2, 64))
        return v.transpose(0, 2, 3, 4, 1, 5, 6).reshape(D, P, 256)
    ls = np.broadcast_to(i["s5_log_step"][:, :, None], i["s5_lambda_re"].shape)
    a["s5in"] = np.stack([np.concatenate([j8(v), rows(v)], 2)
                          for v in (i["s5_lambda_re"], i["s5_lambda_im"], ls)], 2)
    s5b = np.zeros((D, 2, HJ, 2, 16, 2, 2, 64), f)
    s5c = np.zeros((D, 2, J, 2, 64, 2, 16), f)
    for c, (nb, nc_) in enumerate((("s5_b_re", "s5_c_re"), ("s5_b_im", "s5_c_im"))):
        b = i[nb].reshape(D, 2, HJ, 2, 64, 16)
        cc = i[nc_].reshape(D, J, 2, 16, 64)
        for gl in range(2):
            s5b[:, c, :, gl, :, :, gl] = b[:, :, :, gl].transpose(0, 2, 4, 1, 3)
            s5c[:, c, :, gl, :, gl] = cc[:, :, gl].transpose(0, 1, 3, 2)
    a["s5b"] = s5b.reshape(D, 2, P, 256).transpose(0, 2, 1, 3)
    a["s5c"] = s5c.reshape(D, 2, J, P, 32).transpose(0, 3, 1, 2, 4)
    a["s5x0"] = np.stack([i[n].reshape(D, NS, J, P).transpose(0, 3, 2, 1)
                          for n in ("state_s5_re", "state_s5_im")], 2)
    a["wglu"] = i["s5_w_glu"].reshape(D, 2, P, 256).transpose(0, 2, 1, 3)
    a["kpool"] = i["cache_k"].reshape(D, POOL, PAGE, 2, P).transpose(0, 1, 4, 3, 2).reshape(D, POOL, P, 256)
    a["vpool"] = i["cache_v"].reshape(D, POOL, PAGE, 256)
    a["sret"] = i["state_ret"].reshape(D, NS, 2, P, DV).transpose(0, 3, 1, 2, 4)
    a["prev"] = i["state_conv"].reshape(D, NS, 2, N_UP, P).transpose(0, 4, 3, 2, 1)[:, :, up_order]
    a["pages"] = i["page_table"].reshape(1, -1)
    a.update(constants())
    return {k: np.ascontiguousarray(v) for k, v in a.items()}, up_order


_OUTS = {"y": (P, KT, T), "kv": (DEPTH, P, 4, T), "s5": (DEPTH, P, 2, J, NS + 1), "rprompt": (DEPTH, P, 2, DV),
         "rsample": (DEPTH, P, NS, 2, DV), "conv": (DEPTH, P, N_UP, 10), "convprev": (DEPTH, P, N_UP, NS)}


def kernel(**inputs):
    import concourse.bacc as _bacc
    from concourse.bass_utils import run_bass_kernel_spmd as _run

    arrays, up_order = lay_out({k: np.asarray(v) for k, v in inputs.items()})
    nc = _bacc.Bacc("TRN2", target_bir_lowering=False, num_devices=1)
    A = {k: nc.dram_tensor(f"in_{k}", v.shape, mybir.dt.from_np(v.dtype), kind="ExternalInput").ap()
         for k, v in arrays.items()}
    O = {k: nc.dram_tensor(f"out_{k}", s, F32, kind="ExternalOutput").ap() for k, s in _OUTS.items()}
    hybrid_step(nc, A, O)
    res = _run(nc, [{f"in_{k}": v for k, v in arrays.items()}], core_ids=[0]).results[0]
    r = {k: np.asarray(res[f"out_{k}"]) for k in _OUTS}
    D = DEPTH
    y = r["y"].transpose(2, 1, 0).reshape(T, D_MODEL)
    kv = r["kv"].transpose(0, 3, 2, 1).reshape(D, T, 2, HEADS, DH)
    s5 = r["s5"].transpose(0, 2, 4, 3, 1).reshape(D, 2, NS + 1, 16, 64)
    rp = r["rprompt"].transpose(0, 2, 1, 3).reshape(D, 1, HEADS, DH, DV)
    rs = r["rsample"].transpose(0, 2, 3, 1, 4).reshape(D, NS, HEADS, DH, DV)
    back = np.argsort(up_order)
    cv = r["conv"][:, :, back].transpose(0, 3, 2, 1).reshape(D, 10, 2 * D_FF)
    cp = r["convprev"][:, :, back].transpose(0, 3, 2, 1).reshape(D, NS, 2 * D_FF)
    return (y[None, :SEQ], y[SEQ:, None],
            kv[:, None, :SEQ, 0], kv[:, None, :SEQ, 1], kv[:, SEQ:, None, 0], kv[:, SEQ:, None, 1],
            s5[:, 0, :1], s5[:, 1, :1], s5[:, 0, 1:], s5[:, 1, 1:], rp, rs,
            cv[:, None, :2], np.stack([cp, cv[:, 2:]], 2))
```

```python
import math
from contextlib import ExitStack

import numpy as np

import concourse.bass as bass
from concourse import mybir

F32 = mybir.dt.float32
F32R = mybir.dt.float32r
ALU = mybir.AluOpType
ACT = mybir.ActivationFunctionType

P = 128
SEQ, NS = 256, 8
T = SEQ + NS
DEPTH, D_MODEL, D_FF = 2, 1024, 2816
KT = D_MODEL // P
FT = D_FF // P
HEADS, DH, DV = 4, 64, 128
PAGES, PAGE, POOL = 2, 128, 20
ALPHA = (2.0 * DEPTH) ** 0.25
LN_EPS, RMS_EPS = 1e-5, 1e-6
J = 8
HJ = J // 2
DEC = 384

U, QB_, KB, VB_, QC, KC, VC, GC = 0, 2, 4, 6, 8, 10, 12, 16
N_IN, N_OUT, N_UP = 20, KT, 2 * FT
N_DOWN = KT * FT // 8
UNITS = N_IN + N_OUT + N_UP + N_DOWN
RING = 5
SPLIT_FROM = N_IN + N_OUT + 1
SPLITS = UNITS - SPLIT_FROM
SRING = 4
CSLOTS = 8
TILES = N_IN + N_OUT + N_UP + KT
S5_ACT = [5, 6, 8]
B0_AT = [3, 2]

PER = {"norm_a_g": 2, "norm_b_g": 2, "gn_g": 4, "gn_b": 4, "ln1_g": 8, "ln1_b": 8, "ln2_g": 8,
       "ln2_b": 8, "s5_d": 2, "cw0": N_UP, "cw1": N_UP, "cw2": N_UP, "cb": N_UP, "bias": HEADS}
COL, _at = {}, 2 * KT
for _n, _w in PER.items():
    COL[_n] = _at
    _at += _w
PER_LAYER = _at - 2 * KT
N_VEC = 2 * KT + DEPTH * PER_LAYER

CONSTS = ["ident", "tri", "ones", "mask", "perm", "mean_d", "mean_w", "mean_v"]
LOG_GAMMA = np.log1p(-np.exp2(-5.0 - np.arange(HEADS)))
TWO_PI = 2.0 * math.pi
TWO_PI_HI = float(np.float32(6.28125))
TWO_PI_LO = TWO_PI - TWO_PI_HI
PI_SAFE = 3.1415925
TWO_PI_IN = 6.283185
ROUND = 1.5 * 2.0**23
ROUND_15 = 1.5 * 2.0**8


def hybrid_step(nc, A, O):
    with ExitStack() as ctx:
        sems = {}

        def S(name):
            if name not in sems:
                sems[name] = ctx.enter_context(nc.semaphore(name))
            return sems[name]

        place = {}
        here = [-(-nc.sbuf_base // 64) * 64]

        def at(name, shape, over=None, dt=F32):
            size = int(np.prod(shape[1:])) * 4
            if over is None:
                place[name] = here[0]
                here[0] += -(-size // 32) * 32
            else:
                place[name] = place[over[0]] + 4 * over[1]
            return nc.alloc_sbuf_tensor_at(name, shape, dt, offset=place[name])

        hb = at("hb", [P, N_IN, T])
        work = at("work", [P, 6, HJ, T])
        hff_hi = at("hff_hi", [P, FT, T], over=("hb", 0), dt=F32R)
        hff_lo = at("hff_lo", [P, FT, T], over=("hb", FT * T), dt=F32R)
        kv = at("kv", [P, NS, PAGES, 256])
        ZT = at("ZT", [P, 2, 1600])
        Z, SPL = ZT[:, 0], ZT[:, 1]
        here[0] += 4 * (4096 - 3200)
        SR = at("SR", [P, NS, 2, DV])
        VBC = at("VBC", [P, NS, 2, DV])
        here[0] += 512
        w_hi = at("w_hi", [P, SRING, 8, P], over=("kv", 0), dt=F32R)
        w_lo = at("w_lo", [P, SRING, 8, P], over=("ZT", 0), dt=F32R)
        x_hi = at("x_hi", [P, KT, T], over=("SR", 0), dt=F32R)
        x_lo = at("x_lo", [P, KT, T], over=("SR", KT * T), dt=F32R)
        BR, BI, P1, P2, P3, P4 = (work[:, i] for i in range(6))
        ring = at("ring", [P, RING, 8, P])
        x = at("x", [P, KT, T])
        z = at("z", [P, KT, T])
        turn = at("turn", [P, 2, HJ, T])
        rg = turn[:, 0]
        tabs = [(turn[:, 0, :, 0:SEQ], turn[:, 1, :, 0:SEQ]), (z[:, 0:HJ, 0:SEQ], z[:, HJ:J, 0:SEQ])]
        RI = at("RI", [P, HEADS, DEC])
        KD = at("KD", [P, 2, 256])
        VT = at("VT", [P, 2, HEADS * DV])
        VBt = at("VBt", [P, 2, 256])
        tmp = at("tmp", [P, 12, 264], over=("RI", 0))
        sqo = RI[:].rearrange("p a b -> p (a b)")[:, 0:HEADS * T].rearrange("p (a b) -> p a b", b=T)
        s5in = at("s5in", [P, 3, 264])
        s5b = at("s5b", [P, 2, 256])
        bb = at("bb", [P, 2, 256])
        s5c = at("s5c", [P, 2, J, 32])
        s5x0 = at("s5x0", [P, 2, J, NS])
        are, aim, mag, fhi, flo = (at(n, [P, J]) for n in ("are", "aim", "mag", "fhi", "flo"))
        stmp = at("stmp", [P, 4, HJ, NS])
        s5o = at("s5o", [P, 2, J, NS + 1])
        wglu = at("wglu", [P, 2, 256])
        yd = at("yd", [P, 2, T])
        yg = at("yg", [P, 2, T])
        yb = at("yb", [P, 2, T])
        sg = yb
        sq2 = at("sq2", [P, 2, T])
        rs2 = at("rs2", [P, T])
        lnr = at("lnr", [P, T])
        sqt = at("sqt", [P, 3, T])
        acc = at("acc", [P, 2, T])
        qbd = at("qbd", [P, 2, NS, 2])
        eps_all, halfpi = at("eps_all", [P, 2]), at("halfpi", [P, 1])
        eps_t = {LN_EPS: eps_all[:, 0:1], RMS_EPS: eps_all[:, 1:2]}
        VS = at("VS", [NS, HEADS * DV])
        conv = at("conv", [P, CSLOTS, T], over=("yd", 0))
        Oh = at("Oh", [P, HEADS, T])
        RSO = at("RSO", [P, 2, DV])
        qs = at("qs", [P, 2, NS])
        prev = at("prev", [P, N_UP, 2, NS])
        spre = at("spre", [P, N_UP, NS])
        cout = at("cout", [P, N_UP, 10])
        vec = at("vec", [P, N_VEC])
        cst = at("cst", [P, len(CONSTS), P])
        dtab = at("dtab", [P, HEADS, SEQ])
        rope = at("rope", [P, 2, T])
        steps = at("steps", [P, SEQ])
        kdec = at("kdec", [P, 2, HEADS])
        gam = at("gam", [P, 2])
        pidx = at("pidx", [1, NS * PAGES], dt=mybir.dt.int32)
        assert here[0] <= nc.sbuf_usable_end, (here[0], nc.sbuf_usable_end)
        C = {n: cst[:, i] for i, n in enumerate(CONSTS)}
        ps = ctx.enter_context(nc.psum_tensor("ps", [P, 8, 512], F32))
        vs_dram = [nc.dram_tensor(f"vs_scratch{l}", [NS, HEADS * DV], F32, kind="Internal").ap()
                   for l in range(DEPTH)]

        def pv(L, name, i=0, n=1):
            c = L * PER_LAYER + COL[name] + i
            return vec[:, c:c + n]

        PER_LN = {"lnc": 1, "lnd": KT, "lnsq": KT, "lnacc1": 1, "lnacc2": 1,  "lnmean": 1, "lnvar": 1, "lnmu2": 1,
                  "lnv": 1, "lnln": 1, "lnr": 1, "xn": KT, "x": KT}

        def needq(eng, name, q, k):
            eng.wait_ge(S(name), q * PER_LN[name] + k)

        class Engine:

            def __init__(self, eng, own):
                self.eng, self.own, self.n, self.last = eng, own, {}, None

            def did(self, ins, name=None):
                name = name or self.own
                ins.then_inc(S(name), 1)
                self.n[name] = self.n.get(name, 0) + 1
                self.last = (name, self.n[name])

            def settle(self):
                if self.last:
                    self.eng.wait_ge(S(self.last[0]), self.last[1])

        def need(eng, name, L, k):
            eng.wait_ge(S(name), L * PERL.get(name, 0) + k)

        PERL = {"tile": TILES, "in_evac": N_IN, "z": 16, "bb": 1, "tph": 2, "tab": 4, "cneg": 1, "bu": 16, "buev": 16,
                "pre": 2, "poolpre": 2, "scan": 2, "poolpost": 2, "s5x": 2, "s5y": 2, "yd": 2, "gelu": 2,
                "glu": 2, "sig": 2, "ya": 1, "sqa": 1, "rmsa": 1, "rmsar": 1, "cata": 2,
                "rot": 4, "rotrd": 4, "qk": 1, "trk": 1, "kd": 1, "trv": 2, "vt": 2, "trvb": 1, "vbt": 1,
                "trvs": 1, "vs": 1, "rin": 4, "ri": 4, "rstate": 1, "rso": 1, "srg": 2, "sr": 1, "qs": 1,
                "ro": 4, "oev": 4, "gmean": 4, "gd": 4, "gsq": 4, "gvar": 4, "gv1": 4, "gr": 4, "sgc": 1,
                "catc": 4, "qb": 2, "sbz": 4, "zev": 4, "sbzs": 1, "zs": 1, "absz": 1, "spe": 1, "spl": 1,
                "sbs": 4, "zsub": 4, "sbss": 1, "zsubs": 1, "zmin": 1, "wexp": 1, "w": 1, "sby": 2, "ybev": 2,
                "sbys": 1, "ybs": 1, "sqb": 1, "rmsb": 1, "rmsbr": 1, "catb": 2,
                "up_free": N_UP, "fc": N_UP, "fs": FT, "prod": FT, "hff_hi": FT, "hff_lo": FT, "spre": 1,
                "x_hi": KT, "x_lo_dve": KT // 2, "x_lo_pool": KT // 2, "w_hi": SPLITS, "used": UNITS}

        def by_pool(i):
            return i >= N_IN + N_OUT + N_UP and i % 2 == 0

        def wait_low(eng, L, i):
            mine = [u for u in range(SPLIT_FROM, UNITS) if by_pool(u) == by_pool(i)]
            eng.wait_ge(S("w_lo_pool" if by_pool(i) else "w_lo_dve"), L * len(mine) + mine.index(i) + 1)

        def split_slot(i):
            return (i - SPLIT_FROM) % SRING

        def ring_slot(n):
            return n % RING

        block = ctx.enter_context(nc.Block())

        @block.sync
        def _(sp):
            sp.dma_start(s5in[:], A["s5in"][0]).then_inc(S("ld_s5in"), 16)
            sp.dma_start(s5b[:], A["s5b"][0]).then_inc(S("ld_s5b"), 16)
            sp.dma_start(z[:], A["xT"]).then_inc(S("ld_x"), 16)
            sp.dma_start(cst[:], A["cst"]).then_inc(S("ld_cst"), 16)
            sp.dma_start(vec[:], A["vec"]).then_inc(S("ld_vec"), 16)
            sp.dma_start(steps[:], A["steps"]).then_inc(S("ld_steps"), 16)
            sp.dma_start(pidx[:], A["pages"]).then_inc(S("ld_pages"), 16)

            def layer_params(L):
                if L > 0:
                    need(sp, "s5y", L - 1, 2)
                    need(sp, "bb", L - 1, 1)
                    need(sp, "glu", L - 1, 2)
                    need(sp, "bu", L - 1, 16)
                    sp.wait_ge(S("dve_x0"), L * 2)
                    sp.dma_start(s5in[:], A["s5in"][L]).then_inc(S("ld_s5in"), 16)
                    sp.dma_start(s5b[:], A["s5b"][L]).then_inc(S("ld_s5b"), 16)
                sp.dma_start(s5c[:], A["s5c"][L]).then_inc(S("ld_s5c"), 16)
                sp.dma_start(s5x0[:], A["s5x0"][L]).then_inc(S("ld_x0"), 16)
                sp.dma_start(wglu[:], A["wglu"][L]).then_inc(S("ld_wglu"), 16)

            def unit(L, i):
                n = L * UNITS + i
                if n >= RING:
                    former = n - RING
                    if former % UNITS >= SPLIT_FROM:
                        wait_low(sp, former // UNITS, former % UNITS)
                    else:
                        sp.wait_ge(S("used"), former + 1)
                sp.dma_start(ring[:, ring_slot(n)], A["units"][n]).then_inc(S(f"ld_w{ring_slot(n)}"), 16)

            def pages(L, what, part=0, parts=1):
                n = NS * PAGES // parts
                for s in range(part * n, (part + 1) * n):
                    idx = sp.value_load(pidx[0:1, s:s + 1], min_val=0, max_val=POOL - 1)
                    src = A[what][L][bass.ds(idx, 1)].rearrange("a p c -> p (a c)")
                    sp.dma_start(kv[:, s // PAGES, s % PAGES], src).then_inc(S("ld_kv"), 16)

            layer_params(0)
            for L in range(DEPTH):
                for i in range(4):
                    unit(L, i)
                if L == 0:
                    sp.dma_start(rope[:], A["rope"]).then_inc(S("ld_rope"), 16)
                    sp.dma_start(dtab[:], A["dtab"]).then_inc(S("ld_dtab"), 16)
                    sp.dma_start(kdec[:], A["kdec"]).then_inc(S("ld_kdec"), 16)
                    sp.dma_start(gam[:], A["gam"]).then_inc(S("ld_gam"), 16)
                    sp.wait_ge(S("ld_pages"), 16)
                else:
                    sp.wait_ge(S("used"), UNITS * L)
                    need(sp, "spre", L - 1, 1)
                    sp.wait_ge(S("st_prev"), 16 * L)
                for i in range(4, 13):
                    unit(L, i)
                    if i < 8:
                        pages(L, "kpool", i - 4, 4)
                    if i == 8:
                        sp.dma_start(SR[:], A["sret"][L]).then_inc(S("ld_sr"), 16)
                sp.dma_start(prev[:], A["prev"][L]).then_inc(S("ld_prev"), 16)
                need(sp, "sbzs", L, 1)
                pages(L, "vpool")
                for i in range(13, UNITS):
                    unit(L, i)
                    if i == N_IN + N_OUT + N_UP // 2 and L + 1 < DEPTH:
                        layer_params(L + 1)

        @block.tensor
        def _(pe):
            E = Engine(pe, "pe_step")
            mm = nc.tensor.matmul
            holder = {}
            freed = []

            def claim(bank, reader, L, k):
                if bank in holder:
                    h = holder[bank]
                    (needq if h[0] in PER_LN else need)(pe, *h)
                holder[bank] = (reader, L, k)
                return ps[:, bank]

            def main_bank(reader, L, k):
                n = len(freed)
                if n >= 4:
                    need(pe, *freed[n - 4])
                freed.append((reader, L, k))
                return ps[:, n % 4, 0:T]

            def unit_ready(n):
                pe.wait_ge(S(f"ld_w{ring_slot(n)}"), 16 * (n // RING + 1))

            def tile8(L, i, out, rhs, ready=None):
                n = L * UNITS + i
                unit_ready(n)
                for k in range(8):
                    if ready:
                        ready(k)
                    ins = mm(out, ring[:, ring_slot(n), k], rhs(k), start=(k == 0), stop=(k == 7))
                    if k == 7:
                        E.did(ins, "used")

            def split_product(out, i, b, hi, lo, start, stop):
                wh, wl = w_hi[:, split_slot(i), b], w_lo[:, split_slot(i), b]
                mm(out, wh, hi, start=start, stop=False)
                mm(out, wh, lo, start=False, stop=False)
                return mm(out, wl, hi, start=False, stop=stop)

            def ln_shift(q):
                bank = claim(4, "lnd", q, KT)
                E.did(mm(bank[:, 0:T], C["mean_v"], z[:, 0], start=True, stop=True), "lnc")

            def ln_sums(q):
                b1, b2 = claim(5, "xn", q, KT), claim(6, "lnv", q, 1)
                needq(pe, "lnacc1", q, 1)
                mm(b1[:, 0:T], C["mean_d"], acc[:, 0], start=True, stop=False)
                needq(pe, "lnacc2", q, 1)
                mm(b2[:, 0:T], C["mean_d"], acc[:, 1], start=True, stop=False)
                needq(pe, "lnd", q, KT)
                E.did(mm(b1[:, 0:T], C["mean_d"], z[:, KT - 1], start=False, stop=True), "lnmean")
                needq(pe, "lnsq", q, KT)
                E.did(mm(b2[:, 0:T], C["mean_d"], sqt[:, (KT - 1) % 3], start=False, stop=True), "lnvar")

            def s5_b(L, hf):
                if hf == 0:
                    need(pe, "bb", L, 1)
                for jj in range(HJ):
                    for c in range(2):
                        k = 8 * hf + 2 * jj + c + 1
                        bank = claim(4 + 2 * (jj % 2) + c, "buev", L, k)
                        E.did(mm(bank[:, 0:T], bb[32 * jj:32 * jj + 32, c, hf * P:(hf + 1) * P],
                                 hb[32 * jj:32 * jj + 32, U + hf], start=True, stop=True), "bu")

            def s5_c(L, hf):
                need(pe, "s5x", L, hf + 1)
                if hf == 0:
                    need(pe, "cneg", L, 1)
                bank = claim(4, "yd", L, hf + 1)
                for jj in range(HJ):
                    o = bank[32 * jj:32 * jj + 32, 0:T]
                    j = hf * HJ + jj
                    mm(o, s5c[:, 0, j], P1[:, jj], start=True, stop=False, tile_position=(0, 32 * jj))
                    ins = mm(o, s5c[:, 1, j], P3[:, jj], start=False, stop=True, tile_position=(0, 32 * jj))
                E.did(ins, "s5y")

            def s5_glu(L):
                need(pe, "gelu", L, 2)
                pe.wait_ge(S("ld_wglu"), 16 * (L + 1))
                for m in range(2):
                    bank = claim(6 + m, "sig", L, m + 1)
                    for k in range(2):
                        ins = mm(bank[:, 0:T], wglu[:, k, m * P:(m + 1) * P], yg[:, k],
                                 start=(k == 0), stop=(k == 1))
                    E.did(ins, "glu")

            def rms(L, sq, wait, reader, name, b):
                need(pe, wait, L, 1)
                bank = claim(b, reader, L, 1)
                for k in range(2):
                    ins = mm(bank[:, 0:T], C["mean_w"], sq[:, k], start=(k == 0), stop=(k == 1))
                E.did(ins, name)

            def rotate(L):
                for i in range(4):
                    need(pe, "in_evac", L, QC + i + 1)
                    bank = claim(4 + i, "rotrd", L, i + 1)
                    E.did(mm(bank[:, 0:T], C["perm"], hb[:, QC + i], start=True, stop=True), "rot")

            def transposes(L):
                need(pe, "in_evac", L, VC + 4)
                for tt in range(2):
                    bank = claim(4 + tt, "vt", L, tt + 1)
                    for h in range(HEADS):
                        ins = nc.tensor.transpose(bank[:, h * P:(h + 1) * P],
                                                  hb[:, VC + h, tt * P:(tt + 1) * P], C["ident"])
                    E.did(ins, "trv")
                bank = claim(6, "vs", L, 1)
                for h in range(HEADS):
                    ins = nc.tensor.transpose(bank[0:NS, h * P:(h + 1) * P], hb[:, VC + h, SEQ:T], C["ident"])
                E.did(ins, "trvs")

            def k_transposes(L):
                need(pe, "qk", L, 1)
                bank = claim(7, "kd", L, 1)
                for tt in range(2):
                    for ht in range(2):
                        ins = nc.tensor.transpose(bank[:, tt * 256 + ht * P:tt * 256 + (ht + 1) * P],
                                                  hb[:, KC + ht, tt * P:(tt + 1) * P], C["ident"])
                E.did(ins, "trk")

            def causal(bank, kt, qt, h, k0, q0):
                r = slice(64 * (h % 2), 64 * (h % 2) + 64)
                kk, qq = hb[r, k0 + h // 2], hb[r, q0 + h // 2]
                mm(bank[:, 0:SEQ], kk[:, 0:P], qq[:, 0:SEQ], start=True, stop=True)
                return mm(bank[:, SEQ:DEC], kk[:, P:SEQ], qq[:, P:SEQ], start=True, stop=True)

            def ret_inner(L):
                for h in range(HEADS):
                    bank = claim(4 + h, "ri", L, h + 1)
                    E.did(causal(bank, None, None, h, KC, QC), "rin")

            def ret_state(L):
                need(pe, "kd", L, 1)
                need(pe, "vt", L, 2)
                bank = claim(4, "rso", L, 1)
                for h in range(HEADS):
                    o = bank[64 * (h % 2):64 * (h % 2) + 64, (h // 2) * DV:(h // 2 + 1) * DV]
                    for tt in range(2):
                        ins = mm(o, KD[:, tt, 64 * h:64 * h + 64], VT[:, tt, h * DV:(h + 1) * DV],
                                 start=(tt == 0), stop=(tt == 1))
                E.did(ins, "rstate")

            def ret_out(L):
                need(pe, "sr", L, 1)
                need(pe, "qs", L, 1)
                need(pe, "vt", L, 2)
                for h in range(HEADS):
                    need(pe, "ri", L, h + 1)
                    bank = claim(4 + h, "oev", L, h + 1)
                    mm(bank[:, 0:SEQ], VT[:, 0, h * DV:(h + 1) * DV], RI[:, h, 0:SEQ], start=True, stop=False)
                    mm(bank[:, P:SEQ], VT[:, 1, h * DV:(h + 1) * DV], RI[:, h, SEQ:DEC], start=False, stop=True)
                    r = slice(64 * (h % 2), 64 * (h % 2) + 64)
                    for b in range(NS):
                        ins = mm(bank[:, SEQ + b:SEQ + b + 1], SR[r, b, h // 2], qs[r, h // 2, b:b + 1],
                                 start=True, stop=True)
                    E.did(ins, "ro")

            def group_norm(L):
                for h in range(HEADS):
                    need(pe, "oev", L, h + 1)
                    bank = claim(4 + h, "gd", L, h + 1)
                    E.did(mm(bank[:, 0:T], C["mean_v"], Oh[:, h], start=True, stop=True), "gmean")
                for h in range(HEADS):
                    need(pe, "gsq", L, h + 1)
                    bank = claim(4 + h, "gv1", L, h + 1)
                    E.did(mm(bank[:, 0:T], C["mean_v"], sqo[:, h], start=True, stop=True), "gvar")

            def vb_transposes(L):
                need(pe, "in_evac", L, VB_ + 2)
                bank = claim(4, "vbt", L, 1)
                for tt in range(2):
                    for ht in range(2):
                        ins = nc.tensor.transpose(bank[:, tt * 256 + ht * P:tt * 256 + (ht + 1) * P],
                                                  hb[:, VB_ + ht, tt * P:(tt + 1) * P], C["ident"])
                E.did(ins, "trvb")

            def sb_scores(L):
                need(pe, "in_evac", L, KB + 2)
                for h in range(HEADS):
                    bank = claim(4 + h, "zev", L, h + 1)
                    E.did(causal(bank, None, None, h, KB, QB_), "sbz")

            def sb_sample_scores(L):
                need(pe, "qb", L, 2)
                pe.wait_ge(S("ld_kv"), 16 * NS * PAGES * (2 * L + 1))
                bank = claim(4, "zs", L, 1)
                for pg in range(PAGES):
                    for b in range(NS):
                        for ht in range(2):
                            c = 32 * pg + 4 * b + 2 * ht
                            ins = mm(bank[:, c:c + 2], kv[:, b, pg, ht * P:(ht + 1) * P], qbd[:, ht, b],
                                     start=True, stop=True)
                E.did(ins, "sbzs")

            def sb_tails(L):
                need(pe, "spl", L, 1)
                for h in range(HEADS):
                    bank = claim(4 + h, "zsub", L, h + 1)
                    s0, s1 = SPL[:, h * DEC:h * DEC + SEQ], SPL[:, h * DEC + SEQ:(h + 1) * DEC]
                    mm(bank[:, 0:SEQ], C["tri"], s0, start=True, stop=False)
                    mm(bank[:, P:SEQ], C["ones"], s1, start=False, stop=True)
                    E.did(mm(bank[:, SEQ:DEC], C["tri"], s1, start=True, stop=True), "sbs")
                bank = claim(4, "zsubs", L, 1)
                s0, s1 = SPL[:, 4 * DEC:4 * DEC + 32], SPL[:, 4 * DEC + 32:4 * DEC + 64]
                mm(bank[:, 0:32], C["tri"], s0, start=True, stop=False)
                mm(bank[:, 0:32], C["ones"], s1, start=False, stop=True)
                E.did(mm(bank[:, 32:64], C["tri"], s1, start=True, stop=True), "sbss")

            def sb_values(L):
                need(pe, "w", L, 1)
                need(pe, "vbt", L, 1)
                for ht in range(2):
                    bank = claim(4 + ht, "ybev", L, ht + 1)
                    for h in (2 * ht, 2 * ht + 1):
                        r = 64 * (h % 2)
                        o = bank[r:r + 64]
                        w0, w1 = Z[:, h * DEC:h * DEC + SEQ], Z[:, h * DEC + SEQ:(h + 1) * DEC]
                        mm(o[:, 0:SEQ], VBt[:, 0, 64 * h:64 * h + 64], w0, start=True, stop=False,
                           tile_position=(0, r))
                        ins = mm(o[:, P:SEQ], VBt[:, 1, 64 * h:64 * h + 64], w1, start=False, stop=True,
                                 tile_position=(0, r))
                    E.did(ins, "sby")
                pe.wait_ge(S("ld_kv"), 16 * NS * PAGES * (2 * L + 2))
                bank = claim(6, "ybs", L, 1)
                for ht in range(2):
                    for b in range(NS):
                        for pg in range(PAGES):
                            wc = 4 * DEC + 32 * pg + 4 * b + 2 * ht
                            oc = 16 * ht + 2 * b
                            ins = mm(bank[:, oc:oc + 2], kv[:, b, pg, ht * P:(ht + 1) * P], Z[:, wc:wc + 2],
                                     start=(pg == 0), stop=(pg == 1))
                E.did(ins, "sbys")

            pe.wait_ge(S("ld_x"), 16)
            pe.wait_ge(S("ld_cst"), 16)
            ln_shift(0)
            ln_sums(0)
            for L in range(DEPTH):
                for i in range(N_IN):
                    out = main_bank("in_evac", L, i + 1)
                    tile8(L, i, out, lambda k: x[:, k], (lambda k: needq(pe, "x", 2 * L, k + 1)) if i == 0 else None)
                    if i == B0_AT[L]:
                        need(pe, "in_evac", L, 2)
                        s5_b(L, 0)
                    if i == 6:
                        sb_scores(L)
                    if i == 8:
                        sb_sample_scores(L)
                        vb_transposes(L)
                    if i == 9:
                        s5_c(L, 0)
                        s5_b(L, 1)
                    if i == 13:
                        s5_c(L, 1)
                        rotate(L)
                    if i == 14:
                        sb_tails(L)
                    if i == 15:
                        s5_glu(L)
                    if i == 16:
                        transposes(L)
                        k_transposes(L)
                    if i == 17:
                        ret_inner(L)
                        sb_values(L)
                    if i == 18:
                        ret_state(L)
                        rms(L, sq2, "sqa", "rmsar", "rmsa", 5)
                rms(L, sq2, "sqb", "rmsbr", "rmsb", 6)
                ret_out(L)
                group_norm(L)
                cat = [hb[:, U], hb[:, U + 1], hb[:, QB_], hb[:, QB_ + 1]] + [hb[:, GC + h] for h in range(4)]

                def cat_ready(k):
                    need(pe, *[("cata", L, k + 1), ("catb", L, k - 1), ("catc", L, k - 3)][min(k // 2, 2)])

                for i in range(N_OUT):
                    out = main_bank("z", L, i + 1)
                    tile8(L, N_IN + i, out, lambda k: cat[k], cat_ready if i == 0 else None)
                    if i == 2:
                        need(pe, "z", L, 1)
                        ln_shift(2 * L + 1)
                ln_sums(2 * L + 1)
                for i in range(N_UP):
                    out, u = main_bank("up_free", L, i + 1), N_IN + N_OUT + i
                    if u < SPLIT_FROM:
                        tile8(L, u, out, lambda k: x[:, k], lambda k: needq(pe, "x", 2 * L + 1, k + 1))
                        continue
                    wait_low(pe, L, u)
                    for k in range(KT):
                        if u == SPLIT_FROM:
                            need(pe, "x_lo_dve" if k % 2 else "x_lo_pool", L, k // 2 + 1)
                        ins = split_product(out, u, k, x_hi[:, k], x_lo[:, k], k == 0, k == KT - 1)
                    E.did(ins, "used")
                for m in range(KT):
                    out = main_bank("z", L, 8 + m + 1)
                    for k in range(FT):
                        blk = m * FT + k
                        u = N_IN + N_OUT + N_UP + blk // 8
                        if blk % 8 == 0:
                            wait_low(pe, L, u)
                        if m == 0:
                            need(pe, "hff_lo", L, k + 1)
                        ins = split_product(out, u, blk % 8, hff_hi[:, k], hff_lo[:, k], k == 0, k == FT - 1)
                        if blk % 8 == 7:
                            E.did(ins, "used")
                        elif k == FT - 1:
                            E.did(ins, "down")
                    if m == 4:
                        need(pe, "z", L, 9)
                        ln_shift(2 * L + 2)
                ln_sums(2 * L + 2)

        def tile_done(eng, L, i):
            eng.wait_ge(S("used"), L * UNITS + i + 1)

        def down_done(eng, L, m):
            last = (m + 1) * FT - 1
            if last % 8 == 7:
                eng.wait_ge(S("used"), L * UNITS + N_IN + N_OUT + N_UP + last // 8 + 1)
            else:
                ends = [q for q in range(KT) if ((q + 1) * FT) % 8 != 0]
                eng.wait_ge(S("down"), L * len(ends) + ends.index(m) + 1)

        def bcast(ap, shape, axis):
            return ap.unsqueeze(axis).to_broadcast(shape)

        @block.scalar
        def _(act):
            E = Engine(act, "act_step")
            f = nc.scalar.activation

            def inv_sqrt(dst, src, eps, first, last, settle_first=True):
                E.did(f(dst, src, ACT.Ln, bias=eps_t[eps]), first)
                E.settle()
                E.did(f(dst, dst, ACT.Exp, scale=-0.5), last)

            def split_hi(L, i):
                n = L * UNITS + i
                act.wait_ge(S(f"ld_w{ring_slot(n)}"), 16 * (n // RING + 1))
                if i < SPLIT_FROM + SRING:
                    need(act, "sbys", L, 1)
                else:
                    act.wait_ge(S("used"), n - SRING + 1)
                E.did(nc.scalar.copy(w_hi[:, split_slot(i)], ring[:, ring_slot(n)]), "w_hi")

            def ln(q):
                if q > 0:
                    needq(act, "xn", q - 1, KT)
                for t in range(KT):
                    if q % 2 == 1 and t >= 6:
                        split_hi((q - 1) // 2, SPLIT_FROM + t - 6)
                    needq(act, "lnd", q, t + 1)
                    if t >= 3:
                        act.wait_ge(S("pool_ln"), q * (KT - 3) + max(t - 3, 1))
                    E.did(f(sqt[:, t % 3], z[:, t], ACT.Square), "lnsq")
                needq(act, "lnmean", q, 1)
                E.did(f(rs2[:], ps[:, 5, 0:T], ACT.Square), "lnmu2")
                needq(act, "lnv", q, 1)
                E.did(f(lnr[:], lnr[:], ACT.Ln, bias=eps_t[LN_EPS]))
                E.settle()
                E.did(f(lnr[:], lnr[:], ACT.Exp, scale=-0.5), "lnr")
                if q == 0:
                    act.wait_ge(S("ld_vec"), 16)
                    g, b = vec[:, 0:8], vec[:, 8:16]
                else:
                    L, k = (q - 1) // 2, (q - 1) % 2 + 1
                    g, b = pv(L, f"ln{k}_g", 0, 8), pv(L, f"ln{k}_b", 0, 8)
                for t in range(KT):
                    needq(act, "xn", q, t + 1)
                    E.did(f(x[:, t], z[:, t], ACT.Identity, scale=g[:, t:t + 1], bias=b[:, t:t + 1]), "x")
                if q % 2 == 1:
                    act.wait_ge(S("st_sr"), 16 * (L + 1))
                    for t in range(KT):
                        E.did(f(x_hi[:, t], z[:, t], ACT.Identity, scale=g[:, t:t + 1], bias=b[:, t:t + 1]), "x_hi")

            def s5_params(L, part=None):
                act.wait_ge(S("ld_s5in"), 16 * (L + 1))
                if part == 0:
                    act.wait_ge(S("v_s5clear"), L + 1)
                    E.did(f(tmp[:, 0], s5in[:, 2], ACT.Exp), "a_dt")
                if part == 1:
                    act.wait_ge(S("v_ldt"), L + 1)
                    E.did(f(tmp[:, 2], tmp[:, 1], ACT.Exp), "a_mag")
                if part == 2:
                    act.wait_ge(S("v_red"), L + 1)
                    f(tmp[:, 5], tmp[:, 4], ACT.Sin)
                    E.did(f(tmp[:, 6], tmp[:, 7], ACT.Sin, bias=halfpi[:], scale=-1.0), "a_sc")

            def s5_tables(L, hf):
                need(act, "tph", L, hf + 1)
                TC, TS = tabs[hf]
                E.did(f(TS, TS, ACT.Sin, scale=TWO_PI_IN), "tab")
                E.did(f(TC, TC, ACT.Sin, bias=halfpi[:], scale=-TWO_PI_IN), "tab")

            def neg_c(L):
                act.wait_ge(S("ld_s5c"), 16 * (L + 1))
                E.did(nc.scalar.mul(s5c[:, 1], s5c[:, 1], -1.0), "cneg")

            act.wait_ge(S("eps_set"), 3)
            def s5_evac(L, hf):
                for k in range(8):
                    need(act, "bu", L, 8 * hf + k + 1)
                    if k == 0 and hf == 1:
                        need(act, "s5x", L, 1)
                    E.did(nc.scalar.copy((BR, BI)[k % 2][:, k // 2], ps[:, 4 + k % 4, 0:T]), "buev")

            def v_tokens(L):
                for tt in range(2):
                    need(act, "trv", L, tt + 1)
                    E.did(nc.scalar.copy(VT[:, tt], ps[:, 4 + tt]), "vt")
                need(act, "trvs", L, 1)
                E.did(nc.scalar.copy(VS[:], ps[0:NS, 6]), "vs")
                E.settle()
                act.dma_start(vs_dram[L], VS[:]).then_inc(S("st_vs"), 16)

            def v_spread(L):
                act.wait_ge(S("st_vs"), 16 * (L + 1))
                v5 = vs_dram[L].rearrange("b (a c e) -> c b a e", a=2, c=2)
                for c in range(2):
                    act.dma_start(VBC[64 * c:64 * c + 64], v5[c:c + 1].to_broadcast([64, NS, 2, DV])
                                  ).then_inc(S("ld_vbc"), 16)

            def rms_root(L, name, bank, signal):
                need(act, name, L, 1)
                E.did(f(rs2[:], ps[:, bank, 0:T], ACT.Ln, bias=eps_t[RMS_EPS]))
                E.settle()
                E.did(f(rs2[:], rs2[:], ACT.Exp, scale=-0.5), signal)

            def gate(L, p):
                need(act, "up_free", L, 2 * p + 2)
                c = conv[:, (2 * p + 1) % CSLOTS]
                E.did(f(c, c, ACT.Silu), "fs")

            def hidden_hi(L, p):
                need(act, "prod", L, p + 1)
                if p == 0:
                    act.wait_ge(S("st_kv"), 16 * (L + 1))
                E.did(nc.scalar.copy(hff_hi[:, p], conv[:, (2 * p + 1) % CSLOTS]), "hff_hi")

            for part in range(3):
                s5_params(0, part)
            ln(0)
            s5_tables(0, 0)
            for L in range(DEPTH):
                for i in range(N_IN):
                    tile_done(act, L, i)
                    if L > 0 and i == 0:
                        act.wait_ge(S("st_kv"), 16 * L)
                    E.did(nc.scalar.copy(hb[:, i], ps[:, (L * TILES + i) % 4, 0:T]), "in_evac")
                    if i == B0_AT[L]:
                        s5_evac(L, 0)
                        s5_tables(L, 1)
                        neg_c(L)
                    if i == 8:
                        need(act, "trvb", L, 1)
                        E.did(nc.scalar.copy(VBt[:], ps[:, 4].rearrange("p (a b) -> p a b", a=2)), "vbt")
                        E.settle()
                        act.dma_start(O["kv"][L], hb[:, KB:KB + 4]).then_inc(S("st_kv"), 16)
                    if i == 9:
                        s5_evac(L, 1)
                        need(act, "absz", L, 1)
                        E.did(f(SPL[:], SPL[:], ACT.Exp, scale=-1.0))
                        E.settle()
                        E.did(f(SPL[:], SPL[:], ACT.Ln, bias=1.0), "spe")
                    if i == 10:
                        need(act, "yd", L, 1)
                        E.did(f(yg[:, 0], yd[:, 0], ACT.Gelu_apprx_tanh), "gelu")
                        act.wait_ge(S("ld_sr"), 16 * (L + 1))
                        act.wait_ge(S("ld_gam"), 16)
                        for ht in range(2):
                            E.did(nc.scalar.mul(SR[:, :, ht], SR[:, :, ht], gam[:, ht:ht + 1]), "srg")
                    if i == 14:
                        need(act, "yd", L, 2)
                        E.did(f(yg[:, 1], yd[:, 1], ACT.Gelu_apprx_tanh), "gelu")
                    if i == 15:
                        for m in range(2):
                            need(act, "glu", L, m + 1)
                            E.did(f(sg[:, m], ps[:, 6 + m, 0:T], ACT.Sigmoid), "sig")
                    if i == 16:
                        need(act, "zmin", L, 1)
                        E.did(f(Z[:], Z[:], ACT.Exp), "wexp")
                        v_tokens(L)
                    if i == 17:
                        v_spread(L)
                        need(act, "ya", L, 1)
                        E.did(f(sq2[:], yg[:], ACT.Square), "sqa")
                    if i == 18:
                        need(act, "rstate", L, 1)
                        if L > 0:
                            act.wait_ge(S("st_rso"), 16 * L)
                        E.did(nc.scalar.copy(RSO[:], ps[:, 4, 0:2 * DV].rearrange("p (a b) -> p a b", a=2)), "rso")
                        E.settle()
                        act.dma_start(O["rprompt"][L], RSO[:]).then_inc(S("st_rso"), 16)
                        rms_root(L, "rmsa", 5, "rmsar")
                E.settle()
                E.did(f(hb[:, GC:GC + 4], hb[:, GC:GC + 4], ACT.Silu), "sgc")
                need(act, "ybev", L, 2)
                need(act, "ybs", L, 1)
                E.did(f(sq2[:], yb[:], ACT.Square), "sqb")
                need(act, "cata", L, 2)
                rms_root(L, "rmsb", 6, "rmsbr")
                for h in range(HEADS):
                    need(act, "ro", L, h + 1)
                    E.did(nc.scalar.copy(Oh[:, h], ps[:, 4 + h, 0:T]), "oev")
                act.dma_start(O["rsample"][L], SR[:]).then_inc(S("st_sr"), 16)
                for h in range(HEADS):
                    need(act, "gd", L, h + 1)
                    E.did(f(sqo[:, h], Oh[:, h], ACT.Square), "gsq")
                for h in range(HEADS):
                    need(act, "gvar", L, h + 1)
                    inv_sqrt(rg[:, h], ps[:, 4 + h, 0:T], LN_EPS, "gv1", "gr")
                ln(2 * L + 1)
                split_hi(L, SPLIT_FROM + 2)
                for i in range(N_UP):
                    tile_done(act, L, N_IN + N_OUT + i)
                    if i == 0:
                        act.wait_ge(S("ld_vec"), 16)
                    if i >= CSLOTS:
                        need(act, "hff_lo", L, (i - CSLOTS) // 2 + 1)
                    elif L > 0:
                        need(act, "hff_lo", L - 1, FT)
                    E.did(f(conv[:, i % CSLOTS], ps[:, (L * TILES + N_IN + N_OUT + i) % 4, 0:T], ACT.Identity,
                            scale=pv(L, "cw2", i), bias=pv(L, "cb", i)), "fc")
                    if i % 2 == 0 and i >= 2:
                        gate(L, i // 2 - 1)
                    split_hi(L, N_IN + N_OUT + i + 4)
                    if i % 2 == 1 and i >= 3:
                        hidden_hi(L, i // 2 - 1)
                gate(L, FT - 1)
                hidden_hi(L, FT - 1)
                for d in range(4, N_DOWN):
                    split_hi(L, N_IN + N_OUT + N_UP + d)
                    if L + 1 < DEPTH:
                        if d in S5_ACT:
                            s5_params(L + 1, S5_ACT.index(d))
                        if d == 18:
                            s5_tables(L + 1, 0)
                ln(2 * L + 2)
            for name, n in (("st_kv", DEPTH), ("st_rso", DEPTH), ("st_sr", DEPTH), ("st_vs", DEPTH)):
                act.wait_ge(S(name), 16 * n)

        @block.vector
        def _(dve):
            E = Engine(dve, "dve_step")
            tt, ts, stt = nc.vector.tensor_tensor, nc.vector.tensor_scalar, nc.vector.scalar_tensor_tensor
            cp = nc.vector.tensor_copy

            E.did(nc.vector.memset(eps_all[:, 0:1], LN_EPS), "eps_set")
            E.did(nc.vector.memset(eps_all[:, 1:2], RMS_EPS), "eps_set")
            E.did(nc.vector.memset(halfpi[:], math.pi / 2), "eps_set")
            E.did(nc.vector.memset(qbd[:], 0.0))
            E.settle()

            def seq(*makers):
                for m in makers:
                    E.settle()
                    E.did(m())

            def ln_diff(q, t):
                E.settle()
                E.did(tt(z[:, t], z[:, t], ps[:, 4, 0:T], ALU.subtract), "lnd")
                if 0 < t < KT - 1:
                    E.settle()
                    E.did(tt(acc[:, 0], z[:, 0] if t == 1 else acc[:, 0], z[:, t], ALU.add),
                          "lnacc1" if t == KT - 2 else None)

            def ln_tail(q):
                needq(dve, "lnmu2", q, 1)
                needq(dve, "lnvar", q, 1)
                E.did(tt(lnr[:], ps[:, 6, 0:T], rs2[:], ALU.subtract), "lnv")
                for hf in range(2):
                    zz = z[:, 4 * hf:4 * hf + 4]
                    E.did(tt(zz, zz, bcast(ps[:, 5, 0:T], [P, 4, T], 1), ALU.subtract))
                    if hf == 0:
                        needq(dve, "lnr", q, 1)
                    E.settle()
                    for t in range(4 * hf, 4 * hf + 4):
                        E.did(tt(z[:, t], z[:, t], lnr[:], ALU.mult), "xn")

            def split_lo(L, i):
                need(dve, "w_hi", L, i - SPLIT_FROM + 1)
                slot = split_slot(i)
                E.did(tt(w_lo[:, slot], ring[:, ring_slot(L * UNITS + i)], w_hi[:, slot].bitcast(F32), ALU.subtract),
                      "w_lo_dve")

            def gated(L, p):
                need(dve, "fs", L, p + 1)
                c = conv[:, (2 * p + 1) % CSLOTS]
                E.did(tt(c, conv[:, 2 * p % CSLOTS], c, ALU.mult), "prod")

            lr, li = s5in[:, 0], s5in[:, 1]
            dt, ldr, mg, n, r, sn, cs, ab, den, t0, t1, t2 = (tmp[:, i] for i in range(12))

            def s5_rates(L):
                dve.wait_ge(S("ld_s5in"), 16 * (L + 1))
                E.did(ts(lr, lr, -1e-4, None, ALU.min), "v_s5clear")
                dve.wait_ge(S("a_dt"), L + 1)
                E.settle()
                E.did(tt(ldr, lr, dt, ALU.mult), "v_ldt")
                seq(lambda: tt(t0, li, dt, ALU.mult))

            def s5_angle(L):
                seq(lambda: ts(n, t0, 1.0 / TWO_PI, ROUND, ALU.mult, ALU.add),
                    lambda: ts(n, n, -ROUND, None, ALU.add),
                    lambda: stt(r, n, -TWO_PI_HI, t0, ALU.mult, ALU.add))

            def s5_angle2(L):
                seq(lambda: stt(r, n, -TWO_PI_LO, r, ALU.mult, ALU.add),
                    lambda: ts(r, r, PI_SAFE, -PI_SAFE, ALU.min, ALU.max))
                E.settle()
                E.did(stt(ab, r, -1.0, r, ALU.mult, ALU.max), "v_red")

            def s5_turns(L):
                seq(lambda: ts(fhi[:], r[:, 0:J], 1.0 / TWO_PI, ROUND_15, ALU.mult, ALU.add),
                    lambda: ts(fhi[:], fhi[:], -ROUND_15, None, ALU.add),
                    lambda: ts(t1[:, 0:J], r[:, 0:J], 1.0 / TWO_PI, None, ALU.mult),
                    lambda: tt(flo[:], t1[:, 0:J], fhi[:], ALU.subtract))

            def s5_den(L):
                seq(lambda: tt(den, lr, lr, ALU.mult),
                    lambda: tt(t1, li, li, ALU.mult),
                    lambda: tt(den, den, t1, ALU.add),
                    lambda: nc.vector.reciprocal(den, den))

            def s5_a(L):
                dve.wait_ge(S("a_sc"), L + 1)
                dve.wait_ge(S("a_mag"), L + 1)
                seq(lambda: cp(mag[:], mg[:, 0:J]),
                    lambda: tt(t0, mg, cs, ALU.mult),
                    lambda: tt(sn, mg, sn, ALU.mult),
                    lambda: cp(are[:], t0[:, 0:J]),
                    lambda: cp(aim[:], sn[:, 0:J]),
                    lambda: ts(t0, t0, -1.0, None, ALU.add))

            def s5_f_re(L):
                seq(lambda: tt(t1, t0, lr, ALU.mult),
                    lambda: tt(t2, sn, li, ALU.mult),
                    lambda: tt(t1, t1, t2, ALU.add),
                    lambda: tt(t1, t1, den, ALU.mult))

            def s5_f_im(L):
                seq(lambda: tt(sn, sn, lr, ALU.mult),
                    lambda: tt(t0, t0, li, ALU.mult),
                    lambda: tt(t0, sn, t0, ALU.subtract),
                    lambda: tt(t0, t0, den, ALU.mult))

            def s5_bb(L):
                dve.wait_ge(S("ld_s5b"), 16 * (L + 1))
                fr, fi = t1[:, J:264], t0[:, J:264]
                seq(lambda: tt(bb[:, 0], fr, s5b[:, 0], ALU.mult),
                    lambda: tt(t2[:, 0:256], fi, s5b[:, 1], ALU.mult),
                    lambda: tt(bb[:, 0], bb[:, 0], t2[:, 0:256], ALU.subtract),
                    lambda: tt(bb[:, 1], fr, s5b[:, 1], ALU.mult),
                    lambda: tt(t2[:, 0:256], fi, s5b[:, 0], ALU.mult))
                E.settle()
                E.did(tt(bb[:, 1], bb[:, 1], t2[:, 0:256], ALU.add), "bb")

            def s5_phases(L, hf, part=None):
                if L == 0 and hf == 0:
                    dve.wait_ge(S("ld_steps"), 16)
                if hf == 1:
                    needq(dve, "x", 2 * L, KT)
                q, p = tabs[hf]
                st = bcast(steps[:], [P, HJ, SEQ], 1)
                fh = bcast(fhi[:, hf * HJ:(hf + 1) * HJ], [P, HJ, SEQ], 2)
                fl = bcast(flo[:, hf * HJ:(hf + 1) * HJ], [P, HJ, SEQ], 2)
                if part in (0, None):
                    seq(lambda: tt(p, st, fh, ALU.mult),
                        lambda: ts(q, p, ROUND, -ROUND, ALU.add, ALU.add))
                if part in (1, None):
                    seq(lambda: tt(p, p, q, ALU.subtract),
                        lambda: tt(q, st, fl, ALU.mult))
                if part in (2, None):
                    seq(lambda: tt(p, p, q, ALU.add),
                        lambda: ts(q, p, ROUND, -ROUND, ALU.add, ALU.add))
                if part in (3, None):
                    seq(lambda: tt(p, p, q, ALU.subtract))
                    E.settle()
                    E.did(stt(q, p, -1.0, p, ALU.mult, ALU.max), "tph")

            S5_PARTS = (s5_rates, s5_angle, s5_angle2, s5_turns, s5_den, s5_a, s5_f_re, s5_f_im, s5_bb)

            def s5_half(L, hf):
                tm = slice(0, SEQ)
                TC, TS = tabs[hf]
                need(dve, "buev", L, 8 * hf + 8)
                need(dve, "tab", L, 2 * hf + 2)
                if hf == 1:
                    need(dve, "s5y", L, 1)
                E.did(tt(P1[:, :, tm], TC, BR[:, :, tm], ALU.mult))
                E.did(tt(P2[:, :, tm], TS, BI[:, :, tm], ALU.mult))
                E.settle()
                E.did(tt(P1[:, :, tm], P1[:, :, tm], P2[:, :, tm], ALU.add))
                need(dve, "poolpre", L, hf + 1)
                E.did(tt(P3[:, :, tm], P3[:, :, tm], P4[:, :, tm], ALU.subtract))
                E.settle()
                for jj in range(HJ):
                    m = mag[:, hf * HJ + jj:hf * HJ + jj + 1].to_broadcast([P, SEQ])
                    E.did(nc.vector.tensor_tensor_scan(BR[:, jj, tm], m, P1[:, jj, tm], 0.0, ALU.mult, ALU.add))
                    ins = nc.vector.tensor_tensor_scan(BI[:, jj, tm], m, P3[:, jj, tm], 0.0, ALU.mult, ALU.add)
                    E.did(ins, "scan" if jj == HJ - 1 else None)
                E.settle()
                E.did(tt(P1[:, :, tm], TC, BR[:, :, tm], ALU.mult))
                E.did(tt(P2[:, :, tm], TS, BI[:, :, tm], ALU.mult))
                E.settle()
                E.did(tt(P1[:, :, tm], P1[:, :, tm], P2[:, :, tm], ALU.subtract))
                if hf == 0:
                    dve.wait_ge(S("ld_x0"), 16 * (L + 1))
                jr = slice(hf * HJ, (hf + 1) * HJ)
                ar, ai = bcast(are[:, jr], [P, HJ, NS], 2), bcast(aim[:, jr], [P, HJ, NS], 2)
                x0r, x0i = s5x0[:, 0, jr], s5x0[:, 1, jr]
                E.did(tt(stmp[:, 0], ar, x0r, ALU.mult))
                E.did(tt(stmp[:, 1], ai, x0i, ALU.mult))
                E.did(tt(stmp[:, 2], ar, x0i, ALU.mult))
                E.did(tt(stmp[:, 3], ai, x0r, ALU.mult), "dve_x0")
                E.settle()
                E.did(tt(stmp[:, 0], stmp[:, 0], stmp[:, 1], ALU.subtract))
                E.did(tt(stmp[:, 2], stmp[:, 2], stmp[:, 3], ALU.add))
                E.settle()
                E.did(tt(P1[:, :, SEQ:T], stmp[:, 0], BR[:, :, SEQ:T], ALU.add))
                E.did(tt(P3[:, :, SEQ:T], stmp[:, 2], BI[:, :, SEQ:T], ALU.add))
                need(dve, "poolpost", L, hf + 1)
                E.settle()
                E.did(tt(P3[:, :, tm], P3[:, :, tm], P4[:, :, tm], ALU.add))
                E.settle()
                if L > 0 and hf == 0:
                    dve.wait_ge(S("st_s5"), 16 * L)
                E.did(cp(s5o[:, 0, jr], P1[:, :, SEQ - 1:T]))
                E.did(cp(s5o[:, 1, jr], P3[:, :, SEQ - 1:T]), "s5x")

            def rotary(L):
                if L == 0:
                    dve.wait_ge(S("ld_rope"), 16)
                qk = hb[:, QC:QC + 4]
                for i in range(4):
                    need(dve, "rot", L, i + 1)
                    if i == 0:
                        E.settle()
                    E.did(tt(P2[:, i], ps[:, 4 + i, 0:T], rope[:, 1], ALU.mult), "rotrd")
                E.settle()
                E.did(tt(qk, qk, bcast(rope[:, 0], [P, 4, T], 1), ALU.mult))
                E.settle()
                E.did(tt(qk, qk, P2[:], ALU.add), "qk")
                E.settle()
                E.did(ts(qs[:], hb[:, QC:QC + 2, SEQ:T], DH ** -0.5, None, ALU.mult), "qs")

            def ret_inner(L):
                if L == 0:
                    dve.wait_ge(S("ld_dtab"), 16)
                    dve.wait_ge(S("ld_kdec"), 16)
                need(dve, "trk", L, 1)
                kd = kdec[:].unsqueeze(3).to_broadcast([P, 2, HEADS, 64])
                for t2 in range(2):
                    E.did(tt(KD[:, t2].rearrange("p (h d) -> p h d", h=HEADS),
                             ps[:, 7, 256 * t2:256 * t2 + 256].rearrange("p (h d) -> p h d", h=HEADS),
                             kd[:, t2], ALU.mult), "kd" if t2 else None)
                for h in range(HEADS):
                    need(dve, "rin", L, h + 1)
                    E.did(tt(RI[:, h, 0:SEQ], ps[:, 4 + h, 0:SEQ], dtab[:, h], ALU.mult))
                    E.did(tt(RI[:, h, SEQ:DEC], ps[:, 4 + h, SEQ:DEC], dtab[:, h, 0:P], ALU.mult), "ri")

            def ret_samples(L):
                need(dve, "srg", L, 2)
                dve.wait_ge(S("ld_vbc"), 32 * (L + 1))
                for b in range(NS):
                    for ht in range(2):
                        last = b == NS - 1 and ht == 1
                        E.did(stt(SR[:, b, ht], VBC[:, b, ht], hb[:, KC + ht, SEQ + b:SEQ + b + 1], SR[:, b, ht],
                                  ALU.mult, ALU.add), "sr" if last else None)

            def query_blocks(L):
                need(dve, "in_evac", L, QB_ + 2)
                for c in range(2):
                    r = slice(64 * c, 64 * c + 64)
                    E.did(cp(qbd[r, :, :, c], hb[r, QB_:QB_ + 2, SEQ:T]), "qb")

            def sb_first(L):
                for h in range(HEADS):
                    need(dve, "sbz", L, h + 1)
                    E.did(ts(Z[:, h * DEC:(h + 1) * DEC], ps[:, 4 + h, 0:DEC], DH ** -0.5, pv(L, "bias", h),
                             ALU.mult, ALU.add), "zev")
                need(dve, "sbzs", L, 1)
                E.did(stt(Z[:, 4 * DEC:4 * DEC + 64].rearrange("p (n h) -> p n h", h=HEADS),
                          ps[:, 4, 0:64].rearrange("p (n h) -> p n h", h=HEADS), DH ** -0.5,
                          bcast(pv(L, "bias", 0, HEADS), [P, 16, HEADS], 1), ALU.mult, ALU.add), "zs")
                E.settle()
                E.did(stt(SPL[:], Z[:], -1.0, Z[:], ALU.mult, ALU.max), "absz")

            def diagonals(buf):
                v = buf[:, 0:4 * DEC].rearrange("p (h c) -> p h c", h=HEADS)
                return v[:, :, 0:P], v[:, :, SEQ:DEC]

            mask = bcast(C["mask"], [P, HEADS, P], 1)

            def sb_second(L):
                need(dve, "spe", L, 1)
                E.did(stt(SPL[:], Z[:], 0.0, SPL[:], ALU.max, ALU.add))
                E.settle()
                d0, d1 = diagonals(SPL)
                E.did(tt(d0, d0, mask, ALU.mult))
                E.did(tt(d1, d1, mask, ALU.mult), "spl")

            def sb_third(L):
                for h in range(HEADS):
                    need(dve, "sbs", L, h + 1)
                    E.did(tt(Z[:, h * DEC:(h + 1) * DEC], Z[:, h * DEC:(h + 1) * DEC], ps[:, 4 + h, 0:DEC],
                             ALU.subtract), "zsub")
                need(dve, "sbss", L, 1)
                E.did(tt(Z[:, 4 * DEC:4 * DEC + 64], Z[:, 4 * DEC:4 * DEC + 64], ps[:, 4, 0:64], ALU.subtract), "zsubs")
                E.settle()
                E.did(ts(Z[:], Z[:], 0.0, None, ALU.min), "zmin")

            def sb_mask(L):
                need(dve, "wexp", L, 1)
                d0, d1 = diagonals(Z)
                E.did(tt(d0, d0, mask, ALU.mult))
                E.did(tt(d1, d1, mask, ALU.mult), "w")

            def sb_out(L):
                for ht in range(2):
                    need(dve, "sby", L, ht + 1)
                    E.did(cp(yb[:, ht, 0:SEQ], ps[:, 4 + ht, 0:SEQ]), "ybev")
                need(dve, "sbys", L, 1)
                for c in range(2):
                    r = slice(64 * c, 64 * c + 64)
                    E.did(cp(yb[r, :, SEQ:T], ps[r, 6, 0:32].rearrange("p (a b c) -> p a b c", a=2, c=2)[:, :, :, c]),
                          "ybs" if c else None)

            def sb_cat(L):
                need(dve, "rmsbr", L, 1)
                for t in range(2):
                    E.did(stt(hb[:, QB_ + t], yb[:, t], pv(L, "norm_b_g", t), rs2[:], ALU.mult, ALU.mult), "catb")

            def gn_center(L):
                for h in range(HEADS):
                    need(dve, "gmean", L, h + 1)
                    E.did(tt(Oh[:, h], Oh[:, h], ps[:, 4 + h, 0:T], ALU.subtract), "gd")

            def gn_out(L):
                for h in range(HEADS):
                    need(dve, "gr", L, h + 1)
                    E.settle()
                    E.did(tt(Oh[:, h], Oh[:, h], rg[:, h], ALU.mult))
                    E.settle()
                    E.did(ts(Oh[:, h], Oh[:, h], pv(L, "gn_g", h), pv(L, "gn_b", h), ALU.mult, ALU.add))
                need(dve, "sgc", L, 1)
                E.settle()
                for h in range(HEADS):
                    E.did(tt(hb[:, GC + h], Oh[:, h], hb[:, GC + h], ALU.mult), "catc")

            def s5_skip(L, hf):
                need(dve, "s5y", L, hf + 1)
                E.did(stt(yd[:, hf], hb[:, U + hf], pv(L, "s5_d", hf), ps[:, 4, 0:T], ALU.mult, ALU.add), "yd")

            def s5_out(L):
                need(dve, "sig", L, 2)
                E.did(tt(yg[:], yg[:], sg[:], ALU.mult), "ya")

            def s5_cat(L):
                need(dve, "rmsar", L, 1)
                for t in range(2):
                    E.did(stt(hb[:, U + t], yg[:, t], pv(L, "norm_a_g", t), rs2[:], ALU.mult, ALU.mult), "cata")

            def residual(L, first, i):
                bank = ps[:, (L * TILES + (N_IN if first else N_IN + N_OUT + N_UP) + i) % 4, 0:T]
                tile_done(dve, L, N_IN + i) if first else down_done(dve, L, i)
                E.did(stt(z[:, i], x[:, i], ALPHA, bank, ALU.mult, ALU.add), "z")

            for part in S5_PARTS:
                part(0)
            dve.wait_ge(S("ld_x"), 16)
            needq(dve, "lnc", 0, 1)
            for t in range(KT):
                ln_diff(0, t)
            ln_tail(0)
            s5_phases(0, 0)
            for L in range(DEPTH):
                s5_phases(L, 1)
                s5_half(L, 0)
                query_blocks(L)
                sb_first(L)
                s5_skip(L, 0)
                s5_half(L, 1)
                sb_second(L)
                s5_skip(L, 1)
                rotary(L)
                sb_third(L)
                s5_out(L)
                sb_mask(L)
                ret_inner(L)
                sb_out(L)
                ret_samples(L)
                s5_cat(L)
                sb_cat(L)
                gn_center(L)
                gn_out(L)
                for i in range(N_OUT):
                    residual(L, True, i)
                    if i == 3:
                        needq(dve, "lnc", 2 * L + 1, 1)
                        for t in range(3):
                            ln_diff(2 * L + 1, t)
                    if i >= 3:
                        ln_diff(2 * L + 1, i)
                    if i in (5, 6):
                        split_lo(L, SPLIT_FROM + i - 5)
                ln_tail(2 * L + 1)
                need(dve, "sr", L, 1)
                for t in range(1, KT, 2):
                    need(dve, "x_hi", L, t + 1)
                    E.did(tt(x_lo[:, t], x[:, t], x_hi[:, t].bitcast(F32), ALU.subtract), "x_lo_dve")
                split_lo(L, SPLIT_FROM + 2)
                dve.wait_ge(S("ld_prev"), 16 * (L + 1))
                if L > 0:
                    dve.wait_ge(S("st_conv"), 16 * L)
                w0 = bcast(pv(L, "cw0", 0, N_UP), [P, N_UP, NS], 2)
                w1 = bcast(pv(L, "cw1", 0, N_UP), [P, N_UP, NS], 2)
                c10 = cout[:, :, 2:10]
                E.did(tt(spre[:], prev[:, :, 0], w0, ALU.mult))
                E.did(tt(c10, prev[:, :, 1], w1, ALU.mult))
                E.settle()
                E.did(tt(spre[:], spre[:], c10, ALU.add), "spre")
                for i in range(N_UP):
                    need(dve, "fc", L, i + 1)
                    bank, c = ps[:, (L * TILES + N_IN + N_OUT + i) % 4], conv[:, i % CSLOTS]
                    E.settle()
                    E.did(cp(cout[:, i], bank[:, SEQ - 2:T]))
                    E.did(stt(c[:, 1:SEQ], bank[:, 0:SEQ - 1], pv(L, "cw1", i), c[:, 1:SEQ], ALU.mult, ALU.add))
                    E.did(tt(c[:, SEQ:T], c[:, SEQ:T], spre[:, i], ALU.add))
                    E.settle()
                    E.did(stt(c[:, 2:SEQ], bank[:, 0:SEQ - 2], pv(L, "cw0", i), c[:, 2:SEQ], ALU.mult, ALU.add), "up_free")
                    if i % 2 == 1 and i >= 3:
                        gated(L, i // 2 - 1)
                    if not by_pool(N_IN + N_OUT + i + 4):
                        split_lo(L, N_IN + N_OUT + i + 4)
                gated(L, FT - 1)
                done = 0
                for d in range(N_DOWN):
                    if d >= 1 and L + 1 < DEPTH:
                        if d <= len(S5_PARTS):
                            S5_PARTS[d - 1](L + 1)
                        elif d - 1 - len(S5_PARTS) < 4:
                            s5_phases(L + 1, 0, d - 1 - len(S5_PARTS))
                    if 4 <= d + 3 < N_DOWN and not by_pool(N_IN + N_OUT + N_UP + d + 3):
                        split_lo(L, N_IN + N_OUT + N_UP + d + 3)
                    while done < KT and (FT * (done + 1) - 1) // 8 == d:
                        i = done
                        done += 1
                        residual(L, False, i)
                        if i == 5:
                            needq(dve, "lnc", 2 * L + 2, 1)
                            for t in range(5):
                                ln_diff(2 * L + 2, t)
                        if i >= 5:
                            ln_diff(2 * L + 2, i)
                ln_tail(2 * L + 2)

        @block.gpsimd
        def _(pool):
            E = Engine(pool, "pool_step")
            tt = nc.gpsimd.tensor_tensor
            tm = slice(0, SEQ)

            def ln_squares(q):
                for t in range(1, KT - 1):
                    needq(pool, "lnsq", q, t + 1)
                    E.settle()
                    E.did(tt(acc[:, 1], sqt[:, 0] if t == 1 else acc[:, 1], sqt[:, t % 3], ALU.add),
                          "lnacc2" if t == KT - 2 else "pool_ln")

            def split_lo(L, i):
                need(pool, "w_hi", L, i - SPLIT_FROM + 1)
                slot = split_slot(i)
                E.did(tt(w_lo[:, slot], ring[:, ring_slot(L * UNITS + i)], w_hi[:, slot].bitcast(F32), ALU.subtract),
                      "w_lo_pool")

            ln_squares(0)
            for L in range(DEPTH):
                for hf in range(2):
                    TC, TS = tabs[hf]
                    need(pool, "buev", L, 8 * hf + 8)
                    need(pool, "tab", L, 2 * hf + 2)
                    if hf == 1:
                        need(pool, "s5y", L, 1)
                    E.settle()
                    E.did(tt(P4[:, :, tm], TS, BR[:, :, tm], ALU.mult))
                    E.did(tt(P3[:, :, tm], TC, BI[:, :, tm], ALU.mult), "poolpre")
                    need(pool, "scan", L, hf + 1)
                    E.settle()
                    E.did(tt(P4[:, :, tm], TS, BR[:, :, tm], ALU.mult))
                    E.did(tt(P3[:, :, tm], TC, BI[:, :, tm], ALU.mult), "poolpost")
                need(pool, "s5x", L, 2)
                pool.dma_start(O["s5"][L], s5o[:]).then_inc(S("st_s5"), 16)
                ln_squares(2 * L + 1)
                need(pool, "sr", L, 1)
                for t in range(0, KT, 2):
                    need(pool, "x_hi", L, t + 1)
                    E.did(tt(x_lo[:, t], x[:, t], x_hi[:, t].bitcast(F32), ALU.subtract), "x_lo_pool")
                need(pool, "spre", L, 1)
                pool.dma_start(O["convprev"][L], prev[:, :, 1]).then_inc(S("st_prev"), 16)
                for p in range(FT):
                    for i in (N_IN + N_OUT + 2 * p + 6, N_IN + N_OUT + 2 * p + 7):
                        if by_pool(i) and i <= N_IN + N_OUT + N_UP + 3:
                            split_lo(L, i)
                    need(pool, "hff_hi", L, p + 1)
                    E.did(tt(hff_lo[:, p], conv[:, (2 * p + 1) % CSLOTS], hff_hi[:, p].bitcast(F32), ALU.subtract), "hff_lo")
                pool.dma_start(O["conv"][L], cout[:]).then_inc(S("st_conv"), 16)
                for d in range(4, N_DOWN):
                    if by_pool(N_IN + N_OUT + N_UP + d):
                        split_lo(L, N_IN + N_OUT + N_UP + d)
                ln_squares(2 * L + 2)
            needq(pool, "x", 2 * DEPTH, KT)
            pool.dma_start(O["y"], x[:]).then_inc(S("st_y"), 16)
            pool.wait_ge(S("st_y"), 16)
            for name in ("st_s5", "st_prev", "st_conv"):
                pool.wait_ge(S(name), 16 * DEPTH)


def constants():
    f = np.float32
    eye = np.eye(P, dtype=f)
    k, q = np.arange(P)[:, None], np.arange(P)[None, :]
    perm = np.zeros((P, P), f)
    for m in range(P):
        perm[m + 32 if m % 64 < 32 else m - 32, m] = -1.0 if m % 64 < 32 else 1.0
    cst = np.stack([eye, (k >= q).astype(f), np.ones((P, P), f), (k < q).astype(f), perm,
                    np.full((P, P), 1 / D_MODEL, f), np.full((P, P), 1 / 256, f), np.full((P, P), 1 / P, f)], 1)
    pos = np.concatenate([np.arange(SEQ), np.full(NS, SEQ)]).astype(f)
    inv = (10000.0 ** (-np.arange(32, dtype=f) / 32)).astype(f)[np.arange(P) % 32]
    ang = (inv[:, None] * pos[None, :]).astype(f)
    rope = np.stack([np.cos(ang), np.sin(ang)], 1).astype(f)
    gap = np.arange(SEQ)[None, None, :] - np.arange(P)[:, None, None]
    dtab = np.where(gap >= 0, np.exp(LOG_GAMMA[None, :, None] * np.maximum(gap, 0)), 0.0) * DH ** -0.5
    left = SEQ - 1 - (np.arange(P)[:, None] + P * np.arange(2)[None, :])
    kdec = np.exp(LOG_GAMMA[None, None, :] * left[:, :, None])
    gam = np.exp(LOG_GAMMA)[2 * np.arange(2)[None, :] + (np.arange(P) // 64)[:, None]]
    steps = np.broadcast_to(np.arange(SEQ, dtype=f), (P, SEQ))
    return {"cst": cst, "rope": rope, "dtab": dtab.astype(f), "kdec": kdec.astype(f), "gam": gam.astype(f),
            "steps": steps}


def lay_out(i):
    f = np.float32
    D = DEPTH
    a = {}
    xt = np.concatenate([i["x_prompt"][0], i["x_sample"][:, 0]], 0)
    a["xT"] = xt.T.reshape(KT, P, T).transpose(1, 0, 2)
    w_in = i["w_in"].reshape(D, 8, P, N_IN, P).transpose(0, 3, 2, 1, 4)
    w_out = i["w_out"].reshape(D, 8, P, KT, P).transpose(0, 3, 2, 1, 4)
    up_order = [m + FT * g for m in range(FT) for g in range(2)]
    w_up = i["ffn_w_up"].reshape(D, 8, P, N_UP, P).transpose(0, 3, 2, 1, 4)[:, up_order]
    w_dn = i["ffn_w_down"].reshape(D, FT, P, KT, P).transpose(0, 3, 1, 2, 4)
    w_dn = w_dn.reshape(D, N_DOWN, 8, P, P).transpose(0, 1, 3, 2, 4)
    a["units"] = np.concatenate([w_in, w_out, w_up, w_dn], 1).reshape(D * UNITS, P, 8, P)
    col = lambda v: v.reshape(-1, P).T
    upc = lambda v: col(v)[:, up_order]
    cols = [col(i["ln_in_g"]), col(i["ln_in_b"])]
    for l in range(D):
        cols += [col(i[n][l]) for n in ("norm_a_g", "norm_b_g", "ret_gn_g", "ret_gn_b", "ln1_g", "ln1_b",
                                        "ln2_g", "ln2_b", "s5_d")]
        cols += [upc(i["ffn_conv_w"][l, j]) for j in range(3)] + [upc(i["ffn_conv_b"][l])]
        cols += [np.broadcast_to(i["sb_logit_bias"][l], (P, HEADS))]
    a["vec"] = np.concatenate(cols, 1)
    j8 = lambda v: v.reshape(D, J, 2 * 64).transpose(0, 2, 1)
    def rows(v):
        v = v.reshape(D, 2, HJ, 1, 1, 2, 64)
        v = np.broadcast_to(v, (D, 2, HJ, 2, 16, 2, 64))
        return v.transpose(0, 2, 3, 4, 1, 5, 6).reshape(D, P, 256)
    ls = np.broadcast_to(i["s5_log_step"][:, :, None], i["s5_lambda_re"].shape)
    a["s5in"] = np.stack([np.concatenate([j8(v), rows(v)], 2)
                          for v in (i["s5_lambda_re"], i["s5_lambda_im"], ls)], 2)
    s5b = np.zeros((D, 2, HJ, 2, 16, 2, 2, 64), f)
    s5c = np.zeros((D, 2, J, 2, 64, 2, 16), f)
    for c, (nb, nc_) in enumerate((("s5_b_re", "s5_c_re"), ("s5_b_im", "s5_c_im"))):
        b = i[nb].reshape(D, 2, HJ, 2, 64, 16)
        cc = i[nc_].reshape(D, J, 2, 16, 64)
        for gl in range(2):
            s5b[:, c, :, gl, :, :, gl] = b[:, :, :, gl].transpose(0, 2, 4, 1, 3)
            s5c[:, c, :, gl, :, gl] = cc[:, :, gl].transpose(0, 1, 3, 2)
    a["s5b"] = s5b.reshape(D, 2, P, 256).transpose(0, 2, 1, 3)
    a["s5c"] = s5c.reshape(D, 2, J, P, 32).transpose(0, 3, 1, 2, 4)
    a["s5x0"] = np.stack([i[n].reshape(D, NS, J, P).transpose(0, 3, 2, 1)
                          for n in ("state_s5_re", "state_s5_im")], 2)
    a["wglu"] = i["s5_w_glu"].reshape(D, 2, P, 256).transpose(0, 2, 1, 3)
    a["kpool"] = i["cache_k"].reshape(D, POOL, PAGE, 2, P).transpose(0, 1, 4, 3, 2).reshape(D, POOL, P, 256)
    a["vpool"] = i["cache_v"].reshape(D, POOL, PAGE, 256)
    a["sret"] = i["state_ret"].reshape(D, NS, 2, P, DV).transpose(0, 3, 1, 2, 4)
    a["prev"] = i["state_conv"].reshape(D, NS, 2, N_UP, P).transpose(0, 4, 3, 2, 1)[:, :, up_order]
    a["pages"] = i["page_table"].reshape(1, -1)
    a.update(constants())
    return {k: np.ascontiguousarray(v) for k, v in a.items()}, up_order


_OUTS = {"y": (P, KT, T), "kv": (DEPTH, P, 4, T), "s5": (DEPTH, P, 2, J, NS + 1), "rprompt": (DEPTH, P, 2, DV),
         "rsample": (DEPTH, P, NS, 2, DV), "conv": (DEPTH, P, N_UP, 10), "convprev": (DEPTH, P, N_UP, NS)}


def kernel(**inputs):
    import concourse.bacc as _bacc
    from concourse.bass_utils import run_bass_kernel_spmd as _run

    arrays, up_order = lay_out({k: np.asarray(v) for k, v in inputs.items()})
    nc = _bacc.Bacc("TRN2", target_bir_lowering=False, num_devices=1)
    A = {k: nc.dram_tensor(f"in_{k}", v.shape, mybir.dt.from_np(v.dtype), kind="ExternalInput").ap()
         for k, v in arrays.items()}
    O = {k: nc.dram_tensor(f"out_{k}", s, F32, kind="ExternalOutput").ap() for k, s in _OUTS.items()}
    hybrid_step(nc, A, O)
    res = _run(nc, [{f"in_{k}": v for k, v in arrays.items()}], core_ids=[0]).results[0]
    r = {k: np.asarray(res[f"out_{k}"]) for k in _OUTS}
    D = DEPTH
    y = r["y"].transpose(2, 1, 0).reshape(T, D_MODEL)
    kv = r["kv"].transpose(0, 3, 2, 1).reshape(D, T, 2, HEADS, DH)
    s5 = r["s5"].transpose(0, 2, 4, 3, 1).reshape(D, 2, NS + 1, 16, 64)
    rp = r["rprompt"].transpose(0, 2, 1, 3).reshape(D, 1, HEADS, DH, DV)
    rs = r["rsample"].transpose(0, 2, 3, 1, 4).reshape(D, NS, HEADS, DH, DV)
    back = np.argsort(up_order)
    cv = r["conv"][:, :, back].transpose(0, 3, 2, 1).reshape(D, 10, 2 * D_FF)
    cp = r["convprev"][:, :, back].transpose(0, 3, 2, 1).reshape(D, NS, 2 * D_FF)
    return (y[None, :SEQ], y[SEQ:, None],
            kv[:, None, :SEQ, 0], kv[:, None, :SEQ, 1], kv[:, SEQ:, None, 0], kv[:, SEQ:, None, 1],
            s5[:, 0, :1], s5[:, 1, :1], s5[:, 0, 1:], s5[:, 1, 1:], rp, rs,
            cv[:, None, :2], np.stack([cp, cv[:, 2:]], 2))
```

```python
import math
from contextlib import ExitStack

import numpy as np

import concourse.bass as bass
from concourse import mybir

F32 = mybir.dt.float32
F32R = mybir.dt.float32r
ALU = mybir.AluOpType
ACT = mybir.ActivationFunctionType

P = 128
SEQ, NS = 256, 8
T = SEQ + NS
DEPTH, D_MODEL, D_FF = 2, 1024, 2816
KT = D_MODEL // P
FT = D_FF // P
HEADS, DH, DV = 4, 64, 128
PAGES, PAGE, POOL = 2, 128, 20
ALPHA = (2.0 * DEPTH) ** 0.25
LN_EPS, RMS_EPS = 1e-5, 1e-6
J = 8
HJ = J // 2
DEC = 384

U, QB_, KB, VB_, QC, KC, VC, GC = 0, 2, 4, 6, 8, 10, 12, 16
N_IN, N_OUT, N_UP = 20, KT, 2 * FT
N_DOWN = KT * FT // 8
UNITS = N_IN + N_OUT + N_UP + N_DOWN
RING = 5
PLAIN_UP = N_IN + N_OUT
SPLIT = [i for i in range(N_IN, UNITS) if i != PLAIN_UP]
SPLITS = len(SPLIT)
SRING = 4
POOL_FROM = [2, 0]
SB_BANK = [5, 6, 7, 4]
ROT_BANK = [4, 5, 6, 7]
OUT_BANK, GN_BANK = [5, 6, 7, 4], [7, 4, 5, 6]
CSLOTS = 8
TILES = N_IN + N_OUT + N_UP + KT
S5_ACT = [5, 6, 8]
PHASES_AT = [11, 13, 15, 17]
TAB0_AT, TAB1_AT = 3, [5, 3]
B0_AT = [3, 2]

PER = {"norm_a_g": 2, "norm_b_g": 2, "gn_g": 4, "gn_b": 4, "ln1_g": 8, "ln1_b": 8, "ln2_g": 8,
       "ln2_b": 8, "s5_d": 2, "cw0": N_UP, "cw1": N_UP, "cw2": N_UP, "cb": N_UP, "bias": HEADS}
COL, _at = {}, 2 * KT
for _n, _w in PER.items():
    COL[_n] = _at
    _at += _w
PER_LAYER = _at - 2 * KT
N_VEC = 2 * KT + DEPTH * PER_LAYER

CONSTS = ["mean_v", "mean_d", "ident", "tri", "ones", "mask", "perm", "mean_w"]
LOG_GAMMA = np.log1p(-np.exp2(-5.0 - np.arange(HEADS)))
TWO_PI = 2.0 * math.pi
TWO_PI_HI = float(np.float32(6.28125))
TWO_PI_LO = TWO_PI - TWO_PI_HI
PI_SAFE = 3.1415925
TWO_PI_IN = 6.283185
ROUND = 1.5 * 2.0**23
ROUND_15 = 1.5 * 2.0**8


def hybrid_step(nc, A, O):
    with ExitStack() as ctx:
        sems = {}

        def S(name):
            if name not in sems:
                sems[name] = ctx.enter_context(nc.semaphore(name))
            return sems[name]

        place = {}
        here = [-(-nc.sbuf_base // 64) * 64]

        def at(name, shape, over=None, dt=F32):
            size = int(np.prod(shape[1:])) * 4
            if over is None:
                place[name] = here[0]
                here[0] += -(-size // 32) * 32
            else:
                place[name] = place[over[0]] + 4 * over[1]
            return nc.alloc_sbuf_tensor_at(name, shape, dt, offset=place[name])

        hb = at("hb", [P, N_IN, T])
        work = at("work", [P, 6, HJ, T])
        hff_hi = at("hff_hi", [P, FT, T], over=("hb", 0), dt=F32R)
        hff_lo = at("hff_lo", [P, FT, T], over=("hb", FT * T), dt=F32R)
        kv = at("kv", [P, NS, PAGES, 256])
        ZT = at("ZT", [P, 2, 1600])
        Z, SPL = ZT[:, 0], ZT[:, 1]
        here[0] += 4 * (SRING * 8 * P - 3200)
        SR = at("SR", [P, NS, 2, DV])
        VBC = at("VBC", [P, NS, 2, DV])
        here[0] += 4 * (2 * KT * T - 2 * NS * 2 * DV)
        w_hi = at("w_hi", [P, SRING, 8, P], over=("kv", 0), dt=F32R)
        w_lo = at("w_lo", [P, SRING, 8, P], over=("ZT", 0), dt=F32R)
        cat_hi = at("cat_hi", [P, KT, T], over=("work", 0), dt=F32R)
        cat_lo = at("cat_lo", [P, KT, T], over=("work", KT * T), dt=F32R)
        x_hi = at("x_hi", [P, KT, T], over=("SR", 0), dt=F32R)
        x_lo = at("x_lo", [P, KT, T], over=("SR", KT * T), dt=F32R)
        BR, BI, P1, P2, P3, P4 = (work[:, i] for i in range(6))
        ring = at("ring", [P, RING, 8, P])
        x = at("x", [P, KT, T])
        z = at("z", [P, KT, T])
        turn = at("turn", [P, 2, HJ, T])
        rg = turn[:, 0]
        tabs = [(turn[:, 0, :, 0:SEQ], turn[:, 1, :, 0:SEQ]), (z[:, 0:HJ, 0:SEQ], z[:, HJ:J, 0:SEQ])]
        RI = at("RI", [P, HEADS, DEC])
        KD = at("KD", [P, 2, 256])
        VT = at("VT", [P, 2, HEADS * DV])
        VBt = at("VBt", [P, 2, 256])
        disc = at("disc", [P, 12, 264], over=("RI", 0))
        sqo = RI[:].rearrange("p a b -> p (a b)")[:, 0:HEADS * T].rearrange("p (a b) -> p a b", b=T)
        s5in = at("s5in", [P, 3, 264])
        s5b = at("s5b", [P, 2, 256])
        bb = at("bb", [P, 2, 256])
        s5c = at("s5c", [P, 2, J, 32])
        s5x0 = at("s5x0", [P, 2, J, NS])
        are, aim, mag, fhi, flo = (at(n, [P, J]) for n in ("are", "aim", "mag", "fhi", "flo"))
        stmp = at("stmp", [P, 4, HJ, NS])
        s5o = at("s5o", [P, 2, J, NS + 1])
        wglu = at("wglu", [P, 2, 256])
        yd = at("yd", [P, 2, T])
        yg = at("yg", [P, 2, T])
        yb = at("yb", [P, 2, T])
        sg = yb
        sq2 = at("sq2", [P, 2, T])
        rs2 = at("rs2", [P, T])
        lnr = at("lnr", [P, T])
        sqt = at("sqt", [P, 3, T])
        acc = at("acc", [P, 2, T])
        rms2 = at("rms2", [P, 2, T], over=("sqt", 0))
        sqa = at("sqa", [P, 2, T], over=("acc", 0))
        qbd = at("qbd", [P, 2, NS, 2])
        eps_all, halfpi = at("eps_all", [P, 2]), at("halfpi", [P, 1])
        eps_t = {LN_EPS: eps_all[:, 0:1], RMS_EPS: eps_all[:, 1:2]}
        VS = at("VS", [NS, HEADS * DV])
        conv = at("conv", [P, CSLOTS, T], over=("yd", 0))
        Oh = at("Oh", [P, HEADS, T])
        RSO = at("RSO", [P, 2, DV])
        qsd = at("qsd", [P, 2, NS, 2])
        qkd = at("qkd", [P, 2, NS, 2])
        prev = at("prev", [P, N_UP, 2, NS])
        spre = at("spre", [P, N_UP, NS])
        cout = at("cout", [P, N_UP, 10])
        vec = at("vec", [P, N_VEC])
        cst = at("cst", [P, len(CONSTS), P])
        dtab = at("dtab", [P, HEADS, SEQ])
        rope = at("rope", [P, 2, T])
        steps = at("steps", [P, SEQ])
        kdec = at("kdec", [P, 2, HEADS])
        gam = at("gam", [P, 2])
        pidx = at("pidx", [1, NS * PAGES], dt=mybir.dt.int32)
        assert here[0] <= nc.sbuf_usable_end, (here[0], nc.sbuf_usable_end)
        C = {n: cst[:, i] for i, n in enumerate(CONSTS)}
        ps = ctx.enter_context(nc.psum_tensor("ps", [P, 8, 512], F32))
        vs_dram = [nc.dram_tensor(f"vs_scratch{l}", [NS, HEADS * DV], F32, kind="Internal").ap()
                   for l in range(DEPTH)]

        def pv(L, name, i=0, n=1):
            c = L * PER_LAYER + COL[name] + i
            return vec[:, c:c + n]

        PER_LN = {"lnc": 1, "lnd": KT, "lnsq": KT, "lnacc1": 1, "lnacc2": 1,  "lnmean": 1, "lnvar": 1, "lnmu2": 1,
                  "lnv": 1, "lnln": 1, "lnr": 1, "xn": KT, "x": KT}

        def needq(eng, name, q, k):
            eng.wait_ge(S(name), q * PER_LN[name] + k)

        class Engine:

            def __init__(self, eng, own):
                self.eng, self.own, self.n, self.last = eng, own, {}, None

            def did(self, ins, name=None):
                name = name or self.own
                ins.then_inc(S(name), 1)
                self.n[name] = self.n.get(name, 0) + 1
                self.last = (name, self.n[name])

            def settle(self):
                if self.last:
                    self.eng.wait_ge(S(self.last[0]), self.last[1])

        def need(eng, name, L, k):
            eng.wait_ge(S(name), L * PERL[name] + k)

        PERL = {"in_evac": N_IN, "z": 16, "bb": 1, "tph": 2, "tab": 4, "cneg": 1, "bu": 16, "buev": 16,
                "poolpre": 2, "scan": 2, "poolpost": 2, "s5x": 2, "s5y": 2, "yd": 2, "gelu": 2,
                "glu": 2, "sig": 2, "ya": 1, "sqa": 1, "rms": 2, "rmsl": 1, "rmsr": 1, "cata": 2,
                "rot": 4, "rotrd": 4, "qk": 1, "trk": 1, "kd": 1, "trv": 2, "vt": 2, "trvb": 1, "vbt": 1,
                "trvs": 1, "vs": 1, "rin": 4, "ri": 4, "rstate": 1, "rso": 1, "srg": 2, "sr": 1, "qs": 3,
                "rsq": 1, "osamp": 1, "ro": 4, "oev": 4, "gmean": 4, "gd": 4, "gsq": 4, "gvar": 4, "gv1": 4, "gr": 4,
                "catc": 4, "qb": 2, "sbz": 4, "zev": 4, "sbzs": 1, "zs": 1, "absz": 1, "spe": 1, "spl": 1,
                "sbs": 4, "zsub": 4, "sbss": 1, "zsubs": 1, "zmin": 1, "wexp": 1, "w": 1, "sby": 2, "ybev": 2,
                "sbys": 1, "ybs": 1, "sqb": 1, "catb": 2,
                "cat_hi": KT, "cat_lo": KT, "up_free": N_UP, "fc": N_UP, "fs": FT, "prod": FT,
                "hff_hi": FT, "hff_lo": FT, "spre": 1,
                "x_hi_act": KT // 2, "x_hi_dve": KT // 2, "x_lo_dve": KT // 2, "x_lo_pool": KT // 2,
                "w_hi": SPLITS, "used": UNITS}

        def by_pool(i):
            return i in (N_IN, N_IN + 1, N_IN + 5, N_IN + 6, PLAIN_UP + 2) or (i >= N_IN + N_OUT + N_UP and i % 2 == 0)

        def wait_low(eng, L, i):
            mine = [u for u in SPLIT if by_pool(u) == by_pool(i)]
            eng.wait_ge(S("w_lo_pool" if by_pool(i) else "w_lo_dve"), L * len(mine) + mine.index(i) + 1)

        def split_slot(i):
            return SPLIT.index(i) % SRING

        cat = [hb[:, U], hb[:, U + 1], hb[:, QB_], hb[:, QB_ + 1]] + [hb[:, GC + h] for h in range(HEADS)]

        def ring_slot(n):
            return n % RING

        block = ctx.enter_context(nc.Block())

        @block.sync
        def _(sp):
            sp.dma_start(s5in[:], A["s5in"][0]).then_inc(S("ld_s5in"), 16)
            sp.dma_start(cst[:, 0:2], A["cst"][:, 0:2]).then_inc(S("ld_means"), 16)
            sp.dma_start(z[:], A["xT"]).then_inc(S("ld_x"), 16)
            sp.dma_start(cst[:, 2:], A["cst"][:, 2:]).then_inc(S("ld_cst"), 16)
            sp.dma_start(s5b[:], A["s5b"][0]).then_inc(S("ld_s5b"), 16)
            sp.dma_start(vec[:], A["vec"]).then_inc(S("ld_vec"), 16)
            sp.dma_start(steps[:], A["steps"]).then_inc(S("ld_steps"), 16)
            sp.dma_start(pidx[:], A["pages"]).then_inc(S("ld_pages"), 16)

            def layer_params(L):
                if L > 0:
                    need(sp, "s5y", L - 1, 2)
                    need(sp, "bb", L - 1, 1)
                    need(sp, "glu", L - 1, 2)
                    need(sp, "bu", L - 1, 16)
                    sp.wait_ge(S("dve_x0"), L * 2)
                    sp.dma_start(s5in[:], A["s5in"][L]).then_inc(S("ld_s5in"), 16)
                    sp.dma_start(s5b[:], A["s5b"][L]).then_inc(S("ld_s5b"), 16)
                sp.dma_start(s5c[:], A["s5c"][L]).then_inc(S("ld_s5c"), 16)
                sp.dma_start(s5x0[:], A["s5x0"][L]).then_inc(S("ld_x0"), 16)
                sp.dma_start(wglu[:], A["wglu"][L]).then_inc(S("ld_wglu"), 16)

            def unit(L, i):
                n = L * UNITS + i
                if n >= RING:
                    former = n - RING
                    if former % UNITS in SPLIT:
                        wait_low(sp, former // UNITS, former % UNITS)
                    else:
                        sp.wait_ge(S("used"), former + 1)
                sp.dma_start(ring[:, ring_slot(n)], A["units"][n]).then_inc(S(f"ld_w{ring_slot(n)}"), 16)

            def pages(L, what, part=0, parts=1):
                n = NS * PAGES // parts
                for s in range(part * n, (part + 1) * n):
                    idx = sp.value_load(pidx[0:1, s:s + 1], min_val=0, max_val=POOL - 1)
                    src = A[what][L][bass.ds(idx, 1)].rearrange("a p c -> p (a c)")
                    sp.dma_start(kv[:, s // PAGES, s % PAGES], src).then_inc(S("ld_kv"), 16)

            layer_params(0)
            for L in range(DEPTH):
                for i in range(4):
                    unit(L, i)
                if L == 0:
                    sp.dma_start(rope[:], A["rope"]).then_inc(S("ld_rope"), 16)
                    sp.dma_start(dtab[:], A["dtab"]).then_inc(S("ld_dtab"), 16)
                    sp.dma_start(kdec[:], A["kdec"]).then_inc(S("ld_kdec"), 16)
                    sp.dma_start(gam[:], A["gam"]).then_inc(S("ld_gam"), 16)
                    sp.wait_ge(S("ld_pages"), 16)
                else:
                    sp.wait_ge(S("used"), UNITS * L)
                    need(sp, "spre", L - 1, 1)
                    sp.wait_ge(S("st_prev"), 16 * L)
                for i in range(4, 13):
                    unit(L, i)
                    if i < 8:
                        pages(L, "kpool", i - 4, 4)
                    if i == 8:
                        sp.dma_start(SR[:], A["sret"][L]).then_inc(S("ld_sr"), 16)
                sp.dma_start(prev[:], A["prev"][L]).then_inc(S("ld_prev"), 16)
                need(sp, "sbzs", L, 1)
                pages(L, "vpool")
                for i in range(13, UNITS):
                    unit(L, i)
                    if i == N_IN + N_OUT + N_UP // 2 and L + 1 < DEPTH:
                        layer_params(L + 1)
            for t in (0, KT // 2):
                needq(sp, "x", 2 * DEPTH, t + KT // 2)
                sp.dma_start(O["y"][:, t:t + KT // 2], x[:, t:t + KT // 2]).then_inc(S("st_y"), 16)
            sp.wait_ge(S("st_y"), 32)

        @block.tensor
        def _(pe):
            E = Engine(pe, "pe_step")
            mm = nc.tensor.matmul
            holder = {}
            freed = []

            def claim(bank, reader, L, k):
                if bank in holder:
                    h = holder[bank]
                    (needq if h[0] in PER_LN else need)(pe, *h)
                holder[bank] = (reader, L, k)
                return ps[:, bank]

            def main_bank(reader, L, k):
                n = len(freed)
                if n >= 4:
                    need(pe, *freed[n - 4])
                freed.append((reader, L, k))
                return ps[:, n % 4, 0:T]

            def unit_ready(n):
                pe.wait_ge(S(f"ld_w{ring_slot(n)}"), 16 * (n // RING + 1))

            def tile8(L, i, out, rhs, ready=None, between=None):
                n = L * UNITS + i
                unit_ready(n)
                for k in range(8):
                    if ready:
                        ready(k)
                    ins = mm(out, ring[:, ring_slot(n), k], rhs(k), start=(k == 0), stop=(k == 7))
                    if k == 7:
                        E.did(ins, "used")
                    if between:
                        between(k)

            def split_product(out, i, b, hi, lo, start, stop):
                wh, wl = w_hi[:, split_slot(i), b], w_lo[:, split_slot(i), b]
                mm(out, wh, hi, start=start, stop=False)
                mm(out, wh, lo, start=False, stop=False)
                return mm(out, wl, hi, start=False, stop=stop)

            def ln_shift(q):
                bank = claim(4, "lnd", q, KT)
                E.did(mm(bank[:, 0:T], C["mean_v"], z[:, 0], start=True, stop=True), "lnc")

            def ln_sums(q):
                b1, b2 = claim(5, "xn", q, KT), claim(6, "lnv", q, 1)
                first = POOL_FROM[q > 0]
                for t in range(first):
                    needq(pe, "lnsq", q, t + 1)
                    E.did(mm(b2[:, 0:T], C["mean_d"], sqt[:, t % 3], start=(t == 0), stop=False), "lnsq_pe")
                needq(pe, "lnacc1", q, 1)
                mm(b1[:, 0:T], C["mean_d"], acc[:, 0], start=True, stop=False)
                needq(pe, "lnacc2", q, 1)
                mm(b2[:, 0:T], C["mean_d"], acc[:, 1], start=(first == 0), stop=False)
                needq(pe, "lnd", q, KT)
                E.did(mm(b1[:, 0:T], C["mean_d"], z[:, KT - 1], start=False, stop=True), "lnmean")
                needq(pe, "lnsq", q, KT)
                E.did(mm(b2[:, 0:T], C["mean_d"], sqt[:, (KT - 1) % 3], start=False, stop=True), "lnvar")

            def s5_b(L, hf):
                if hf == 0:
                    need(pe, "bb", L, 1)
                for jj in range(HJ):
                    for c in range(2):
                        k = 8 * hf + 2 * jj + c + 1
                        bank = claim(4 + 2 * (jj % 2) + c, "buev", L, k)
                        E.did(mm(bank[:, 0:T], bb[32 * jj:32 * jj + 32, c, hf * P:(hf + 1) * P],
                                 hb[32 * jj:32 * jj + 32, U + hf], start=True, stop=True), "bu")

            def s5_c(L, hf):
                need(pe, "s5x", L, hf + 1)
                if hf == 0:
                    need(pe, "cneg", L, 1)
                bank = claim(7, "yd", L, hf + 1)
                for jj in range(HJ):
                    o = bank[32 * jj:32 * jj + 32, 0:T]
                    j = hf * HJ + jj
                    mm(o, s5c[:, 0, j], P1[:, jj], start=True, stop=False, tile_position=(0, 32 * jj))
                    ins = mm(o, s5c[:, 1, j], P3[:, jj], start=False, stop=True, tile_position=(0, 32 * jj))
                E.did(ins, "s5y")

            def s5_glu(L):
                need(pe, "gelu", L, 2)
                pe.wait_ge(S("ld_wglu"), 16 * (L + 1))
                for m in range(2):
                    bank = claim(5 + m, "sig", L, m + 1)
                    for k in range(2):
                        ins = mm(bank[:, 0:T], wglu[:, k, m * P:(m + 1) * P], yg[:, k],
                                 start=(k == 0), stop=(k == 1))
                    E.did(ins, "glu")

            def rms(L, sq, wait, reader, name, b):
                need(pe, wait, L, 1)
                bank = claim(b, reader, L, 1)
                for k in range(2):
                    ins = mm(bank[:, 0:T], C["mean_w"], sq[:, k], start=(k == 0), stop=(k == 1))
                E.did(ins, name)

            def rotate(L):
                for i in range(4):
                    need(pe, "in_evac", L, QC + i + 1)
                    bank = claim(ROT_BANK[i], "rotrd", L, i + 1)
                    E.did(mm(bank[:, 0:T], C["perm"], hb[:, QC + i], start=True, stop=True), "rot")

            def transposes(L):
                need(pe, "in_evac", L, VC + 4)
                for tt in range(2):
                    bank = claim(4 + tt, "vt", L, tt + 1)
                    for h in range(HEADS):
                        ins = nc.tensor.transpose(bank[:, h * P:(h + 1) * P],
                                                  hb[:, VC + h, tt * P:(tt + 1) * P], C["ident"])
                    E.did(ins, "trv")
                bank = claim(6, "vs", L, 1)
                for h in range(HEADS):
                    ins = nc.tensor.transpose(bank[0:NS, h * P:(h + 1) * P], hb[:, VC + h, SEQ:T], C["ident"])
                E.did(ins, "trvs")

            def k_transposes(L):
                need(pe, "qk", L, 1)
                bank = claim(4, "kd", L, 1)
                for tt in range(2):
                    for ht in range(2):
                        ins = nc.tensor.transpose(bank[:, tt * 256 + ht * P:tt * 256 + (ht + 1) * P],
                                                  hb[:, KC + ht, tt * P:(tt + 1) * P], C["ident"])
                E.did(ins, "trk")

            def causal(bank, h, k0, q0):
                r = slice(64 * (h % 2), 64 * (h % 2) + 64)
                kk, qq = hb[r, k0 + h // 2], hb[r, q0 + h // 2]
                mm(bank[:, 0:SEQ], kk[:, 0:P], qq[:, 0:SEQ], start=True, stop=True)
                return mm(bank[:, SEQ:DEC], kk[:, P:SEQ], qq[:, P:SEQ], start=True, stop=True)

            def ret_inner(L):
                for h in range(HEADS):
                    bank = claim(4 + h, "ri", L, h + 1)
                    E.did(causal(bank, h, KC, QC), "rin")

            def ret_state(L):
                need(pe, "kd", L, 1)
                need(pe, "vt", L, 2)
                bank = claim(7, "rso", L, 1)
                for h in range(HEADS):
                    o = bank[64 * (h % 2):64 * (h % 2) + 64, (h // 2) * DV:(h // 2 + 1) * DV]
                    for tt in range(2):
                        ins = mm(o, KD[:, tt, 64 * h:64 * h + 64], VT[:, tt, h * DV:(h + 1) * DV],
                                 start=(tt == 0), stop=(tt == 1))
                E.did(ins, "rstate")

            def ret_samples(L, part):
                if part == 0:
                    need(pe, "srg", L, 2)
                    need(pe, "qs", L, 3)
                    claim(7, "osamp", L, 1)
                    mm(ps[:, 7, 32:64], C["ones"], qkd[:].rearrange("p a b c -> p (a b c)"), start=True, stop=True)
                for n in (2 * part, 2 * part + 1):
                    ht, b = n // NS, n % NS
                    ins = mm(ps[:, 7, 2 * n:2 * n + 2], SR[:, b, ht], qsd[:, ht, b], start=True, stop=True)
                if part == 7:
                    E.did(ins, "rsq")

            def ret_out(L):
                need(pe, "vt", L, 2)
                for h in range(HEADS):
                    need(pe, "ri", L, h + 1)
                    bank = claim(OUT_BANK[h], "oev", L, h + 1)
                    mm(bank[:, 0:SEQ], VT[:, 0, h * DV:(h + 1) * DV], RI[:, h, 0:SEQ], start=True, stop=False)
                    E.did(mm(bank[:, P:SEQ], VT[:, 1, h * DV:(h + 1) * DV], RI[:, h, SEQ:DEC], start=False, stop=True),
                          "ro")

            def group_norm(L):
                need(pe, "osamp", L, 1)
                for h in range(HEADS):
                    need(pe, "oev", L, h + 1)
                    bank = claim(GN_BANK[h], "gd", L, h + 1)
                    E.did(mm(bank[:, 0:T], C["mean_v"], Oh[:, h], start=True, stop=True), "gmean")
                for h in range(HEADS):
                    need(pe, "gsq", L, h + 1)
                    bank = claim(GN_BANK[h], "gv1", L, h + 1)
                    E.did(mm(bank[:, 0:T], C["mean_v"], sqo[:, h], start=True, stop=True), "gvar")

            def vb_transposes(L):
                need(pe, "in_evac", L, VB_ + 2)
                bank = claim(5, "vbt", L, 1)
                for tt in range(2):
                    for ht in range(2):
                        ins = nc.tensor.transpose(bank[:, tt * 256 + ht * P:tt * 256 + (ht + 1) * P],
                                                  hb[:, VB_ + ht, tt * P:(tt + 1) * P], C["ident"])
                E.did(ins, "trvb")

            def sb_scores(L, heads):
                need(pe, "in_evac", L, KB + 2)
                for h in heads:
                    bank = claim(SB_BANK[h], "zev", L, h + 1)
                    E.did(causal(bank, h, KB, QB_), "sbz")

            def sb_sample_scores(L, part):
                if part == 0:
                    need(pe, "qb", L, 2)
                    pe.wait_ge(S("ld_kv"), 16 * NS * PAGES * (2 * L + 1))
                    claim(4, "zs", L, 1)
                pg, b = part // NS, part % NS
                for ht in range(2):
                    c = 32 * pg + 4 * b + 2 * ht
                    ins = mm(ps[:, 4, c:c + 2], kv[:, b, pg, ht * P:(ht + 1) * P], qbd[:, ht, b],
                             start=True, stop=True)
                if part == 15:
                    E.did(ins, "sbzs")

            def sb_tails(L):
                need(pe, "spl", L, 1)
                for h in range(HEADS):
                    bank = claim(4 + h, "zsub", L, h + 1)
                    s0, s1 = SPL[:, h * DEC:h * DEC + SEQ], SPL[:, h * DEC + SEQ:(h + 1) * DEC]
                    mm(bank[:, 0:SEQ], C["tri"], s0, start=True, stop=False)
                    mm(bank[:, P:SEQ], C["ones"], s1, start=False, stop=True)
                    E.did(mm(bank[:, SEQ:DEC], C["tri"], s1, start=True, stop=True), "sbs")
                bank = claim(4, "zsubs", L, 1)
                s0, s1 = SPL[:, 4 * DEC:4 * DEC + 32], SPL[:, 4 * DEC + 32:4 * DEC + 64]
                mm(bank[:, 0:32], C["tri"], s0, start=True, stop=False)
                mm(bank[:, 0:32], C["ones"], s1, start=False, stop=True)
                E.did(mm(bank[:, 32:64], C["tri"], s1, start=True, stop=True), "sbss")

            def sb_values(L):
                need(pe, "w", L, 1)
                need(pe, "vbt", L, 1)
                for ht in range(2):
                    bank = claim(6 + ht, "ybev", L, ht + 1)
                    for h in (2 * ht, 2 * ht + 1):
                        r = 64 * (h % 2)
                        o = bank[r:r + 64]
                        w0, w1 = Z[:, h * DEC:h * DEC + SEQ], Z[:, h * DEC + SEQ:(h + 1) * DEC]
                        mm(o[:, 0:SEQ], VBt[:, 0, 64 * h:64 * h + 64], w0, start=True, stop=False,
                           tile_position=(0, r))
                        ins = mm(o[:, P:SEQ], VBt[:, 1, 64 * h:64 * h + 64], w1, start=False, stop=True,
                                 tile_position=(0, r))
                    E.did(ins, "sby")

            def sb_sample_values(L, part):
                if part == 0:
                    need(pe, "w", L, 1)
                    pe.wait_ge(S("ld_kv"), 16 * NS * PAGES * (2 * L + 2))
                    claim(4, "ybs", L, 1)
                ht, b = part // NS, part % NS
                for pg in range(PAGES):
                    wc = 4 * DEC + 32 * pg + 4 * b + 2 * ht
                    oc = 16 * ht + 2 * b
                    ins = mm(ps[:, 4, oc:oc + 2], kv[:, b, pg, ht * P:(ht + 1) * P], Z[:, wc:wc + 2],
                             start=(pg == 0), stop=(pg == 1))
                if part == 15:
                    E.did(ins, "sbys")

            pe.wait_ge(S("ld_x"), 16)
            pe.wait_ge(S("ld_means"), 16)
            ln_shift(0)
            ln_sums(0)
            for L in range(DEPTH):
                for i in range(N_IN):
                    out = main_bank("in_evac", L, i + 1)
                    small, first = {5: (sb_sample_scores, 0), 6: (sb_sample_scores, 8), 16: (ret_samples, 0),
                                    18: (sb_sample_values, 0),
                                    19: (sb_sample_values, 8)}.get(i, (None, 0))
                    tile8(L, i, out, lambda k: x[:, k], (lambda k: needq(pe, "x", 2 * L, k + 1)) if i == 0 else None,
                          (lambda k: small(L, first + k)) if small else None)
                    if i == B0_AT[L]:
                        need(pe, "in_evac", L, 2)
                        s5_b(L, 0)
                    if i == 6:
                        sb_scores(L, (0, 1, 2))
                    if i == 8:
                        if L == 0:
                            pe.wait_ge(S("ld_cst"), 16)
                        sb_scores(L, (3,))
                        vb_transposes(L)
                    if i == 9:
                        s5_c(L, 0)
                        s5_b(L, 1)
                    if i == 13:
                        s5_c(L, 1)
                        rotate(L)
                    if i == 14:
                        sb_tails(L)
                    if i == 15:
                        s5_glu(L)
                        k_transposes(L)
                    if i == 16:
                        transposes(L)
                    if i == 17:
                        ret_inner(L)
                    if i == 18:
                        sb_values(L)
                ret_out(L)
                rms(L, sqa, "sqa", "rmsl", "rms", 5)
                rms(L, sq2, "sqb", "rmsl", "rms", 6)
                group_norm(L)
                outs = [main_bank("z", L, i + 1) for i in range(3)]
                for k in range(KT):
                    for i in range(3):
                        if k == 0:
                            wait_low(pe, L, N_IN + i)
                        need(pe, "cat_lo", L, k + 1)
                        ins = split_product(outs[i], N_IN + i, k, cat_hi[:, k], cat_lo[:, k], k == 0, k == KT - 1)
                        if k == KT - 1:
                            E.did(ins, "used")
                for i in range(3, N_OUT):
                    out = main_bank("z", L, i + 1)
                    wait_low(pe, L, N_IN + i)
                    for k in range(KT):
                        ins = split_product(out, N_IN + i, k, cat_hi[:, k], cat_lo[:, k], k == 0, k == KT - 1)
                    E.did(ins, "used")
                    if i == 3:
                        need(pe, "z", L, 1)
                        ln_shift(2 * L + 1)
                ln_sums(2 * L + 1)
                ret_state(L)
                for i in range(N_UP):
                    out, u = main_bank("up_free", L, i + 1), N_IN + N_OUT + i
                    if u == PLAIN_UP:
                        tile8(L, u, out, lambda k: x[:, k], lambda k: needq(pe, "x", 2 * L + 1, k + 1))
                        continue
                    wait_low(pe, L, u)
                    for k in range(KT):
                        if u == PLAIN_UP + 1:
                            need(pe, "x_lo_dve" if k % 2 else "x_lo_pool", L, k // 2 + 1)
                        ins = split_product(out, u, k, x_hi[:, k], x_lo[:, k], k == 0, k == KT - 1)
                    E.did(ins, "used")
                for m in range(KT):
                    out = main_bank("z", L, 8 + m + 1)
                    for k in range(FT):
                        blk = m * FT + k
                        u = N_IN + N_OUT + N_UP + blk // 8
                        if blk % 8 == 0:
                            wait_low(pe, L, u)
                        if m == 0:
                            need(pe, "hff_lo", L, k + 1)
                        ins = split_product(out, u, blk % 8, hff_hi[:, k], hff_lo[:, k], k == 0, k == FT - 1)
                        if blk % 8 == 7:
                            E.did(ins, "used")
                        elif k == FT - 1:
                            E.did(ins, "down")
                    if m == 2:
                        need(pe, "z", L, 9)
                        ln_shift(2 * L + 2)
                ln_sums(2 * L + 2)

        def tile_done(eng, L, i):
            eng.wait_ge(S("used"), L * UNITS + i + 1)

        def down_done(eng, L, m):
            last = (m + 1) * FT - 1
            if last % 8 == 7:
                eng.wait_ge(S("used"), L * UNITS + N_IN + N_OUT + N_UP + last // 8 + 1)
            else:
                ends = [q for q in range(KT) if ((q + 1) * FT) % 8 != 0]
                eng.wait_ge(S("down"), L * len(ends) + ends.index(m) + 1)

        def branch_done(L, k):
            return [("cata", L, k + 1), ("catb", L, k - 1), ("catc", L, k - 3)][min(k // 2, 2)]

        def bcast(ap, shape, axis):
            return ap.unsqueeze(axis).to_broadcast(shape)

        @block.scalar
        def _(act):
            E = Engine(act, "act_step")
            f = nc.scalar.activation

            def inv_sqrt(dst, src, eps, first, last):
                E.did(f(dst, src, ACT.Ln, bias=eps_t[eps]), first)
                E.settle()
                E.did(f(dst, dst, ACT.Exp, scale=-0.5), last)

            def split_hi(L, i):
                n = L * UNITS + i
                act.wait_ge(S(f"ld_w{ring_slot(n)}"), 16 * (n // RING + 1))
                if SPLIT.index(i) < SRING:
                    need(act, "sbys", L, 1)
                else:
                    former = SPLIT[SPLIT.index(i) - SRING]
                    act.wait_ge(S("used"), L * UNITS + former + 1)
                E.did(nc.scalar.copy(w_hi[:, split_slot(i)], ring[:, ring_slot(n)]), "w_hi")

            def logs():
                nc.scalar.preload_act_table_set("natural_log_exp_and_others")

            def ln(q):
                logs()
                if q > 0:
                    needq(act, "xn", q - 1, KT)
                for t in range(KT):
                    if q % 2 == 1 and t == 2:
                        split_hi((q - 1) // 2, N_IN + 7)
                    if q % 2 == 1 and t in (5, 6):
                        split_hi((q - 1) // 2, PLAIN_UP + t - 4)
                    needq(act, "lnd", q, t + 1)
                    first = POOL_FROM[q > 0]
                    if t >= 3 and t - 3 < first:
                        act.wait_ge(S("lnsq_pe"), t - 2)
                    elif t >= 3:
                        done_before = q * (KT - 3) - (POOL_FROM[0] if q else 0)
                        act.wait_ge(S("pool_ln"), done_before + max(t - 3 - first, 1))
                    E.did(f(sqt[:, t % 3], z[:, t], ACT.Square), "lnsq")
                needq(act, "lnmean", q, 1)
                E.did(f(rs2[:], ps[:, 5, 0:T], ACT.Square), "lnmu2")
                needq(act, "lnv", q, 1)
                E.did(f(lnr[:], lnr[:], ACT.Ln, bias=eps_t[LN_EPS]))
                E.settle()
                E.did(f(lnr[:], lnr[:], ACT.Exp, scale=-0.5), "lnr")
                if q == 0:
                    act.wait_ge(S("ld_vec"), 16)
                    g, b = vec[:, 0:8], vec[:, 8:16]
                else:
                    L, k = (q - 1) // 2, (q - 1) % 2 + 1
                    g, b = pv(L, f"ln{k}_g", 0, 8), pv(L, f"ln{k}_b", 0, 8)
                for t in range(KT):
                    needq(act, "xn", q, t + 1)
                    E.did(f(x[:, t], z[:, t], ACT.Identity, scale=g[:, t:t + 1], bias=b[:, t:t + 1]), "x")
                if q % 2 == 1:
                    act.wait_ge(S("st_sr"), 16 * (L + 1))
                    E.settle()
                    for t in range(1, KT, 2):
                        E.did(nc.scalar.copy(x_hi[:, t], x[:, t]), "x_hi_act")

            def s5_params(L, part):
                act.wait_ge(S("ld_s5in"), 16 * (L + 1))
                if part == 0:
                    act.wait_ge(S("v_s5clear"), L + 1)
                    E.did(f(disc[:, 0], s5in[:, 2], ACT.Exp), "a_dt")
                if part == 1:
                    act.wait_ge(S("v_ldt"), L + 1)
                    E.did(f(disc[:, 2], disc[:, 1], ACT.Exp), "a_mag")
                if part == 2:
                    act.wait_ge(S("v_red"), L + 1)
                    f(disc[:, 5], disc[:, 4], ACT.Sin)
                    E.did(f(disc[:, 6], disc[:, 7], ACT.Sin, bias=halfpi[:], scale=-1.0), "a_sc")

            def s5_tables(L, hf):
                need(act, "tph", L, hf + 1)
                TC, TS = tabs[hf]
                E.did(f(TS, TS, ACT.Sin, scale=TWO_PI_IN), "tab")
                E.did(f(TC, TC, ACT.Sin, bias=halfpi[:], scale=-TWO_PI_IN), "tab")

            def neg_c(L):
                act.wait_ge(S("ld_s5c"), 16 * (L + 1))
                E.did(nc.scalar.mul(s5c[:, 1], s5c[:, 1], -1.0), "cneg")

            def s5_evac(L, hf):
                for k in range(8):
                    need(act, "bu", L, 8 * hf + k + 1)
                    if k == 0 and hf == 1:
                        need(act, "s5x", L, 1)
                    E.did(nc.scalar.copy((BR, BI)[k % 2][:, k // 2], ps[:, 4 + k % 4, 0:T]), "buev")

            def v_tokens(L):
                for tt in range(2):
                    need(act, "trv", L, tt + 1)
                    E.did(nc.scalar.copy(VT[:, tt], ps[:, 4 + tt]), "vt")
                need(act, "trvs", L, 1)
                E.did(nc.scalar.copy(VS[:], ps[0:NS, 6]), "vs")
                E.settle()
                act.dma_start(vs_dram[L], VS[:]).then_inc(S("st_vs"), 16)

            def v_spread(L):
                act.wait_ge(S("st_vs"), 16 * (L + 1))
                v5 = vs_dram[L].rearrange("b (a c e) -> c b a e", a=2, c=2)
                for c in range(2):
                    act.dma_start(VBC[64 * c:64 * c + 64], v5[c:c + 1].to_broadcast([64, NS, 2, DV])
                                  ).then_inc(S("ld_vbc"), 16)

            def branch_hi(L, k):
                need(act, *branch_done(L, k))
                E.did(nc.scalar.copy(cat_hi[:, k], cat[k]), "cat_hi")

            def gate(L, p):
                need(act, "up_free", L, 2 * p + 2)
                c = conv[:, (2 * p + 1) % CSLOTS]
                E.did(f(c, c, ACT.Silu), "fs")

            def hidden_hi(L, p):
                need(act, "prod", L, p + 1)
                if p == 0:
                    act.wait_ge(S("st_kv"), 16 * (L + 1))
                E.did(nc.scalar.copy(hff_hi[:, p], conv[:, (2 * p + 1) % CSLOTS]), "hff_hi")

            act.wait_ge(S("eps_set"), 4)
            s5_params(0, 0)
            s5_params(0, 1)
            ln(0)
            s5_params(0, 2)
            for L in range(DEPTH):
                for i in range(N_IN):
                    tile_done(act, L, i)
                    if L > 0 and i == 0:
                        act.wait_ge(S("st_kv"), 16 * L)
                    tile = ps[:, (L * TILES + i) % 4, 0:T]
                    E.did(f(hb[:, i], tile, ACT.Silu) if i >= GC else nc.scalar.copy(hb[:, i], tile), "in_evac")
                    if i == 3:
                        E.settle()
                        for c in range(2):
                            r = slice(64 * c, 64 * c + 64)
                            E.did(nc.scalar.copy(qbd[r, :, :, c], hb[r, QB_:QB_ + 2, SEQ:T]), "qb")
                    if i == B0_AT[L]:
                        s5_evac(L, 0)
                        neg_c(L)
                    if i == TAB0_AT and L == 0:
                        s5_tables(0, 0)
                    if i == TAB1_AT[L]:
                        s5_tables(L, 1)
                    if i == 8:
                        need(act, "trvb", L, 1)
                        E.did(nc.scalar.copy(VBt[:], ps[:, 5].rearrange("p (a b) -> p a b", a=2)), "vbt")
                        E.settle()
                        act.dma_start(O["kv"][L], hb[:, KB:KB + 4]).then_inc(S("st_kv"), 16)
                    if i == 9:
                        s5_evac(L, 1)
                        logs()
                        need(act, "absz", L, 1)
                        E.did(f(SPL[:], SPL[:], ACT.Exp, scale=-1.0))
                        E.settle()
                        E.did(f(SPL[:], SPL[:], ACT.Ln, bias=1.0), "spe")
                    if i == 10:
                        need(act, "yd", L, 1)
                        E.did(f(yg[:, 0], yd[:, 0], ACT.Gelu_apprx_tanh), "gelu")
                        act.wait_ge(S("ld_sr"), 16 * (L + 1))
                        act.wait_ge(S("ld_gam"), 16)
                        for ht in range(2):
                            E.did(nc.scalar.mul(SR[:, :, ht], SR[:, :, ht], gam[:, ht:ht + 1]), "srg")
                    if i == 14:
                        need(act, "yd", L, 2)
                        E.did(f(yg[:, 1], yd[:, 1], ACT.Gelu_apprx_tanh), "gelu")
                    if i == 15:
                        logs()
                        need(act, "zmin", L, 1)
                        E.did(f(Z[:], Z[:], ACT.Exp), "wexp")
                        for m in range(2):
                            need(act, "glu", L, m + 1)
                            E.did(f(sg[:, m], ps[:, 5 + m, 0:T], ACT.Sigmoid), "sig")
                    if i == 16:
                        v_tokens(L)
                    if i == 17:
                        v_spread(L)
                        need(act, "ya", L, 1)
                        E.did(f(sqa[:], yg[:], ACT.Square), "sqa")
                logs()
                split_hi(L, N_IN)
                for h in range(HEADS):
                    need(act, "ro", L, h + 1)
                    E.did(nc.scalar.copy(Oh[:, h, 0:SEQ], ps[:, OUT_BANK[h], 0:SEQ]), "oev")
                need(act, "ybev", L, 2)
                need(act, "ybs", L, 1)
                E.did(f(sq2[:], yb[:], ACT.Square), "sqb")
                split_hi(L, N_IN + 1)
                need(act, "rms", L, 2)
                E.did(f(rms2[:], ps[:, 5:7, 0:T], ACT.Ln, bias=eps_t[RMS_EPS]), "rmsl")
                E.settle()
                E.did(f(rms2[:], rms2[:], ACT.Exp, scale=-0.5), "rmsr")
                split_hi(L, N_IN + 2)
                for h in range(HEADS):
                    need(act, "gd", L, h + 1)
                    E.did(f(sqo[:, h], Oh[:, h], ACT.Square), "gsq")
                for k in range(4):
                    branch_hi(L, k)
                for h in range(HEADS):
                    need(act, "gvar", L, h + 1)
                    inv_sqrt(rg[:, h], ps[:, GN_BANK[h], 0:T], LN_EPS, "gv1", "gr")
                for k in range(4, KT):
                    branch_hi(L, k)
                split_hi(L, N_IN + 3)
                for u in (N_IN + 4, N_IN + 5, N_IN + 6):
                    split_hi(L, u)
                ln(2 * L + 1)
                need(act, "rstate", L, 1)
                if L > 0:
                    act.wait_ge(S("st_rso"), 16 * L)
                E.did(nc.scalar.copy(RSO[:], ps[:, 7, 0:2 * DV].rearrange("p (a b) -> p a b", a=2)), "rso")
                E.settle()
                act.dma_start(O["rprompt"][L], RSO[:]).then_inc(S("st_rso"), 16)
                split_hi(L, PLAIN_UP + 3)
                for i in range(N_UP):
                    tile_done(act, L, N_IN + N_OUT + i)
                    if i == 0:
                        act.wait_ge(S("ld_vec"), 16)
                    if i >= CSLOTS:
                        need(act, "hff_lo", L, (i - CSLOTS) // 2 + 1)
                    elif L > 0:
                        need(act, "hff_lo", L - 1, FT)
                    E.did(f(conv[:, i % CSLOTS], ps[:, (L * TILES + N_IN + N_OUT + i) % 4, 0:T], ACT.Identity,
                            scale=pv(L, "cw2", i), bias=pv(L, "cb", i)), "fc")
                    if i % 2 == 0 and i >= 2:
                        gate(L, i // 2 - 1)
                    split_hi(L, N_IN + N_OUT + i + 4)
                    if i % 2 == 1 and i >= 3:
                        hidden_hi(L, i // 2 - 1)
                gate(L, FT - 1)
                hidden_hi(L, FT - 1)
                for d in range(4, N_DOWN):
                    split_hi(L, N_IN + N_OUT + N_UP + d)
                    if L + 1 < DEPTH:
                        if d in S5_ACT:
                            s5_params(L + 1, S5_ACT.index(d))
                        if d == N_DOWN - 1:
                            s5_tables(L + 1, 0)
                ln(2 * L + 2)
            for name in ("st_kv", "st_rso", "st_sr", "st_vs"):
                act.wait_ge(S(name), 16 * DEPTH)

        @block.vector
        def _(dve):
            E = Engine(dve, "dve_step")
            tt, ts, stt = nc.vector.tensor_tensor, nc.vector.tensor_scalar, nc.vector.scalar_tensor_tensor
            cp = nc.vector.tensor_copy

            E.did(nc.vector.memset(eps_all[:, 0:1], LN_EPS), "eps_set")
            E.did(nc.vector.memset(eps_all[:, 1:2], RMS_EPS), "eps_set")
            E.did(nc.vector.memset(halfpi[:], math.pi / 2), "eps_set")
            E.did(nc.vector.memset(qsd[:], 0.0))
            E.did(nc.vector.memset(qbd[:], 0.0), "eps_set")
            E.settle()

            def seq(*makers):
                for m in makers:
                    E.settle()
                    E.did(m())

            def ln_diff(q, t, ahead=False):
                if not ahead:
                    E.settle()
                before = E.last
                E.did(tt(z[:, t], z[:, t], ps[:, 4, 0:T], ALU.subtract), "lnd")
                if ahead:
                    t -= 1
                    if 0 < t < KT - 1:
                        dve.wait_ge(S(before[0]), before[1])
                if 0 < t < KT - 1:
                    if not ahead:
                        E.settle()
                    E.did(tt(acc[:, 0], z[:, 0] if t == 1 else acc[:, 0], z[:, t], ALU.add),
                          "lnacc1" if t == KT - 2 else None)

            def ln_tail(q):
                needq(dve, "lnmu2", q, 1)
                needq(dve, "lnsq", q, 4)

                def center(t0, t1):
                    mean = bcast(ps[:, 5, 0:T], [P, t1 - t0, T], 1)
                    E.did(tt(z[:, t0:t1], z[:, t0:t1], mean, ALU.subtract))

                E.settle()
                center(0, 2)
                needq(dve, "lnvar", q, 1)
                E.did(tt(lnr[:], ps[:, 6, 0:T], rs2[:], ALU.subtract), "lnv")
                needq(dve, "lnsq", q, KT)
                center(2, 5)
                needq(dve, "lnr", q, 1)
                E.settle()
                for t in range(5):
                    E.did(tt(z[:, t], z[:, t], lnr[:], ALU.mult), "xn")
                center(5, KT)
                E.settle()
                for t in range(5, KT):
                    E.did(tt(z[:, t], z[:, t], lnr[:], ALU.mult), "xn")

            def split_lo(L, i):
                need(dve, "w_hi", L, SPLIT.index(i) + 1)
                slot = split_slot(i)
                E.did(tt(w_lo[:, slot], ring[:, ring_slot(L * UNITS + i)], w_hi[:, slot].bitcast(F32), ALU.subtract),
                      "w_lo_dve")

            def gated(L, p):
                need(dve, "fs", L, p + 1)
                c = conv[:, (2 * p + 1) % CSLOTS]
                E.did(tt(c, conv[:, 2 * p % CSLOTS], c, ALU.mult), "prod")

            lr, li = s5in[:, 0], s5in[:, 1]
            dt, ldr, mg, n, r, sn, cs, ab, den, t0, t1, t2 = (disc[:, i] for i in range(12))

            def s5_rates(L):
                dve.wait_ge(S("ld_s5in"), 16 * (L + 1))
                E.did(ts(lr, lr, -1e-4, None, ALU.min), "v_s5clear")
                dve.wait_ge(S("a_dt"), L + 1)
                E.settle()
                E.did(tt(ldr, lr, dt, ALU.mult), "v_ldt")
                seq(lambda: tt(t0, li, dt, ALU.mult))

            def s5_angle(L):
                seq(lambda: ts(n, t0, 1.0 / TWO_PI, ROUND, ALU.mult, ALU.add),
                    lambda: ts(n, n, -ROUND, None, ALU.add),
                    lambda: stt(r, n, -TWO_PI_HI, t0, ALU.mult, ALU.add))

            def s5_angle2(L):
                seq(lambda: stt(r, n, -TWO_PI_LO, r, ALU.mult, ALU.add),
                    lambda: ts(r, r, PI_SAFE, -PI_SAFE, ALU.min, ALU.max))
                E.settle()
                E.did(stt(ab, r, -1.0, r, ALU.mult, ALU.max), "v_red")

            def s5_turns(L):
                seq(lambda: ts(fhi[:], r[:, 0:J], 1.0 / TWO_PI, ROUND_15, ALU.mult, ALU.add),
                    lambda: ts(fhi[:], fhi[:], -ROUND_15, None, ALU.add),
                    lambda: ts(t1[:, 0:J], r[:, 0:J], 1.0 / TWO_PI, None, ALU.mult),
                    lambda: tt(flo[:], t1[:, 0:J], fhi[:], ALU.subtract))

            def s5_den(L):
                seq(lambda: tt(den, lr, lr, ALU.mult),
                    lambda: tt(t1, li, li, ALU.mult),
                    lambda: tt(den, den, t1, ALU.add),
                    lambda: nc.vector.reciprocal(den, den))

            def s5_a(L):
                dve.wait_ge(S("a_sc"), L + 1)
                dve.wait_ge(S("a_mag"), L + 1)
                seq(lambda: cp(mag[:], mg[:, 0:J]),
                    lambda: tt(t0, mg, cs, ALU.mult),
                    lambda: tt(sn, mg, sn, ALU.mult),
                    lambda: cp(are[:], t0[:, 0:J]),
                    lambda: cp(aim[:], sn[:, 0:J]),
                    lambda: ts(t0, t0, -1.0, None, ALU.add))

            def s5_f_re(L):
                seq(lambda: tt(t1, t0, lr, ALU.mult),
                    lambda: tt(t2, sn, li, ALU.mult),
                    lambda: tt(t1, t1, t2, ALU.add),
                    lambda: tt(t1, t1, den, ALU.mult))

            def s5_f_im(L):
                seq(lambda: tt(sn, sn, lr, ALU.mult),
                    lambda: tt(t0, t0, li, ALU.mult),
                    lambda: tt(t0, sn, t0, ALU.subtract),
                    lambda: tt(t0, t0, den, ALU.mult))

            def s5_bb(L):
                dve.wait_ge(S("ld_s5b"), 16 * (L + 1))
                fr, fi = t1[:, J:264], t0[:, J:264]
                seq(lambda: tt(bb[:, 0], fr, s5b[:, 0], ALU.mult),
                    lambda: tt(t2[:, 0:256], fi, s5b[:, 1], ALU.mult),
                    lambda: tt(bb[:, 0], bb[:, 0], t2[:, 0:256], ALU.subtract),
                    lambda: tt(bb[:, 1], fr, s5b[:, 1], ALU.mult),
                    lambda: tt(t2[:, 0:256], fi, s5b[:, 0], ALU.mult))
                E.settle()
                E.did(tt(bb[:, 1], bb[:, 1], t2[:, 0:256], ALU.add), "bb")

            def s5_phases(L, hf, part=None):
                if L == 0 and hf == 0:
                    dve.wait_ge(S("ld_steps"), 16)
                if hf == 1:
                    needq(dve, "x", 2 * L, KT)
                q, p = tabs[hf]
                st = bcast(steps[:], [P, HJ, SEQ], 1)
                fh = bcast(fhi[:, hf * HJ:(hf + 1) * HJ], [P, HJ, SEQ], 2)
                fl = bcast(flo[:, hf * HJ:(hf + 1) * HJ], [P, HJ, SEQ], 2)
                if part in (0, None):
                    seq(lambda: tt(p, st, fh, ALU.mult),
                        lambda: ts(q, p, ROUND, -ROUND, ALU.add, ALU.add))
                if part in (1, None):
                    seq(lambda: tt(p, p, q, ALU.subtract),
                        lambda: tt(q, st, fl, ALU.mult))
                if part in (2, None):
                    seq(lambda: tt(p, p, q, ALU.add),
                        lambda: ts(q, p, ROUND, -ROUND, ALU.add, ALU.add))
                if part in (3, None):
                    seq(lambda: tt(p, p, q, ALU.subtract))
                    E.settle()
                    E.did(stt(q, p, -1.0, p, ALU.mult, ALU.max), "tph")

            S5_PARTS = (s5_rates, s5_angle, s5_angle2, s5_turns, s5_den, s5_a, s5_f_re, s5_f_im, s5_bb)

            def s5_half(L, hf):
                tm = slice(0, SEQ)
                TC, TS = tabs[hf]
                need(dve, "buev", L, 8 * hf + 8)
                need(dve, "tab", L, 2 * hf + 2)
                if hf == 1:
                    need(dve, "s5y", L, 1)
                E.did(tt(P1[:, :, tm], TC, BR[:, :, tm], ALU.mult))
                E.did(tt(P2[:, :, tm], TS, BI[:, :, tm], ALU.mult))
                E.settle()
                E.did(tt(P1[:, :, tm], P1[:, :, tm], P2[:, :, tm], ALU.add))
                need(dve, "poolpre", L, hf + 1)
                E.did(tt(P3[:, :, tm], P3[:, :, tm], P4[:, :, tm], ALU.subtract))
                E.settle()
                for jj in range(HJ):
                    m = mag[:, hf * HJ + jj:hf * HJ + jj + 1].to_broadcast([P, SEQ])
                    E.did(nc.vector.tensor_tensor_scan(BR[:, jj, tm], m, P1[:, jj, tm], 0.0, ALU.mult, ALU.add))
                    ins = nc.vector.tensor_tensor_scan(BI[:, jj, tm], m, P3[:, jj, tm], 0.0, ALU.mult, ALU.add)
                    E.did(ins, "scan" if jj == HJ - 1 else None)
                E.settle()
                E.did(tt(P1[:, :, tm], TC, BR[:, :, tm], ALU.mult))
                E.did(tt(P2[:, :, tm], TS, BI[:, :, tm], ALU.mult))
                E.settle()
                E.did(tt(P1[:, :, tm], P1[:, :, tm], P2[:, :, tm], ALU.subtract))
                if hf == 0:
                    dve.wait_ge(S("ld_x0"), 16 * (L + 1))
                jr = slice(hf * HJ, (hf + 1) * HJ)
                ar, ai = bcast(are[:, jr], [P, HJ, NS], 2), bcast(aim[:, jr], [P, HJ, NS], 2)
                x0r, x0i = s5x0[:, 0, jr], s5x0[:, 1, jr]
                E.did(tt(stmp[:, 0], ar, x0r, ALU.mult))
                E.did(tt(stmp[:, 1], ai, x0i, ALU.mult))
                E.did(tt(stmp[:, 2], ar, x0i, ALU.mult))
                E.did(tt(stmp[:, 3], ai, x0r, ALU.mult), "dve_x0")
                E.settle()
                E.did(tt(stmp[:, 0], stmp[:, 0], stmp[:, 1], ALU.subtract))
                E.did(tt(stmp[:, 2], stmp[:, 2], stmp[:, 3], ALU.add))
                E.settle()
                E.did(tt(P1[:, :, SEQ:T], stmp[:, 0], BR[:, :, SEQ:T], ALU.add))
                E.did(tt(P3[:, :, SEQ:T], stmp[:, 2], BI[:, :, SEQ:T], ALU.add))
                need(dve, "poolpost", L, hf + 1)
                E.settle()
                E.did(tt(P3[:, :, tm], P3[:, :, tm], P4[:, :, tm], ALU.add))
                E.settle()
                if L > 0 and hf == 0:
                    dve.wait_ge(S("st_s5"), 16 * L)
                E.did(cp(s5o[:, 0, jr], P1[:, :, SEQ - 1:T]))
                E.did(cp(s5o[:, 1, jr], P3[:, :, SEQ - 1:T]), "s5x")

            def rotary(L):
                if L == 0:
                    dve.wait_ge(S("ld_rope"), 16)
                qk = hb[:, QC:QC + 4]
                for i in range(4):
                    need(dve, "rot", L, i + 1)
                    if i == 0:
                        E.settle()
                    E.did(tt(P2[:, i], ps[:, ROT_BANK[i], 0:T], rope[:, 1], ALU.mult), "rotrd")
                E.settle()
                E.did(tt(qk, qk, bcast(rope[:, 0], [P, 4, T], 1), ALU.mult))
                E.settle()
                E.did(tt(qk, qk, P2[:], ALU.add), "qk")
                E.settle()
                for c in range(2):
                    r = slice(64 * c, 64 * c + 64)
                    E.did(ts(qsd[r, :, :, c], hb[r, QC:QC + 2, SEQ:T], DH ** -0.5, None, ALU.mult), "qs")
                E.settle()
                E.did(tt(qkd[:], qsd[:], bcast(hb[:, KC:KC + 2, SEQ:T], [P, 2, NS, 2], 3), ALU.mult), "qs")

            def sample_out(L):
                need(dve, "in_evac", L, VC + 4)
                need(dve, "rsq", L, 1)
                for ht in range(2):
                    o, v = Oh[:, 2 * ht:2 * ht + 2, SEQ:T], hb[:, VC + 2 * ht:VC + 2 * ht + 2, SEQ:T]
                    sq, dots = (ps[:, 7, c:c + 16].rearrange("p (b c) -> p c b", c=2) for c in (16 * ht, 32 + 16 * ht))
                    E.did(tt(o, v, dots, ALU.mult))
                    E.settle()
                    E.did(tt(o, o, sq, ALU.add), "osamp" if ht else None)

            def keys_decayed(L):
                if L == 0:
                    dve.wait_ge(S("ld_dtab"), 16)
                    dve.wait_ge(S("ld_kdec"), 16)
                need(dve, "trk", L, 1)
                kd = kdec[:].unsqueeze(3).to_broadcast([P, 2, HEADS, 64])
                for t2 in range(2):
                    E.did(tt(KD[:, t2].rearrange("p (h d) -> p h d", h=HEADS),
                             ps[:, 4, 256 * t2:256 * t2 + 256].rearrange("p (h d) -> p h d", h=HEADS),
                             kd[:, t2], ALU.mult), "kd" if t2 else None)

            def ret_inner(L):
                for h in range(HEADS):
                    need(dve, "rin", L, h + 1)
                    E.did(tt(RI[:, h, 0:SEQ], ps[:, 4 + h, 0:SEQ], dtab[:, h], ALU.mult))
                    E.did(tt(RI[:, h, SEQ:DEC], ps[:, 4 + h, SEQ:DEC], dtab[:, h, 0:P], ALU.mult), "ri")

            def ret_states(L, samples):
                need(dve, "srg", L, 2)
                dve.wait_ge(S("ld_vbc"), 32 * (L + 1))
                for b in samples:
                    for ht in range(2):
                        last = b == NS - 1 and ht == 1
                        E.did(stt(SR[:, b, ht], VBC[:, b, ht], hb[:, KC + ht, SEQ + b:SEQ + b + 1], SR[:, b, ht],
                                  ALU.mult, ALU.add), "sr" if last else None)

            def sb_first(L):
                need(dve, "sbzs", L, 1)
                E.did(stt(Z[:, 4 * DEC:4 * DEC + 64].rearrange("p (n h) -> p n h", h=HEADS),
                          ps[:, 4, 0:64].rearrange("p (n h) -> p n h", h=HEADS), DH ** -0.5,
                          bcast(pv(L, "bias", 0, HEADS), [P, 16, HEADS], 1), ALU.mult, ALU.add), "zs")
                for h in range(HEADS):
                    need(dve, "sbz", L, h + 1)
                    E.did(ts(Z[:, h * DEC:(h + 1) * DEC], ps[:, SB_BANK[h], 0:DEC], DH ** -0.5, pv(L, "bias", h),
                             ALU.mult, ALU.add), "zev")
                E.settle()
                E.did(stt(SPL[:], Z[:], -1.0, Z[:], ALU.mult, ALU.max), "absz")

            def diagonals(buf):
                v = buf[:, 0:4 * DEC].rearrange("p (h c) -> p h c", h=HEADS)
                return v[:, :, 0:P], v[:, :, SEQ:DEC]

            mask = bcast(C["mask"], [P, HEADS, P], 1)

            def sb_second(L):
                need(dve, "spe", L, 1)
                E.did(stt(SPL[:], Z[:], 0.0, SPL[:], ALU.max, ALU.add))
                E.settle()
                d0, d1 = diagonals(SPL)
                E.did(tt(d0, d0, mask, ALU.mult))
                E.did(tt(d1, d1, mask, ALU.mult), "spl")

            def sb_third(L):
                for h in range(HEADS):
                    need(dve, "sbs", L, h + 1)
                    E.did(tt(Z[:, h * DEC:(h + 1) * DEC], Z[:, h * DEC:(h + 1) * DEC], ps[:, 4 + h, 0:DEC],
                             ALU.subtract), "zsub")
                need(dve, "sbss", L, 1)
                E.did(tt(Z[:, 4 * DEC:4 * DEC + 64], Z[:, 4 * DEC:4 * DEC + 64], ps[:, 4, 0:64], ALU.subtract), "zsubs")
                E.settle()
                E.did(ts(Z[:], Z[:], 0.0, None, ALU.min), "zmin")

            def sb_mask(L):
                need(dve, "wexp", L, 1)
                d0, d1 = diagonals(Z)
                E.did(tt(d0, d0, mask, ALU.mult))
                E.did(tt(d1, d1, mask, ALU.mult), "w")

            def sb_out(L):
                for ht in range(2):
                    need(dve, "sby", L, ht + 1)
                    E.did(cp(yb[:, ht, 0:SEQ], ps[:, 6 + ht, 0:SEQ]), "ybev")
                need(dve, "sbys", L, 1)
                for c in range(2):
                    r = slice(64 * c, 64 * c + 64)
                    E.did(cp(yb[r, :, SEQ:T], ps[r, 4, 0:32].rearrange("p (a b c) -> p a b c", a=2, c=2)[:, :, :, c]),
                          "ybs" if c else None)

            def sb_cat(L):
                need(dve, "rmsr", L, 1)
                for t in range(2):
                    E.did(stt(hb[:, QB_ + t], yb[:, t], pv(L, "norm_b_g", t), rms2[:, 1], ALU.mult, ALU.mult), "catb")

            def gn_center(L):
                for h in range(HEADS):
                    need(dve, "gmean", L, h + 1)
                    E.did(tt(Oh[:, h], Oh[:, h], ps[:, GN_BANK[h], 0:T], ALU.subtract), "gd")

            def gn_out(L):
                need(dve, "in_evac", L, N_IN)
                for h in range(HEADS):
                    need(dve, "gr", L, h + 1)
                    E.did(stt(Oh[:, h], Oh[:, h], pv(L, "gn_g", h), rg[:, h], ALU.mult, ALU.mult))
                    E.settle()
                    E.did(stt(hb[:, GC + h], Oh[:, h], pv(L, "gn_b", h), hb[:, GC + h], ALU.add, ALU.mult), "catc")

            def s5_skip(L, hf):
                need(dve, "s5y", L, hf + 1)
                E.did(stt(yd[:, hf], hb[:, U + hf], pv(L, "s5_d", hf), ps[:, 7, 0:T], ALU.mult, ALU.add), "yd")

            def s5_out(L):
                need(dve, "sig", L, 2)
                E.did(tt(yg[:], yg[:], sg[:], ALU.mult), "ya")

            def s5_cat(L):
                need(dve, "rmsr", L, 1)
                for t in range(2):
                    E.did(stt(hb[:, U + t], yg[:, t], pv(L, "norm_a_g", t), rms2[:, 0], ALU.mult, ALU.mult), "cata")

            def residual(L, first, i):
                bank = ps[:, (L * TILES + (N_IN if first else N_IN + N_OUT + N_UP) + i) % 4, 0:T]
                tile_done(dve, L, N_IN + i) if first else down_done(dve, L, i)
                E.did(stt(z[:, i], x[:, i], ALPHA, bank, ALU.mult, ALU.add), "z")

            for part in S5_PARTS[:3]:
                part(0)
            dve.wait_ge(S("ld_x"), 16)
            needq(dve, "lnc", 0, 1)
            for t in range(KT):
                ln_diff(0, t, ahead=True)
            ln_tail(0)
            for part in S5_PARTS[3:]:
                part(0)
            s5_phases(0, 0)
            for L in range(DEPTH):
                s5_phases(L, 1)
                s5_half(L, 0)
                sb_first(L)
                s5_skip(L, 0)
                s5_half(L, 1)
                sb_second(L)
                s5_skip(L, 1)
                rotary(L)
                sb_third(L)
                keys_decayed(L)
                sb_mask(L)
                s5_out(L)
                sample_out(L)
                ret_inner(L)
                sb_out(L)
                ret_states(L, range(NS // 2))
                gn_center(L)
                s5_cat(L)
                sb_cat(L)
                split_lo(L, N_IN + 2)
                gn_out(L)
                split_lo(L, N_IN + 3)
                ret_states(L, range(NS // 2, NS))
                split_lo(L, N_IN + 4)
                for i in range(N_OUT):
                    residual(L, True, i)
                    if i == 2:
                        needq(dve, "lnc", 2 * L + 1, 1)
                        ln_diff(2 * L + 1, 0)
                        ln_diff(2 * L + 1, 1)
                    if i >= 2:
                        ln_diff(2 * L + 1, i)
                    if i == 2:
                        split_lo(L, N_IN + 7)
                    if i == 5:
                        split_lo(L, PLAIN_UP + 1)
                ln_tail(2 * L + 1)
                dve.wait_ge(S("st_sr"), 16 * (L + 1))
                for t in range(0, KT, 2):
                    needq(dve, "x", 2 * L + 1, t + 1)
                    E.did(cp(x_hi[:, t], x[:, t]), "x_hi_dve")
                for t in range(1, KT, 2):
                    need(dve, "x_hi_act", L, t // 2 + 1)
                    E.did(tt(x_lo[:, t], x[:, t], x_hi[:, t].bitcast(F32), ALU.subtract), "x_lo_dve")
                split_lo(L, PLAIN_UP + 3)
                dve.wait_ge(S("ld_prev"), 16 * (L + 1))
                if L > 0:
                    dve.wait_ge(S("st_conv"), 16 * L)
                w0 = bcast(pv(L, "cw0", 0, N_UP), [P, N_UP, NS], 2)
                w1 = bcast(pv(L, "cw1", 0, N_UP), [P, N_UP, NS], 2)
                c10 = cout[:, :, 2:10]
                E.did(tt(spre[:], prev[:, :, 0], w0, ALU.mult))
                E.did(tt(c10, prev[:, :, 1], w1, ALU.mult))
                E.settle()
                E.did(tt(spre[:], spre[:], c10, ALU.add), "spre")
                for i in range(N_UP):
                    need(dve, "fc", L, i + 1)
                    bank, c = ps[:, (L * TILES + N_IN + N_OUT + i) % 4], conv[:, i % CSLOTS]
                    E.settle()
                    E.did(cp(cout[:, i], bank[:, SEQ - 2:T]))
                    E.did(stt(c[:, 1:SEQ], bank[:, 0:SEQ - 1], pv(L, "cw1", i), c[:, 1:SEQ], ALU.mult, ALU.add))
                    E.did(tt(c[:, SEQ:T], c[:, SEQ:T], spre[:, i], ALU.add))
                    E.settle()
                    E.did(stt(c[:, 2:SEQ], bank[:, 0:SEQ - 2], pv(L, "cw0", i), c[:, 2:SEQ], ALU.mult, ALU.add),
                          "up_free")
                    if i % 2 == 1 and i >= 3:
                        gated(L, i // 2 - 1)
                    if not by_pool(N_IN + N_OUT + i + 4):
                        split_lo(L, N_IN + N_OUT + i + 4)
                gated(L, FT - 1)
                done = 0
                for d in range(N_DOWN):
                    if d >= 1 and L + 1 < DEPTH:
                        if d <= len(S5_PARTS):
                            S5_PARTS[d - 1](L + 1)
                        elif d in PHASES_AT:
                            s5_phases(L + 1, 0, PHASES_AT.index(d))
                    if 4 <= d + 3 < N_DOWN and not by_pool(N_IN + N_OUT + N_UP + d + 3):
                        split_lo(L, N_IN + N_OUT + N_UP + d + 3)
                    while done < KT and (FT * (done + 1) - 1) // 8 == d:
                        i = done
                        done += 1
                        residual(L, False, i)
                        if i == 3:
                            needq(dve, "lnc", 2 * L + 2, 1)
                            for t in range(3):
                                ln_diff(2 * L + 2, t)
                        if i >= 3:
                            ln_diff(2 * L + 2, i)
                ln_tail(2 * L + 2)

        @block.gpsimd
        def _(pool):
            E = Engine(pool, "pool_step")
            tt = nc.gpsimd.tensor_tensor
            tm = slice(0, SEQ)

            def ln_squares(q):
                first = POOL_FROM[q > 0]
                for t in range(first + 1, KT - 1):
                    needq(pool, "lnsq", q, t + 1)
                    E.settle()
                    E.did(tt(acc[:, 1], sqt[:, first % 3] if t == first + 1 else acc[:, 1], sqt[:, t % 3], ALU.add),
                          "lnacc2" if t == KT - 2 else "pool_ln")

            def split_lo(L, i):
                need(pool, "w_hi", L, SPLIT.index(i) + 1)
                slot = split_slot(i)
                E.did(tt(w_lo[:, slot], ring[:, ring_slot(L * UNITS + i)], w_hi[:, slot].bitcast(F32), ALU.subtract),
                      "w_lo_pool")

            def branch_lo(L, k):
                need(pool, "cat_hi", L, k + 1)
                E.did(tt(cat_lo[:, k], cat[k], cat_hi[:, k].bitcast(F32), ALU.subtract), "cat_lo")

            ln_squares(0)
            for L in range(DEPTH):
                for hf in range(2):
                    TC, TS = tabs[hf]
                    need(pool, "buev", L, 8 * hf + 8)
                    need(pool, "tab", L, 2 * hf + 2)
                    if hf == 1:
                        need(pool, "s5y", L, 1)
                    E.settle()
                    E.did(tt(P4[:, :, tm], TS, BR[:, :, tm], ALU.mult))
                    E.did(tt(P3[:, :, tm], TC, BI[:, :, tm], ALU.mult), "poolpre")
                    need(pool, "scan", L, hf + 1)
                    E.settle()
                    E.did(tt(P4[:, :, tm], TS, BR[:, :, tm], ALU.mult))
                    E.did(tt(P3[:, :, tm], TC, BI[:, :, tm], ALU.mult), "poolpost")
                need(pool, "s5x", L, 2)
                pool.dma_start(O["s5"][L], s5o[:]).then_inc(S("st_s5"), 16)
                split_lo(L, N_IN)
                split_lo(L, N_IN + 1)
                for k in range(KT):
                    branch_lo(L, k)
                split_lo(L, N_IN + 5)
                split_lo(L, N_IN + 6)
                need(pool, "sr", L, 1)
                pool.dma_start(O["rsample"][L], SR[:]).then_inc(S("st_sr"), 16)
                ln_squares(2 * L + 1)
                split_lo(L, PLAIN_UP + 2)
                for t in range(0, KT, 2):
                    need(pool, "x_hi_dve", L, t // 2 + 1)
                    E.did(tt(x_lo[:, t], x[:, t], x_hi[:, t].bitcast(F32), ALU.subtract), "x_lo_pool")
                need(pool, "spre", L, 1)
                pool.dma_start(O["convprev"][L], prev[:, :, 1]).then_inc(S("st_prev"), 16)
                for p in range(FT):
                    for i in (N_IN + N_OUT + 2 * p + 6, N_IN + N_OUT + 2 * p + 7):
                        if by_pool(i) and i <= N_IN + N_OUT + N_UP + 3:
                            split_lo(L, i)
                    need(pool, "hff_hi", L, p + 1)
                    E.did(tt(hff_lo[:, p], conv[:, (2 * p + 1) % CSLOTS], hff_hi[:, p].bitcast(F32), ALU.subtract),
                          "hff_lo")
                pool.dma_start(O["conv"][L], cout[:]).then_inc(S("st_conv"), 16)
                for d in range(4, N_DOWN):
                    if by_pool(N_IN + N_OUT + N_UP + d):
                        split_lo(L, N_IN + N_OUT + N_UP + d)
                ln_squares(2 * L + 2)
            for name in ("st_s5", "st_prev", "st_conv"):
                pool.wait_ge(S(name), 16 * DEPTH)


def constants():
    f = np.float32
    eye = np.eye(P, dtype=f)
    k, q = np.arange(P)[:, None], np.arange(P)[None, :]
    perm = np.zeros((P, P), f)
    for m in range(P):
        perm[m + 32 if m % 64 < 32 else m - 32, m] = -1.0 if m % 64 < 32 else 1.0
    cst = np.stack([np.full((P, P), 1 / P, f), np.full((P, P), 1 / D_MODEL, f), eye, (k >= q).astype(f),
                    np.ones((P, P), f), (k < q).astype(f), perm, np.full((P, P), 1 / 256, f)], 1)
    pos = np.concatenate([np.arange(SEQ), np.full(NS, SEQ)]).astype(f)
    inv = (10000.0 ** (-np.arange(32, dtype=f) / 32)).astype(f)[np.arange(P) % 32]
    ang = (inv[:, None] * pos[None, :]).astype(f)
    rope = np.stack([np.cos(ang), np.sin(ang)], 1).astype(f)
    gap = np.arange(SEQ)[None, None, :] - np.arange(P)[:, None, None]
    dtab = np.where(gap >= 0, np.exp(LOG_GAMMA[None, :, None] * np.maximum(gap, 0)), 0.0) * DH ** -0.5
    left = SEQ - 1 - (np.arange(P)[:, None] + P * np.arange(2)[None, :])
    kdec = np.exp(LOG_GAMMA[None, None, :] * left[:, :, None])
    gam = np.exp(LOG_GAMMA)[2 * np.arange(2)[None, :] + (np.arange(P) // 64)[:, None]]
    steps = np.broadcast_to(np.arange(SEQ, dtype=f), (P, SEQ))
    return {"cst": cst, "rope": rope, "dtab": dtab.astype(f), "kdec": kdec.astype(f), "gam": gam.astype(f),
            "steps": steps}


def lay_out(i):
    f = np.float32
    D = DEPTH
    a = {}
    xt = np.concatenate([i["x_prompt"][0], i["x_sample"][:, 0]], 0)
    a["xT"] = xt.T.reshape(KT, P, T).transpose(1, 0, 2)
    w_in = i["w_in"].reshape(D, 8, P, N_IN, P).transpose(0, 3, 2, 1, 4)
    w_out = i["w_out"].reshape(D, 8, P, KT, P).transpose(0, 3, 2, 1, 4)
    up_order = [m + FT * g for m in range(FT) for g in range(2)]
    w_up = i["ffn_w_up"].reshape(D, 8, P, N_UP, P).transpose(0, 3, 2, 1, 4)[:, up_order]
    w_dn = i["ffn_w_down"].reshape(D, FT, P, KT, P).transpose(0, 3, 1, 2, 4)
    w_dn = w_dn.reshape(D, N_DOWN, 8, P, P).transpose(0, 1, 3, 2, 4)
    a["units"] = np.concatenate([w_in, w_out, w_up, w_dn], 1).reshape(D * UNITS, P, 8, P)
    col = lambda v: v.reshape(-1, P).T
    upc = lambda v: col(v)[:, up_order]
    cols = [col(i["ln_in_g"]), col(i["ln_in_b"])]
    for l in range(D):
        cols += [col(i[n][l]) for n in ("norm_a_g", "norm_b_g", "ret_gn_g", "ret_gn_b", "ln1_g", "ln1_b",
                                        "ln2_g", "ln2_b", "s5_d")]
        cols += [upc(i["ffn_conv_w"][l, j]) for j in range(3)] + [upc(i["ffn_conv_b"][l])]
        cols += [np.broadcast_to(i["sb_logit_bias"][l], (P, HEADS))]
    a["vec"] = np.concatenate(cols, 1)
    j8 = lambda v: v.reshape(D, J, 2 * 64).transpose(0, 2, 1)
    def rows(v):
        v = v.reshape(D, 2, HJ, 1, 1, 2, 64)
        v = np.broadcast_to(v, (D, 2, HJ, 2, 16, 2, 64))
        return v.transpose(0, 2, 3, 4, 1, 5, 6).reshape(D, P, 256)
    ls = np.broadcast_to(i["s5_log_step"][:, :, None], i["s5_lambda_re"].shape)
    a["s5in"] = np.stack([np.concatenate([j8(v), rows(v)], 2)
                          for v in (i["s5_lambda_re"], i["s5_lambda_im"], ls)], 2)
    s5b = np.zeros((D, 2, HJ, 2, 16, 2, 2, 64), f)
    s5c = np.zeros((D, 2, J, 2, 64, 2, 16), f)
    for c, (nb, nc_) in enumerate((("s5_b_re", "s5_c_re"), ("s5_b_im", "s5_c_im"))):
        b = i[nb].reshape(D, 2, HJ, 2, 64, 16)
        cc = i[nc_].reshape(D, J, 2, 16, 64)
        for gl in range(2):
            s5b[:, c, :, gl, :, :, gl] = b[:, :, :, gl].transpose(0, 2, 4, 1, 3)
            s5c[:, c, :, gl, :, gl] = cc[:, :, gl].transpose(0, 1, 3, 2)
    a["s5b"] = s5b.reshape(D, 2, P, 256).transpose(0, 2, 1, 3)
    a["s5c"] = s5c.reshape(D, 2, J, P, 32).transpose(0, 3, 1, 2, 4)
    a["s5x0"] = np.stack([i[n].reshape(D, NS, J, P).transpose(0, 3, 2, 1)
                          for n in ("state_s5_re", "state_s5_im")], 2)
    a["wglu"] = i["s5_w_glu"].reshape(D, 2, P, 256).transpose(0, 2, 1, 3)
    a["kpool"] = i["cache_k"].reshape(D, POOL, PAGE, 2, P).transpose(0, 1, 4, 3, 2).reshape(D, POOL, P, 256)
    a["vpool"] = i["cache_v"].reshape(D, POOL, PAGE, 256)
    a["sret"] = i["state_ret"].reshape(D, NS, 2, P, DV).transpose(0, 3, 1, 2, 4)
    a["prev"] = i["state_conv"].reshape(D, NS, 2, N_UP, P).transpose(0, 4, 3, 2, 1)[:, :, up_order]
    a["pages"] = i["page_table"].reshape(1, -1)
    a.update(constants())
    return {k: np.ascontiguousarray(v) for k, v in a.items()}, up_order


_OUTS = {"y": (P, KT, T), "kv": (DEPTH, P, 4, T), "s5": (DEPTH, P, 2, J, NS + 1), "rprompt": (DEPTH, P, 2, DV),
         "rsample": (DEPTH, P, NS, 2, DV), "conv": (DEPTH, P, N_UP, 10), "convprev": (DEPTH, P, N_UP, NS)}


def kernel(**inputs):
    import concourse.bacc as _bacc
    from concourse.bass_utils import run_bass_kernel_spmd as _run

    arrays, up_order = lay_out({k: np.asarray(v) for k, v in inputs.items()})
    nc = _bacc.Bacc("TRN2", target_bir_lowering=False, num_devices=1)
    A = {k: nc.dram_tensor(f"in_{k}", v.shape, mybir.dt.from_np(v.dtype), kind="ExternalInput").ap()
         for k, v in arrays.items()}
    O = {k: nc.dram_tensor(f"out_{k}", s, F32, kind="ExternalOutput").ap() for k, s in _OUTS.items()}
    hybrid_step(nc, A, O)
    res = _run(nc, [{f"in_{k}": v for k, v in arrays.items()}], core_ids=[0]).results[0]
    r = {k: np.asarray(res[f"out_{k}"]) for k in _OUTS}
    D = DEPTH
    y = r["y"].transpose(2, 1, 0).reshape(T, D_MODEL)
    kv = r["kv"].transpose(0, 3, 2, 1).reshape(D, T, 2, HEADS, DH)
    s5 = r["s5"].transpose(0, 2, 4, 3, 1).reshape(D, 2, NS + 1, 16, 64)
    rp = r["rprompt"].transpose(0, 2, 1, 3).reshape(D, 1, HEADS, DH, DV)
    rs = r["rsample"].transpose(0, 2, 3, 1, 4).reshape(D, NS, HEADS, DH, DV)
    back = np.argsort(up_order)
    cv = r["conv"][:, :, back].transpose(0, 3, 2, 1).reshape(D, 10, 2 * D_FF)
    cp = r["convprev"][:, :, back].transpose(0, 3, 2, 1).reshape(D, NS, 2 * D_FF)
    return (y[None, :SEQ], y[SEQ:, None],
            kv[:, None, :SEQ, 0], kv[:, None, :SEQ, 1], kv[:, SEQ:, None, 0], kv[:, SEQ:, None, 1],
            s5[:, 0, :1], s5[:, 1, :1], s5[:, 0, 1:], s5[:, 1, 1:], rp, rs,
            cv[:, None, :2], np.stack([cp, cv[:, 2:]], 2))
```
